# Optimizing a Trainium2 kernel written in Bass

```python
import jax, jax.numpy as jnp
from jax import lax
import numpy as np

D_MODEL = 1024
BATCH = 1
SEQ = 1024
DEPTH = 2

N_META = 16
HEAD_DIM = 64
N_HEADS = D_MODEL // HEAD_DIM
N_A_LAYERS = DEPTH // 2
N_B_LAYERS = DEPTH - N_A_LAYERS
DECAY_LORA = 64
ICLR_LORA = 64
VRES_LORA = 32
Q_BLOCK = 128
NORM_EPS = 1e-6
GN_EPS = 64e-5
A_IN_WIDTH = 4 * D_MODEL + DECAY_LORA + ICLR_LORA

kernel_name = "yoco_rwkv7_fox_hybrid"

def rmsnorm(x, g):
    xf = x.astype(jnp.float32)
    xf = xf * lax.rsqrt(jnp.mean(xf * xf, axis=-1, keepdims=True) + NORM_EPS)
    return xf.astype(x.dtype) * g

def token_shift(u, mu):
    prev = jnp.pad(u, ((0, 0), (1, 0), (0, 0)))[:, :-1]
    return u + mu * (prev - u)

def wkv7_scan(r, decay, k, v, kk, a):
    B, T, H, N = r.shape
    def step(S, inp):
        r_t, w_t, k_t, v_t, kk_t, a_t = inp
        sa = jnp.einsum('bhij,bhj->bhi', S, -kk_t)
        S = (S * w_t[:, :, None, :]
             + sa[..., None] * (kk_t * a_t)[:, :, None, :]
             + v_t[..., None] * k_t[:, :, None, :])
        y = jnp.einsum('bhij,bhj->bhi', S, r_t)
        return S, y
    xs = tuple(jnp.moveaxis(t.astype(jnp.float32), 1, 0) for t in (r, decay, k, v, kk, a))
    S0 = jnp.zeros((B, H, N, N), jnp.float32)
    _, ys = lax.scan(step, S0, xs)
    return jnp.moveaxis(ys, 0, 1)

def rwkv7_layer(h, v_first, norm, w_in, mu, decay_up, decay_bias, iclr_up, iclr_bias,
                vres_up, vres_bias, k_k, k_a, r_k, gn_w, gn_b, w_out):
    B, T, D = h.shape
    H, N = N_HEADS, HEAD_DIM
    xn = rmsnorm(h, norm)
    proj = token_shift(xn @ w_in, mu)
    r = proj[..., :D]
    k = proj[..., D:2 * D]
    v = proj[..., 2 * D:3 * D]
    z = proj[..., 3 * D:4 * D]
    w_lo = proj[..., 4 * D:4 * D + DECAY_LORA]
    a_lo = proj[..., 4 * D + DECAY_LORA:4 * D + DECAY_LORA + ICLR_LORA]
    w_log = -jax.nn.softplus(-(decay_bias + jnp.tanh(w_lo) @ decay_up).astype(jnp.float32)) - 0.5
    decay = jnp.exp(-jnp.exp(w_log))
    a = jax.nn.sigmoid(iclr_bias + a_lo @ iclr_up)
    if v_first is None:
        v_first = v
    else:
        vres_lo = proj[..., 4 * D + DECAY_LORA + ICLR_LORA:]
        v = v + (v_first - v) * jax.nn.sigmoid(vres_bias + vres_lo @ vres_up)
    kk = (k * k_k).reshape(B, T, H, N)
    kkf = kk.astype(jnp.float32)
    kk = (kkf / jnp.maximum(jnp.sqrt(jnp.sum(kkf * kkf, axis=-1, keepdims=True)), 1e-12)).astype(k.dtype)
    k = k * (1 + (a - 1) * k_a)
    rh = r.reshape(B, T, H, N)
    kh = k.reshape(B, T, H, N)
    vh = v.reshape(B, T, H, N)
    y = wkv7_scan(rh, decay.reshape(B, T, H, N), kh, vh, kk, a.reshape(B, T, H, N))
    mean = jnp.mean(y, axis=-1, keepdims=True)
    var = jnp.mean(jnp.square(y - mean), axis=-1, keepdims=True)
    y = ((y - mean) * lax.rsqrt(var + GN_EPS)).astype(h.dtype).reshape(B, T, D) * gn_w + gn_b
    bonus = jnp.sum(rh * kh * r_k.reshape(H, N), axis=-1, keepdims=True) * vh
    out = (y + bonus.reshape(B, T, D)) * jax.nn.silu(z)
    return h + out @ w_out, v_first

def head_rmsnorm(x, g):
    xf = x.astype(jnp.float32)
    xf = xf * lax.rsqrt(jnp.mean(xf * xf, axis=-1, keepdims=True) + NORM_EPS)
    return xf.astype(x.dtype) * g

def shared_kv(h, kv_norm, kv_w, kv_f_bias, k_norm):
    B, T, D = h.shape
    kvf = rmsnorm(h, kv_norm) @ kv_w
    k_sh = head_rmsnorm(kvf[..., :D].reshape(B, T, N_HEADS, HEAD_DIM), k_norm)
    v_sh = kvf[..., D:2 * D].reshape(B, T, N_HEADS, HEAD_DIM)
    log_f = jax.nn.log_sigmoid(kvf[..., 2 * D:].astype(jnp.float32) + kv_f_bias)
    c_all = jnp.cumsum(log_f, axis=1)
    return k_sh, v_sh, c_all

def fox_attention(q, k, v, c_all):
    B, S, H, N = q.shape
    T = k.shape[1]
    n_blk = S // Q_BLOCK
    scale = HEAD_DIM ** -0.5
    q_blk = q.reshape(B, n_blk, Q_BLOCK, H, N).transpose(1, 0, 3, 2, 4)
    cq_blk = c_all[:, N_META:].reshape(B, n_blk, Q_BLOCK, H).transpose(1, 0, 3, 2)
    kh = k.transpose(0, 2, 1, 3)
    vh = v.transpose(0, 2, 1, 3)
    ck = c_all.transpose(0, 2, 1)
    key_pos = jnp.arange(T)

    def one_block(args):
        qb, cqb, blk = args
        q_pos = N_META + blk * Q_BLOCK + jnp.arange(Q_BLOCK)
        logits = (jnp.einsum('bhqn,bhkn->bhqk', qb, kh).astype(jnp.float32) * scale
                  + cqb[..., None] - ck[:, :, None, :])
        mask = key_pos[None, :] <= q_pos[:, None]
        logits = jnp.where(mask, logits, -jnp.inf)
        p = jax.nn.softmax(logits, axis=-1)
        return jnp.einsum('bhqk,bhkn->bhqn', p.astype(vh.dtype), vh)

    out = lax.map(one_block, (q_blk, cq_blk, jnp.arange(n_blk)))
    return out.transpose(1, 0, 3, 2, 4).reshape(B, S, H, N)

def fox_layer(h, k_sh, v_sh, c_all, norm, w_in, q_norm, w_out):
    B, S, D = h.shape
    proj = rmsnorm(h, norm) @ w_in
    q = head_rmsnorm(proj[..., :D].reshape(B, S, N_HEADS, HEAD_DIM), q_norm)
    z = proj[..., D:]
    attn = fox_attention(q, k_sh, v_sh, c_all).reshape(B, S, D)
    return h + (attn * jax.nn.silu(z)) @ w_out

def setup_inputs(seed: int = 0) -> dict:
    key = jax.random.key(seed)
    ks = iter(jax.random.split(key, 40))
    D, H, NA, NB = D_MODEL, N_HEADS, N_A_LAYERS, N_B_LAYERS

    def nrm(shape, scale):
        return scale * jax.random.normal(next(ks), shape, jnp.float32)

    def unif(shape):
        return jax.random.uniform(next(ks), shape, jnp.float32, 0.05, 0.95)

    return {
        "x": nrm((BATCH, SEQ, D), 1.0),
        "meta_tokens": nrm((N_META, D), 1.0),
        "a_norm": 1.0 + nrm((NA, D), 0.1),
        "a_w_in": nrm((NA, D, A_IN_WIDTH), D ** -0.5),
        "a_shift_mu": unif((NA, A_IN_WIDTH)),
        "a_vres_down": nrm((NA - 1, D, VRES_LORA), D ** -0.5),
        "a_vres_mu": unif((NA - 1, VRES_LORA)),
        "a_vres_up": nrm((NA - 1, VRES_LORA, D), VRES_LORA ** -0.5),
        "a_vres_bias": 0.5 + nrm((NA - 1, D), 0.1),
        "a_decay_up": nrm((NA, DECAY_LORA, D), 0.5 * DECAY_LORA ** -0.5),
        "a_decay_bias": -0.5 + nrm((NA, D), 0.5),
        "a_iclr_up": nrm((NA, ICLR_LORA, D), ICLR_LORA ** -0.5),
        "a_iclr_bias": nrm((NA, D), 0.1),
        "a_k_k": 0.85 + nrm((NA, D), 0.05),
        "a_k_a": 1.0 + nrm((NA, D), 0.05),
        "a_r_k": nrm((NA, D), 0.1),
        "a_gn_w": 1.0 + nrm((NA, D), 0.1),
        "a_gn_b": nrm((NA, D), 0.02),
        "a_w_out": nrm((NA, D, D), 0.5 * D ** -0.5),
        "kv_norm": 1.0 + nrm((D,), 0.1),
        "kv_w": nrm((D, 2 * D + H), D ** -0.5),
        "kv_f_bias": 3.0 + nrm((H,), 0.5),
        "k_norm": 1.0 + nrm((HEAD_DIM,), 0.1),
        "b_norm": 1.0 + nrm((NB, D), 0.1),
        "b_w_in": nrm((NB, D, 2 * D), D ** -0.5),
        "b_q_norm": 1.0 + nrm((NB, HEAD_DIM), 0.1),
        "b_w_out": nrm((NB, D, D), 0.5 * D ** -0.5),
    }

def reference(x, meta_tokens, a_norm, a_w_in, a_shift_mu, a_vres_down, a_vres_mu, a_vres_up,
              a_vres_bias, a_decay_up, a_decay_bias, a_iclr_up, a_iclr_bias, a_k_k, a_k_a, a_r_k,
              a_gn_w, a_gn_b, a_w_out, kv_norm, kv_w, kv_f_bias, k_norm, b_norm, b_w_in,
              b_q_norm, b_w_out):
    B = x.shape[0]
    meta = jnp.broadcast_to(meta_tokens.astype(x.dtype)[None], (B, N_META, D_MODEL))
    h = jnp.concatenate([meta, x], axis=1)
    v_first = None
    k_sh = v_sh = c_all = None
    for layer in range(DEPTH):
        if layer < N_A_LAYERS:
            l = layer
            if l == 0:
                w_in, mu, vres_up, vres_bias = a_w_in[0], a_shift_mu[0], None, None
            else:
                w_in = jnp.concatenate([a_w_in[l], a_vres_down[l - 1]], axis=1)
                mu = jnp.concatenate([a_shift_mu[l], a_vres_mu[l - 1]], axis=0)
                vres_up, vres_bias = a_vres_up[l - 1], a_vres_bias[l - 1]
            h, v_first = rwkv7_layer(h, v_first, a_norm[l], w_in, mu, a_decay_up[l], a_decay_bias[l],
                                     a_iclr_up[l], a_iclr_bias[l], vres_up, vres_bias, a_k_k[l],
                                     a_k_a[l], a_r_k[l], a_gn_w[l], a_gn_b[l], a_w_out[l])
            if layer == N_A_LAYERS - 1:
                k_sh, v_sh, c_all = shared_kv(h, kv_norm, kv_w, kv_f_bias, k_norm)
                h = h[:, N_META:]
        else:
            j = layer - N_A_LAYERS
            h = fox_layer(h, k_sh, v_sh, c_all, b_norm[j], b_w_in[j], b_q_norm[j], b_w_out[j])
    return h


_drawn_inputs = setup_inputs


def setup_inputs(seed=0):
    import zlib

    import numpy as np

    out = dict(_drawn_inputs(seed))
    spreads = {}
    factors = {'meta_tokens': 3.75,
     'a_decay_up': 3.6,
     'a_iclr_bias': 5.31,
     'a_k_k': 8.0,
     'a_k_a': 4.152,
     'a_gn_b': 8.0,
     'kv_norm': 4.775,
     'kv_f_bias': 2.835,
     'k_norm': 8.0,
     'b_norm': 4.862,
     'b_q_norm': 7.581}
    for name, (base, spread) in spreads.items():
        noise = np.random.default_rng([zlib.crc32(name.encode()), seed]).standard_normal(out[name].shape)
        drawn = base * np.exp(spread * noise) if base else spread * noise
        out[name] = __import__('jax').numpy.asarray(drawn.astype(out[name].dtype))
    for name, factor in factors.items():
        out[name] = (out[name] * factor).astype(out[name].dtype)
    return out
```

```python
from contextlib import ExitStack

import numpy as np

import concourse.bass as bass
from concourse import mybir

F32 = mybir.dt.float32
F32R = mybir.dt.float32r
BF16 = mybir.dt.bfloat16
ALU = mybir.AluOpType
ACT = mybir.ActivationFunctionType
AX = mybir.AxisListType

P = 128
D = 1024
SEQ = 1024
META = 16
T = SEQ + META
HD = 64
H = D // HD
KO = D // P
SEG = 348
TP = 3 * SEG
CH = 64
NT = 9
OFF = NT * P - T
TW = OFF + TP
LORA = 64
A_COLS = 4 * D + 2 * LORA
RMS_EPS = 1e-6
GN_EPS = 64e-5
KK_FLOOR = 1e-12
C_DECAY = float(np.exp(-0.5)) / 2
LN_SCALE = 2.0 ** 20
MASKED = -1e30
SCALE = HD ** -0.5

(Q_MUR, Q_MUK, Q_MUV, Q_MUZ, Q_DB, Q_IB, Q_KK, Q_KA, Q_RK, Q_GW, Q_GB,
 Q_NR, Q_NK, Q_NV, Q_NZ, Q_HDB, Q_HIB, Q_NKA) = range(18)
NQ = 18
ROW_LORA, ROW_AN, ROW_KVN, ROW_BN, ROW_KN, ROW_QN, NROWS = 88, 89, 97, 105, 113, 114, 115
C_LORA = NQ * KO
C_AN, C_KVN, C_BN, C_KN, C_QN, C_NLORA = (C_LORA + 1, C_LORA + 9, C_LORA + 17, C_LORA + 25,
                                          C_LORA + 26, C_LORA + 27)
NCOLS = C_LORA + 28

class Signals:

    def __init__(self, sem):
        self.x_loaded0 = sem("x_loaded0")
        self.x_loaded1 = sem("x_loaded1")
        self.rows_loaded = sem("rows_loaded")
        self.w_asked = sem("w_asked")
        self.consts_loaded = sem("consts_loaded")
        self.up_loaded = sem("up_loaded")
        self.w_loaded0 = sem("w_loaded0")
        self.w_loaded1 = sem("w_loaded1")
        self.w_scaled = sem("w_scaled")
        self.w_hi = sem("w_hi")
        self.w_lo = sem("w_lo")
        self.proj_done = sem("proj_done")
        self.param_tr = sem("param_tr")
        self.param_copied = sem("param_copied")
        self.param_derived = sem("param_derived")
        self.pads_zero = sem("pads_zero")
        self.setup_dve = sem("setup_dve")
        self.setup_pool = sem("setup_pool")
        self.x_tr = sem("x_tr")
        self.x_evac = sem("x_evac")
        self.xt_stored = sem("xt_stored")
        self.h_sq = sem("h_sq")
        self.h_sumsq = sem("h_sumsq")
        self.h_ln = sem("h_ln")
        self.h_rstd = sem("h_rstd")
        self.xn_mul = sem("xn_mul")
        self.x_hi = sem("x_hi")
        self.x_lo = sem("x_lo")
        self.mu_done = sem("mu_done")
        self.shifted = sem("shifted")
        self.lora_tanh = sem("lora_tanh")
        self.pair_free = sem("pair_free")
        self.pair_params = sem("pair_params")
        self.up_copied = sem("up_copied")
        self.dec_done = sem("dec_done")
        self.icl_done = sem("icl_done")
        self.dec_tanh = sem("dec_tanh")
        self.icl_tanh = sem("icl_tanh")
        self.logw = sem("logw")
        self.cumlog = sem("cumlog")
        self.iclr = sem("iclr")
        self.cum_before = sem("cum_before")
        self.exp_in = sem("exp_in")
        self.exp_neg = sem("exp_neg")
        self.exp_before = sem("exp_before")
        self.chunk_end = sem("chunk_end")
        self.kk_raw = sem("kk_raw")
        self.kk_sq = sem("kk_sq")
        self.kk_sumsq = sem("kk_sumsq")
        self.kk_guard = sem("kk_guard")
        self.kk_ln = sem("kk_ln")
        self.kk_rn = sem("kk_rn")
        self.kk_norm = sem("kk_norm")
        self.a_tilde = sem("a_tilde")
        self.r_tilde = sem("r_tilde")
        self.k_mix = sem("k_mix")
        self.k_new = sem("k_new")
        self.k_tilde = sem("k_tilde")
        self.kk_a = sem("kk_a")
        self.b_tilde = sem("b_tilde")
        self.bonus_prod = sem("bonus_prod")
        self.bonus_sum = sem("bonus_sum")
        self.bonus = sem("bonus")
        self.z_tanh = sem("z_tanh")
        self.z_gate = sem("z_gate")
        self.state_zero = sem("state_zero")
        self.tr_done = sem("tr_done")
        self.rows_ready = sem("rows_ready")
        self.a_done = sem("a_done")
        self.a_masked = sem("a_masked")
        self.q_done = sem("q_done")
        self.q_copied = sem("q_copied")
        self.p_done = sem("p_done")
        self.p_masked = sem("p_masked")
        self.x_done = sem("x_done")
        self.x_added = sem("x_added")
        self.wu_done = sem("wu_done")
        self.wu_copied = sem("wu_copied")
        self.u_done = sem("u_done")
        self.u_ready = sem("u_ready")
        self.s_done = sem("s_done")
        self.s_ready = sem("s_ready")
        self.s_scaled = sem("s_scaled")
        self.y_done = sem("y_done")
        self.y_copied = sem("y_copied")
        self.gn_mean = sem("gn_mean")
        self.gn_centred = sem("gn_centred")
        self.gn_sq = sem("gn_sq")
        self.gn_var = sem("gn_var")
        self.gn_ln = sem("gn_ln")
        self.gn_rstd = sem("gn_rstd")
        self.gn_scaled = sem("gn_scaled")
        self.gn_affine = sem("gn_affine")
        self.gn_bonus = sem("gn_bonus")
        self.out_ready = sem("out_ready")
        self.out_stored = sem("out_stored")
        self.o_loaded0 = sem("o_loaded0")
        self.o_loaded1 = sem("o_loaded1")
        self.xt_loaded = sem("xt_loaded")
        self.res_added = sem("res_added")
        self.f_logit = sem("f_logit")
        self.f_abs = sem("f_abs")
        self.f_exp = sem("f_exp")
        self.f_ln = sem("f_ln")
        self.f_min = sem("f_min")
        self.f_log = sem("f_log")
        self.f_cum = sem("f_cum")
        self.c_tr = sem("c_tr")
        self.c_col = sem("c_col")
        self.c_scaled = sem("c_scaled")
        self.c_hi = sem("c_hi")
        self.c_lo = sem("c_lo")
        self.c_stored = sem("c_stored")
        self.vone_ones = sem("vone_ones")
        self.bpair_free = sem("bpair_free")
        self.c_rows = sem("c_rows")
        self.bias_col = sem("bias_col")
        self.b_evac = sem("b_evac")
        self.hn_sq = sem("hn_sq")
        self.hn_sumsq = sem("hn_sumsq")
        self.hn_ln = sem("hn_ln")
        self.hn_rstd = sem("hn_rstd")
        self.hn_full = sem("hn_full")
        self.kq_hi = sem("kq_hi")
        self.kq_lo = sem("kq_lo")
        self.v_tr = sem("v_tr")
        self.v_rows = sem("v_rows")
        self.bz_tanh = sem("bz_tanh")
        self.bz_gate = sem("bz_gate")
        self.smax_done = sem("smax_done")
        self.smax = sem("smax")
        self.m_row_done = sem("m_row_done")
        self.m_row = sem("m_row")
        self.st_done = sem("st_done")
        self.p_exp = sem("p_exp")
        self.pv_done = sem("pv_done")
        self.d_ln = sem("d_ln")
        self.d_recip = sem("d_recip")
        self.o_norm = sem("o_norm")
        self.o_gated = sem("o_gated")
        self.ob_stored = sem("ob_stored")
        self.fin_sum = sem("fin_sum")
        self.fin_tr = sem("fin_tr")
        self.fin_evac = sem("fin_evac")
        self.fin_stored0 = sem("fin_stored0")
        self.fin_stored1 = sem("fin_stored1")


def build(nc, x, meta, rows, w_in, up, w_out, kv_w, f_bias, b_w_in, b_w_out, ident_d, masks_d, levels_d,
          causal_d, out):
    ctx = ExitStack()
    with ctx:
        def sb(name, shape, dt=F32):
            return ctx.enter_context(nc.sbuf_tensor(name, shape, dt))

        S = Signals(lambda name: ctx.enter_context(nc.semaphore(name)))

        X_LOADED, W_LOADED = (S.x_loaded0, S.x_loaded1), (S.w_loaded0, S.w_loaded1)
        O_LOADED, FIN_STORED = (S.o_loaded0, S.o_loaded1), (S.fin_stored0, S.fin_stored1)

        xt_scr = nc.dram_tensor("xt_scr", (P, KO * TP), F32, kind="Internal").ap()
        oa_scr = nc.dram_tensor("oa_scr", (KO, P, TP), F32, kind="Internal").ap()
        ob_scr = nc.dram_tensor("ob_scr", (KO, P, SEQ), F32, kind="Internal").ap()
        c_scr = nc.dram_tensor("c_scr", (H, 2, TP), F32, kind="Internal").ap()

        ident = sb("ident", [P, P])
        identb = sb("identb", [P, P], BF16)
        head_ones = sb("head_ones", [P, P])
        all_ones = sb("all_ones", [P, P])
        ones_r = sb("ones_r", [P, P], F32R)
        masks = sb("masks", [P, 2 * P])
        levels = sb("levels", [P, 6 * P])
        causal = sb("causal", [P, 2 * P], BF16)
        params = sb("params", [P, NCOLS])
        pp = sb("pp", [P, NQ])
        cst = sb("cst", [P, 4])
        fb_in = sb("fb_in", [P, 1])
        EPS_RMS, EPS_GN, LN_BACK = (cst[:, i:i + 1] for i in range(3))

        xh = sb("xh", [P, KO, TP], F32R)
        xl = sb("xl", [P, KO, TP], F32R)
        wr = sb("wr", [P, 2, KO, P])
        wh = sb("wh", [P, 2, KO, P], F32R)
        wl = sb("wl", [P, 2, KO, P], F32R)
        kqr = sb("kqr", [P, 4, TP], F32R)
        grow = sb("grow", [1, SEQ], F32R)
        crow = sb("crow", [2, TP], F32R)
        ARENA = 21800
        arena = sb("arena", [P, ARENA])
        ps = ctx.enter_context(nc.psum_tensor("ps", [P, 8, 512], F32))

        at = [0]

        def carve(n):
            at[0] += n
            assert at[0] <= ARENA, at[0]
            return arena[:, at[0] - n:at[0]]

        h_t = carve(KO * TP).rearrange("p (k t) -> p k t", k=KO)
        sq2 = [carve(TP), carve(TP)]
        rstd = carve(TP)
        xrow = [carve(D), carve(D)]
        prow = carve(P)
        causal_f = carve(2 * P)
        at[0] = 0
        reset = carve(TP)
        ar = carve(2 * TW).rearrange("p (a t) -> p a t", a=2)
        b_t, k_t, v_t = carve(TW), carve(TW), carve(TW)
        zz, bon, y_t, sq, mix = (carve(TP) for _ in range(5))
        mut = carve(TP + 1)
        upall, lo, upf = carve(D), carve(TP), carve(P)
        st, pc = carve(P), carve(2 * NT)
        shared = at[0]
        lw, cum, aa, kr, kk, rr = (carve(TP) for _ in range(6))
        e_in = y_t
        at[0] = shared
        rows_sb = [carve(4 * P).rearrange("p (a t) -> p a t", a=4) for _ in range(2)]
        amat = [[carve(4 * P) for _ in range(2)] for _ in range(2)]
        xs = carve(4 * P).rearrange("p (e a t) -> p e a t", e=2, a=2)
        pm = carve(2 * P).rearrange("p (e t) -> p e t", e=2)
        wu = [carve(2 * P).rearrange("p (a t) -> p a t", a=2) for _ in range(2)]
        qs, us, sp = carve(P), carve(P), carve(P)
        at[0] = KO * TP
        vflat = carve(NT * 2 * P).rearrange("p (t x) -> p t x", t=NT)
        kb, qb, zb, vb, bsq, brs = (carve(TP) for _ in range(6))
        pt = [carve(512) for _ in range(3)]
        dln = carve(512)
        ob = carve(SEQ)
        mcol = carve(KO)
        cb = carve(2 * NT).rearrange("p (t e) -> p t e", e=2)
        ccol = carve(NT * H).rearrange("p (t h) -> p t h", h=H)
        at[0] = KO * TP
        fin = [carve(SEQ), carve(SEQ)]
        fo = [carve(SEQ).rearrange("p (t c) -> p t c", t=KO) for _ in range(2)]
        osq = [carve(TP), carve(TP)]

        G = [ps[:, 0:3, 0:SEG], ps[:, 3:6, 0:SEG]]

        def seg3(a):
            return a.rearrange("p (c t) -> p c t", c=3)

        def param(c, n=1):
            return params[:, c:c + n]

        def q(i):
            return pp[:, i:i + 1]

        def f32(a):
            return a.bitcast(F32)

        TILE_TOK = [META] + [P] * KO
        TILE_AT = [0] + [META + P * i for i in range(KO)]
        N_A = 1
        N_AO = N_A + 4 * KO
        N_F = N_AO + KO
        N_B = N_F + 1
        N_BO = N_B + 4 * KO
        A_ORDER = [Q_MUK, Q_MUV, Q_MUR, Q_MUZ]
        UNITS = [(qb_, kt) for qb_ in range(2) for kt in range(4 * qb_ + 5)]

        block = ctx.enter_context(nc.Block())

        @block.sync
        def _(sp_):
            sync = sp_
            for dst, src in ((ident[:, :], ident_d), (masks[:, :], masks_d), (levels[:, :], levels_d),
                             (causal_f, causal_d), (fb_in[0:H, :], f_bias)):
                sync.dma_start(dst, src).then_inc(S.consts_loaded, 16)
            sync.dma_start(prow[0:NROWS, :], rows).then_inc(S.rows_loaded, 16)
            sync.dma_start(xrow[0][0:META, :], meta).then_inc(X_LOADED[0], 16)
            for t in range(1, NT):
                if t >= 2:
                    sync.wait_ge(S.x_tr, t - 1)
                sync.dma_start(xrow[t % 2][:, :], x[(t - 1) * P:t * P, :]).then_inc(X_LOADED[t % 2], 16)

            def load_w(n, src, slot, wait):
                if wait is not None:
                    sync.wait_ge(S.w_lo, wait)
                    if not isinstance(wait, int):
                        sync.sem_inc(S.w_asked, 1)
                sync.dma_start(wr[:, slot, :, 0:src.shape[2]], src).then_inc(W_LOADED[slot], 16)

            wi = w_in.rearrange("(k p) n -> p k n", p=P)
            kvw = kv_w.rearrange("(k p) n -> p k n", p=P)
            bw = b_w_in.rearrange("(k p) n -> p k n", p=P)
            load_w(0, wi[:, :, 4 * D:4 * D + P], 0, None)
            sync.wait_ge(S.xt_stored, 16)
            sync.wait_ge(S.x_lo, KO)
            sync.dma_start(upall, up).then_inc(S.up_loaded, 16)
            with sync.Fori(0, KO) as p:
                cols = [sync.snap(p * P + base) for base in (D, 2 * D, 0, 3 * D)]
                for j, col in enumerate(cols):
                    load_w(None, wi[:, :, bass.ds(col, P)], (N_A + j) % 2, 4 * p + N_A + j)
            wo = w_out.rearrange("(k p) n -> p k n", p=P)
            for m in range(KO):
                if m == 0:
                    sync.wait_ge(S.pair_free, KO + 1)
                    sync.dma_start(h_t.rearrange("p k t -> p (k t)"), xt_scr).then_inc(S.xt_loaded, 16)
                    for k in range(KO):
                        if k >= 2:
                            sync.wait_ge(S.x_lo, KO + k - 1)
                        sync.dma_start(osq[k % 2], oa_scr[k]).then_inc(O_LOADED[k % 2], 16)
                        if k == 0:
                            load_w(N_AO, wo[:, :, 0:P], N_AO % 2, N_AO)
                        if k == 1:
                            load_w(N_AO + 1, wo[:, :, P:2 * P], (N_AO + 1) % 2, N_AO + 1)
                elif m >= 2:
                    load_w(N_AO + m, wo[:, :, m * P:(m + 1) * P], (N_AO + m) % 2, N_AO + m)
            load_w(N_F, kvw[:, :, 2 * D:2 * D + H], N_F % 2, N_F)
            with sync.Fori(0, KO) as p:
                cols = [sync.snap(p * P + base) for base in (0, D)]
                heads = [sync.snap(2 * p + e) for e in range(2)]
                for j, (w, col) in enumerate(((kvw, cols[0]), (bw, cols[0]), (kvw, cols[1]), (bw, cols[1]))):
                    load_w(None, w[:, :, bass.ds(col, P)], (N_B + j) % 2, 4 * p + N_B + j)
                for e in range(2):
                    if e == 0:
                        sync.wait_ge(S.bpair_free, p + 1)
                    else:
                        sync.wait_ge(S.smax_done, 16 * p + 8)
                    sync.dma_start(f32(crow[:, :]), c_scr[bass.ds(heads[e], 1)].rearrange("a b t -> (a b) t"))\
                        .then_inc(S.c_rows, 16)
            bwo = b_w_out.rearrange("(k p) n -> p k n", p=P)
            sync.wait_ge(S.bpair_free, KO + 1)
            for k in range(KO):
                if k >= 2:
                    sync.wait_ge(S.x_lo, 3 * KO + k - 1)
                sync.dma_start(osq[k % 2][:, 0:SEQ], ob_scr[k]).then_inc(O_LOADED[k % 2], 16)
                if k < 2:
                    load_w(N_BO + k, bwo[:, :, k * P:(k + 1) * P], (N_BO + k) % 2, N_BO + k)
            out_v = out.rearrange("(t p) c -> p t c", p=P)
            for m in range(KO):
                if m + 2 < KO:
                    n = N_BO + m + 2
                    load_w(n, bwo[:, :, (m + 2) * P:(m + 3) * P], n % 2, n)
                sync.wait_ge(S.fin_evac, m + 1)
                sync.dma_start(out_v[:, :, m * P:(m + 1) * P], fo[m % 2]).then_inc(FIN_STORED[m % 2], 16)
            for i in range(2):
                sync.wait_ge(FIN_STORED[i], 16 * KO // 2)
            sync.wait_ge(S.c_stored, 16)

        @block.gpsimd
        def _(pool):
            pool.memset(f32(ones_r[:, :]), 1.0).then_inc(S.setup_pool, 1)
            pool.memset(head_ones[:, :], 0.0).then_inc(S.setup_pool, 1)
            pool.wait_ge(S.setup_pool, 2)
            for e in range(2):
                b = slice(e * HD, (e + 1) * HD)
                pool.memset(head_ones[b, b], 1.0).then_inc(S.setup_pool, 1)
            pool.wait_ge(S.setup_pool, 4)
            pool.wait_ge(S.x_evac, NT)
            pool.wait_ge(S.pads_zero, 1)
            pool.dma_start(xt_scr, h_t.rearrange("p k t -> p (k t)")).then_inc(S.xt_stored, 16)

            def scale_w(slot, gain, loaded, width=P):
                pool.wait_ge(W_LOADED[slot], loaded)
                pool.tensor_tensor(wr[:, slot, :, 0:width], wr[:, slot, :, 0:width],
                                   param(gain, KO).unsqueeze(2).to_broadcast([P, KO, width]),
                                   ALU.mult).then_inc(S.w_scaled, 1)

            pool.wait_ge(S.param_derived, 4)
            scale_w(0, C_AN, 16)
            pool.wait_ge(S.xt_stored, 16)
            pool.wait_ge(S.x_lo, KO)
            pool.wait_ge(S.shifted, 1)
            pool.sem_inc(S.pair_free, 1)
            with pool.Fori(0, KO) as p:
                v = p + 1
                for j in range(4):
                    scale_w((N_A + j) % 2, C_AN, 32 * p + 16 * ((N_A + j) // 2 + 1))
                pool.wait_ge(S.cumlog, v)
                pool.tensor_tensor(lw, cum, lw, ALU.subtract).then_inc(S.cum_before, 1)
                pool.wait_ge(S.k_mix, v)
                pool.wait_ge(S.shifted, 4 * p + 2)
                pool.wait_ge(S.kk_raw, v)
                pool.tensor_tensor(kr, kr, mix, ALU.mult).then_inc(S.k_new, 1)
                pool.wait_ge(S.exp_neg, v)
                pool.wait_ge(S.k_new, v)
                pool.tensor_tensor(k_t[:, OFF:], kr, cum, ALU.mult).then_inc(S.k_tilde, 1)
                pool.wait_ge(S.kk_norm, v)
                pool.wait_ge(S.kk_sumsq, v)
                pool.tensor_tensor(sq, kk, aa, ALU.mult).then_inc(S.kk_a, 1)
                pool.wait_ge(S.kk_a, v)
                pool.tensor_tensor(b_t[:, OFF:], sq, cum, ALU.mult).then_inc(S.b_tilde, 1)
                pool.wait_ge(S.out_ready, v)
                pool.dma_start(oa_scr[bass.ds(p, 1)].rearrange("a p t -> (a p) t"), y_t).then_inc(S.out_stored, 16)
                pool.wait_ge(S.out_stored, 16 * v)
                pool.sem_inc(S.pair_free, 1)
            scale_w(N_F % 2, C_KVN, 16 * (N_F // 2 + 1), H)
            pool.wait_ge(S.c_lo, 1)
            pool.dma_start(c_scr[:, 0, :], f32(kqr[0:H, 0, :])).then_inc(S.c_stored, 16)
            pool.wait_ge(S.c_stored, 16)
            pool.dma_start(c_scr[:, 1, :], f32(kqr[0:H, 1, :])).then_inc(S.c_stored, 16)
            pool.wait_ge(S.c_stored, 32)
            pool.sem_inc(S.bpair_free, 1)
            with pool.Fori(0, KO) as p:
                for j, gain in enumerate((C_KVN, C_BN, C_KVN, C_BN)):
                    scale_w((N_B + j) % 2, gain, 32 * p + 16 * ((N_B + j) // 2 + 1))
                pool.wait_ge(S.o_gated, p + 1)
                pool.dma_start(ob_scr[bass.ds(p, 1)].rearrange("a p t -> (a p) t"), ob).then_inc(S.ob_stored, 16)
                pool.wait_ge(S.ob_stored, 16 * p + 16)
                pool.sem_inc(S.bpair_free, 1)

        @block.scalar
        def _(act):
            def split_hi(slot, loaded, scaled, hi_free, width=P):
                if scaled is None:
                    act.wait_ge(W_LOADED[slot], loaded)
                else:
                    act.wait_ge(S.w_scaled, scaled)
                if hi_free is not None:
                    act.wait_ge(S.proj_done, hi_free)
                act.activation(wh[:, slot, :, 0:width], wr[:, slot, :, 0:width], ACT.Copy).then_inc(S.w_hi, 1)

            def normalise(r):
                for k in range(KO):
                    if k >= 2:
                        act.wait_ge(S.h_sumsq, KO * r + k - 1)
                    if r:
                        act.wait_ge(S.res_added, k + 1)
                    else:
                        act.wait_ge(S.x_evac, NT)
                        act.wait_ge(S.pads_zero, 1)
                    act.activation(sq2[k % 2], h_t[:, k, :], ACT.Square).then_inc(S.h_sq, 1)
                act.wait_ge(S.h_sumsq, KO * (r + 1))
                act.wait_ge(S.setup_dve, 3)
                act.activation(seg3(rstd), G[0], ACT.Ln, scale=1.0 / D, bias=EPS_RMS).then_inc(S.h_ln, 1)
                act.wait_ge(S.h_ln, r + 1)
                act.activation(rstd, rstd, ACT.Exp, scale=-0.5).then_inc(S.h_rstd, 1)
                for k in range(KO):
                    act.wait_ge(S.xn_mul, KO * r + k + 1)
                    act.activation(xh[:, k, :], sq2[k % 2], ACT.Copy).then_inc(S.x_hi, 1)

            def shift_mu(parity, mu, done, free):
                act.wait_ge(S.proj_done, done)
                act.wait_ge(S.shifted, free)
                act.activation(seg3(mut[:, 1:]), G[parity], ACT.Copy, scale=mu).then_inc(S.mu_done, 1)

            normalise(0)
            split_hi(0, None, 1, None)
            act.wait_ge(S.proj_done, 1)
            act.activation(seg3(mut[:, 1:]), G[0], ACT.Copy, scale=param(C_LORA)).then_inc(S.mu_done, 1)
            act.wait_ge(S.shifted, 1)
            act.activation(lo[0:LORA, :], lo[0:LORA, :], ACT.Tanh).then_inc(S.lora_tanh, 1)
            with act.Fori(0, KO) as p:
                v = p + 1
                act.wait_ge(S.pair_free, v)
                act.wait_ge(S.pair_params, v)
                act.wait_ge(S.up_loaded, 16)
                act.activation(upf, upall[:, bass.ds(p * P, P)], ACT.Copy).then_inc(S.up_copied, 1)
                split_hi((N_A + 0) % 2, None, 4 * p + 2, None)
                split_hi((N_A + 1) % 2, None, 4 * p + 3, 4 * p + 1)
                act.wait_ge(S.dec_done, v)
                act.activation(seg3(lw), G[0], ACT.Tanh, scale=0.5, bias=q(Q_HDB)).then_inc(S.dec_tanh, 1)
                act.wait_ge(S.icl_done, v)
                act.activation(seg3(aa), G[1], ACT.Tanh, scale=0.5, bias=q(Q_HIB)).then_inc(S.icl_tanh, 1)
                shift_mu(0, q(Q_MUK), 4 * p + 2, 4 * p + 1)
                split_hi((N_A + 2) % 2, None, 4 * p + 4, 4 * p + 2)
                shift_mu(1, q(Q_MUV), 4 * p + 3, 4 * p + 2)
                split_hi((N_A + 3) % 2, None, 4 * p + 5, 4 * p + 3)
                act.activation(kk, kr, ACT.Copy, scale=q(Q_KK)).then_inc(S.kk_raw, 1)
                act.wait_ge(S.kk_raw, v)
                act.activation(sq, kk, ACT.Square).then_inc(S.kk_sq, 1)
                act.wait_ge(S.iclr, v)
                act.activation(mix, aa, ACT.Identity, scale=q(Q_KA), bias=q(Q_NKA)).then_inc(S.k_mix, 1)
                act.wait_ge(S.cumlog, v)
                act.activation(e_in, cum, ACT.Exp).then_inc(S.exp_in, 1)
                act.wait_ge(S.cum_before, v)
                act.activation(cum, cum, ACT.Exp, scale=-1.0).then_inc(S.exp_neg, 1)
                act.activation(lw, lw, ACT.Exp).then_inc(S.exp_before, 1)
                shift_mu(0, q(Q_MUR), 4 * p + 4, 4 * p + 3)
                shift_mu(0, q(Q_MUZ), 4 * p + 5, 4 * p + 4)
                act.wait_ge(S.kk_guard, v)
                act.activation(bon, bon, ACT.Ln, scale=LN_SCALE)\
                    .then_inc(S.kk_ln, 1)
                act.wait_ge(S.kk_ln, v)
                act.activation(bon, bon, ACT.Exp, scale=-0.5, bias=LN_BACK).then_inc(S.kk_rn, 1)
                act.wait_ge(S.shifted, 4 * p + 5)
                act.wait_ge(S.bonus_sum, v)
                act.activation(mix, zz, ACT.Tanh, scale=0.5).then_inc(S.z_tanh, 1)

                def chain_act(u, slot):
                    n = 18 * p + 2 * u
                    if slot in (0, 2):
                        c = 2 * u + slot // 2
                        if c == 0:
                            act.wait_ge(S.state_zero, v)
                        else:
                            act.wait_ge(S.s_ready, 36 * p + 2 * c)
                        act.activation(sp, st, ACT.Copy, scale=pc[:, c:c + 1]).then_inc(S.s_scaled, 1)
                    if slot == 4:
                        act.wait_ge(S.y_done, 9 * p + u + 1)
                        lo_, n_ = (OFF, META) if u == 0 else (0, P)
                        act.activation(y_t[:, TILE_AT[u]:TILE_AT[u] + n_], ps[:, 2, lo_:P], ACT.Copy)\
                            .then_inc(S.y_copied, 1)

                for u in range(NT):
                    act.wait_ge(S.tr_done, 9 * p + u + 1)
                    if u == 0:
                        act.wait_ge(S.bonus_prod, v)
                        act.wait_ge(S.b_tilde, v)
                        act.wait_ge(S.chunk_end, v)
                    if u >= 2:
                        act.wait_ge(S.y_done, 9 * p + u - 1)
                    act.activation(rows_sb[u % 2].rearrange("p a t -> p (a t)"), ps[:, 4, :], ACT.Copy)\
                        .then_inc(S.rows_ready, 1)
                    act.wait_ge(S.q_done, 9 * p + u + 1)
                    act.activation(qs, ps[:, 1, P:2 * P], ACT.Copy).then_inc(S.q_copied, 1)
                    if u:
                        for slot in range(5):
                            chain_act(u - 1, slot)
                for slot in range(5):
                    chain_act(NT - 1, slot)
                act.wait_ge(S.gn_centred, v)
                act.activation(sq, y_t, ACT.Square).then_inc(S.gn_sq, 1)
                act.wait_ge(S.gn_var, v)
                act.activation(seg3(sq), G[0], ACT.Ln, scale=1.0 / HD, bias=EPS_GN).then_inc(S.gn_ln, 1)
                act.wait_ge(S.gn_ln, v)
                act.activation(sq, sq, ACT.Exp, scale=-0.5).then_inc(S.gn_rstd, 1)

            def split_rows(r, width):
                for k in range(KO):
                    act.wait_ge(O_LOADED[k % 2], 16 * (KO // 2 * (r // 2) + k // 2 + 1))
                    act.activation(xh[:, k, 0:width], osq[k % 2][:, 0:width], ACT.Copy).then_inc(S.x_hi, 1)

            for n in (N_AO, N_AO + 1):
                split_hi(n % 2, 16 * (n // 2 + 1), None, n - 1)
                if n == N_AO:
                    split_rows(1, TP)
            for m in range(KO - 2):
                n = N_AO + m + 2
                split_hi(n % 2, 16 * (n // 2 + 1), None, n - 1)
            normalise(1)
            n = N_F
            split_hi(n % 2, None, N_AO + 1, n - 1, H)
            act.wait_ge(S.f_logit, 1)
            act.activation(brs[0:H, :], bsq[0:H, :], ACT.Abs).then_inc(S.f_abs, 1)
            act.wait_ge(S.f_abs, 1)
            act.activation(brs[0:H, :], brs[0:H, :], ACT.Exp, scale=-1.0).then_inc(S.f_exp, 1)
            act.wait_ge(S.f_exp, 1)
            act.activation(brs[0:H, :], brs[0:H, :], ACT.Ln, bias=1.0).then_inc(S.f_ln, 1)
            act.wait_ge(S.c_scaled, 1)
            act.activation(kqr[0:H, 0, :], bsq[0:H, :], ACT.Copy).then_inc(S.c_hi, 1)
            with act.Fori(0, KO) as p:
                v = p + 1
                n = 4 * p + N_B
                act.wait_ge(S.bpair_free, v)
                split_hi((N_B + 0) % 2, None, 4 * p + N_AO + 2, n - 1)
                split_hi((N_B + 1) % 2, None, 4 * p + N_AO + 3, n)
                for j, dst in enumerate((kb, qb)):
                    act.wait_ge(S.proj_done, n + j + 1)
                    act.activation(seg3(dst), G[j], ACT.Copy).then_inc(S.b_evac, 1)
                    split_hi((N_B + 2 + j) % 2, None, 4 * p + N_AO + 4 + j, n + j + 1)
                for j, src in enumerate((kb, qb)):
                    act.wait_ge(S.b_evac, 4 * p + (j + 1 if j == 0 else 2))
                    if j:
                        act.wait_ge(S.hn_sumsq, 2 * p + 1)
                    act.activation(bsq, src, ACT.Square).then_inc(S.hn_sq, 1)
                    if j == 0:
                        act.wait_ge(S.proj_done, n + 3)
                        act.activation(seg3(vb), G[0], ACT.Copy).then_inc(S.b_evac, 1)
                    act.wait_ge(S.hn_sumsq, 2 * p + j + 1)
                    if j:
                        act.wait_ge(S.hn_full, 2 * p + 1)
                    act.activation(seg3(brs), G[1], ACT.Ln, scale=1.0 / HD, bias=EPS_RMS).then_inc(S.hn_ln, 1)
                    act.wait_ge(S.hn_ln, 2 * p + j + 1)
                    act.activation(brs, brs, ACT.Exp, scale=-0.5).then_inc(S.hn_rstd, 1)
                    act.wait_ge(S.hn_full, 2 * p + j + 1)
                    act.activation(kqr[:, 2 * j, :], src, ACT.Copy).then_inc(S.kq_hi, 1)
                act.wait_ge(S.proj_done, n + 4)
                act.activation(seg3(zb), G[0], ACT.Copy).then_inc(S.b_evac, 1)
                act.wait_ge(S.b_evac, 4 * p + 4)
                act.activation(bsq, zb, ACT.Tanh, scale=0.5).then_inc(S.bz_tanh, 1)
                for e in range(2):
                    for a in range(2):
                        act.wait_ge(S.m_row_done, 4 * p + 2 * e + a + 1)
                        act.activation(grow[0:1, a * 512:(a + 1) * 512], ps[0:1, 7, :], ACT.Copy, scale=-1.0)\
                            .then_inc(S.m_row, 1)
                    for w, (qb_, kt) in enumerate(UNITS):
                        n_k = TILE_TOK[kt]
                        q0 = max(qb_ * 512, (kt - 1) * P)
                        n_q = qb_ * 512 + 512 - q0
                        base = 28 * p + 14 * e + w
                        act.wait_ge(S.st_done, base + 1)
                        if w >= 3:
                            act.wait_ge(S.pv_done, base - 2)
                        act.activation(pt[w % 3][0:n_k, 0:n_q], ps[0:n_k, 3 + w % 3, 0:n_q], ACT.Exp,
                                       scale=SCALE, bias=cb[0:n_k, kt, e:e + 1]).then_inc(S.p_exp, 1)
                        if kt == 4 * qb_ + 4:
                            b, o = slice(e * HD, (e + 1) * HD), slice((1 - e) * HD, (2 - e) * HD)
                            act.wait_ge(S.pv_done, base + 1)
                            if e or qb_:
                                act.wait_ge(S.o_norm, 4 * p + 2 * e + qb_)
                            act.activation(dln[b, :], ps[o, 6, :], ACT.Ln).then_inc(S.d_ln, 1)
                            act.wait_ge(S.d_ln, 4 * p + 2 * e + qb_ + 1)
                            act.activation(dln[b, :], dln[b, :], ACT.Exp, scale=-1.0).then_inc(S.d_recip, 1)
            for n in (N_BO, N_BO + 1):
                split_hi(n % 2, 16 * (n // 2 + 1), None, n - 1)
                if n == N_BO:
                    split_rows(3, SEQ)
            for m in range(KO):
                n = N_BO + m + 2
                if m < KO - 2:
                    split_hi(n % 2, 16 * (n // 2 + 1), None, n - 1)
                act.wait_ge(S.fin_tr, m + 1)
                if m >= 2:
                    act.wait_ge(FIN_STORED[m % 2], 16 * (m // 2))
                act.activation(fo[m % 2].rearrange("p (b t) c -> p b (t c)", b=2), ps[:, 4 + 2 * (m % 2):6 + 2 * (m % 2), :],
                               ACT.Copy).then_inc(S.fin_evac, 1)

        @block.vector
        def _(dve):
            def split_lo(slot, n, width=P):
                dve.wait_ge(S.w_hi, n + 1)
                dve.tensor_tensor(wl[:, slot, :, 0:width], wr[:, slot, :, 0:width], f32(wh[:, slot, :, 0:width]),
                                  ALU.subtract).then_inc(S.w_lo, 1)

            def normalise(r):
                dve.wait_ge(S.h_rstd, r + 1)

                def lo(k):
                    dve.wait_ge(S.x_hi, 2 * KO * r + k + 1)
                    dve.tensor_tensor(xl[:, k, :], sq2[k % 2], f32(xh[:, k, :]), ALU.subtract).then_inc(S.x_lo, 1)
                for k in range(KO):
                    if k >= 2:
                        lo(k - 2)
                        dve.wait_ge(S.x_lo, 2 * KO * r + k - 1)
                    dve.tensor_tensor(sq2[k % 2], h_t[:, k, :], rstd, ALU.mult).then_inc(S.xn_mul, 1)
                lo(KO - 2)
                lo(KO - 1)

            def shift(dst, parity, keep, count, extra=None):
                dve.wait_ge(S.mu_done, count)
                dve.scalar_tensor_tensor(seg3(dst), G[parity], keep, seg3(mut[:, 0:TP]), ALU.mult, ALU.add)\
                    .then_inc(S.shifted, 1)

            for i, val in enumerate((RMS_EPS, GN_EPS, 0.5 * float(np.log(LN_SCALE)))):
                dve.memset(cst[:, i:i + 1], val).then_inc(S.setup_dve, 1)
            dve.memset(all_ones[:, :], 1.0).then_inc(S.setup_dve, 1)
            dve.wait_ge(S.consts_loaded, 80)
            dve.tensor_copy(causal[:, :], causal_f).then_inc(S.setup_dve, 1)
            dve.tensor_copy(identb[:, :], ident[:, :]).then_inc(S.setup_dve, 1)
            dve.memset(h_t[:, :, T:TP], 0.0).then_inc(S.pads_zero, 1)
            for t in range(NT):
                dve.wait_ge(S.x_tr, t + 1)
                g, n = 2 * (t % 2), TILE_TOK[t]
                dve.tensor_copy(h_t[:, :, TILE_AT[t]:TILE_AT[t] + n],
                                ps[:, g:g + 2, :].rearrange("p b (k t) -> p (b k) t", k=4)[:, :, 0:n])\
                    .then_inc(S.x_evac, 1)
            dve.wait_ge(S.param_tr, 1)
            dve.tensor_copy(params[:, 0:ROW_LORA], ps[:, 6, 0:ROW_LORA]).then_inc(S.param_copied, 1)
            dve.tensor_copy(params[:, C_LORA:C_LORA + NROWS - ROW_LORA], ps[:, 6, ROW_LORA:NROWS])\
                .then_inc(S.param_copied, 1)
            dve.wait_ge(S.param_copied, 2)
            dve.tensor_scalar(param(Q_NR * KO, 4 * KO), param(Q_MUR * KO, 4 * KO), -1.0, 1.0, ALU.mult, ALU.add)\
                .then_inc(S.param_derived, 1)
            dve.tensor_scalar(param(Q_HDB * KO, 2 * KO), param(Q_DB * KO, 2 * KO), 0.5, None, ALU.mult)\
                .then_inc(S.param_derived, 1)
            dve.tensor_scalar(param(Q_NKA * KO, KO), param(Q_KA * KO, KO), -1.0, 1.0, ALU.mult, ALU.add)\
                .then_inc(S.param_derived, 1)
            dve.tensor_scalar(param(C_NLORA), param(C_LORA), -1.0, 1.0, ALU.mult, ALU.add)\
                .then_inc(S.param_derived, 1)
            normalise(0)
            dve.wait_ge(S.xt_stored, 16)
            dve.wait_ge(S.x_lo, KO)
            dve.memset(reset, 1.0).then_inc(S.setup_dve, 1)
            dve.wait_ge(S.setup_dve, 7)
            dve.memset(reset[:, 0:1], 0.0).then_inc(S.setup_dve, 1)
            dve.memset(reset[:, META:TP:CH], 0.0).then_inc(S.setup_dve, 1)
            dve.memset(ar[:, :, 0:OFF], 0.0).then_inc(S.setup_dve, 1)
            for a in (b_t, k_t, v_t):
                dve.memset(a[:, 0:OFF], 0.0).then_inc(S.setup_dve, 1)
            dve.memset(mut[:, 0:1], 0.0).then_inc(S.setup_dve, 1)
            dve.memset(pc[:, 0:1], 1.0).then_inc(S.setup_dve, 1)
            dve.memset(f32(wl[:, 1, 0, 0:1]), 0.0).then_inc(S.w_lo, 1)
            dve.wait_ge(S.setup_dve, 15)
            split_lo(0, 0)
            dve.wait_ge(S.mu_done, 1)
            dve.scalar_tensor_tensor(seg3(lo), G[0], param(C_NLORA), seg3(mut[:, 0:TP]), ALU.mult, ALU.add)\
                .then_inc(S.shifted, 1)
            with dve.Fori(0, KO) as p:
                v = p + 1
                n = 4 * p + N_A
                dve.wait_ge(S.pair_free, v)
                dve.tensor_copy(pp[:, :].unsqueeze(2), param(0, NQ * KO).rearrange("p (q k) -> p q k", k=KO)[:, :, bass.ds(p, 1)])\
                    .then_inc(S.pair_params, 1)
                dve.memset(st, 0.0).then_inc(S.state_zero, 1)
                split_lo((N_A + 0) % 2, n)
                split_lo((N_A + 1) % 2, n + 1)
                dve.wait_ge(S.dec_tanh, v)
                dve.tensor_scalar(lw, lw, -C_DECAY, -C_DECAY, ALU.mult, ALU.add).then_inc(S.logw, 1)
                dve.wait_ge(S.icl_tanh, v)
                dve.tensor_scalar(aa, aa, 0.5, 0.5, ALU.mult, ALU.add).then_inc(S.iclr, 1)
                dve.wait_ge(S.logw, v)
                dve.tensor_tensor_scan(cum, reset, lw, 0.0, ALU.mult, ALU.add).then_inc(S.cumlog, 1)
                dve.wait_ge(S.pair_params, v)
                shift(kr, 0, q(Q_NK), 4 * p + 2)
                split_lo((N_A + 2) % 2, n + 2)
                shift(v_t[:, OFF:], 1, q(Q_NV), 4 * p + 3)
                split_lo((N_A + 3) % 2, n + 3)
                dve.wait_ge(S.exp_in, v)
                dve.tensor_copy(pc[:, 1:2 * NT], e_in[:, META - 1:T:CH]).then_inc(S.chunk_end, 1)
                shift(rr, 0, q(Q_NR), 4 * p + 4)
                dve.wait_ge(S.shifted, 4 * p + 4)
                dve.tensor_tensor(ar[:, 1, OFF:], rr, e_in, ALU.mult).then_inc(S.r_tilde, 1)
                dve.wait_ge(S.kk_sumsq, v)
                dve.tensor_scalar(seg3(bon), G[1], KK_FLOOR ** 2, None, ALU.max).then_inc(S.kk_guard, 1)
                dve.wait_ge(S.k_new, v)
                dve.wait_ge(S.k_mix, v)
                dve.scalar_tensor_tensor(mix, rr, q(Q_RK), kr, ALU.mult, ALU.mult).then_inc(S.bonus_prod, 1)
                shift(zz, 0, q(Q_NZ), 4 * p + 5)
                dve.wait_ge(S.kk_rn, v)
                dve.tensor_tensor(kk, kk, bon, ALU.mult).then_inc(S.kk_norm, 1)
                dve.wait_ge(S.kk_norm, v)
                dve.wait_ge(S.exp_before, v)
                dve.scalar_tensor_tensor(ar[:, 0, OFF:], kk, -1.0, lw, ALU.mult, ALU.mult).then_inc(S.a_tilde, 1)
                dve.wait_ge(S.bonus_sum, v)
                dve.tensor_tensor(seg3(bon), G[1], seg3(v_t[:, OFF:]), ALU.mult).then_inc(S.bonus, 1)
                dve.wait_ge(S.z_tanh, v)
                dve.scalar_tensor_tensor(zz, mix, 1.0, zz, ALU.add, ALU.mult).then_inc(S.z_gate, 1)

                def chain_dve(u, slot):
                    if slot == 4:
                        return
                    h, c = slot // 2, 2 * u + slot // 2
                    b = slice(h * CH, (h + 1) * CH)
                    if slot % 2 == 0:
                        dve.wait_ge(S.u_done, 18 * p + c + 1)
                        if h == 0 and u:
                            dve.wait_ge(S.y_done, 9 * p + u)
                        dve.wait_ge(S.wu_copied, 9 * p + u + 1)
                        dve.tensor_tensor(us[b, :], ps[b, 7, 0:P], wu[u % 2][b, 1, :], ALU.add).then_inc(S.u_ready, 1)
                    else:
                        dve.wait_ge(S.s_done, 18 * p + c + 1)
                        dve.wait_ge(S.s_scaled, 18 * p + c + 1)
                        for e in range(2):
                            d = slice(e * HD, (e + 1) * HD)
                            dve.scalar_tensor_tensor(st[d, d], ps[d, 0, d], pc[d, c:c + 1], sp[d, d],
                                                     ALU.mult, ALU.add).then_inc(S.s_ready, 1)

                for u in range(NT):
                    t9 = 9 * p + u
                    for e in range(2):
                        dve.wait_ge(S.a_done, 2 * t9 + e + 1)
                        if u >= 2:
                            dve.wait_ge(S.y_done, t9 - 1)
                        dve.tensor_tensor(amat[u % 2][e].rearrange("p (a t) -> p a t", a=2),
                                          ps[:, 3 + e, :].rearrange("p (a t) -> p a t", a=2),
                                          masks[:, :].unsqueeze(1).to_broadcast([P, 2, 2 * P]), ALU.mult)\
                            .then_inc(S.a_masked, 1)
                    for l in range(6):
                        n6 = 6 * t9 + l
                        dve.wait_ge(S.p_done, n6 + 1)
                        dve.tensor_tensor(pm, ps[:, 5, 0:2 * P].rearrange("p (e t) -> p e t", e=2),
                                          levels[:, l * P:(l + 1) * P].unsqueeze(1).to_broadcast([P, 2, P]), ALU.mult)\
                            .then_inc(S.p_masked, 1)
                        dve.wait_ge(S.x_done, n6 + 1)
                        old = xs.rearrange("p e a t -> p (e a) t") if l else \
                            ident[:, :].unsqueeze(1).to_broadcast([P, 4, P])
                        dve.tensor_tensor(xs.rearrange("p e a t -> p (e a) t"),
                                          ps[:, 6, :].rearrange("p (a t) -> p a t", a=4), old, ALU.add)\
                            .then_inc(S.x_added, 1)
                        if u and l < 5:
                            chain_dve(u - 1, l)
                    dve.wait_ge(S.wu_done, t9 + 1)
                    dve.tensor_copy(wu[u % 2], ps[:, 1, :].rearrange("p (a t) -> p a t", a=4)[:, 0:3:2, :])\
                        .then_inc(S.wu_copied, 1)
                for slot in range(5):
                    chain_dve(NT - 1, slot)
                dve.wait_ge(S.gn_mean, v)
                dve.scalar_tensor_tensor(seg3(y_t), G[1], -1.0 / HD, seg3(y_t), ALU.mult, ALU.add)\
                    .then_inc(S.gn_centred, 1)
                dve.wait_ge(S.gn_rstd, v)
                dve.tensor_tensor(y_t, y_t, sq, ALU.mult).then_inc(S.gn_scaled, 1)
                dve.wait_ge(S.gn_scaled, v)
                dve.tensor_scalar(y_t, y_t, q(Q_GW), q(Q_GB), ALU.mult, ALU.add).then_inc(S.gn_affine, 1)
                dve.wait_ge(S.gn_affine, v)
                dve.tensor_tensor(y_t, y_t, bon, ALU.add).then_inc(S.gn_bonus, 1)
                dve.wait_ge(S.gn_bonus, v)
                dve.scalar_tensor_tensor(y_t, y_t, 0.5, zz, ALU.mult, ALU.mult).then_inc(S.out_ready, 1)

            def split_rows(r, width):
                for k in range(KO):
                    dve.wait_ge(S.x_hi, KO * r + k + 1)
                    dve.tensor_tensor(xl[:, k, 0:width], osq[k % 2][:, 0:width], f32(xh[:, k, 0:width]), ALU.subtract)\
                        .then_inc(S.x_lo, 1)

            split_lo(N_AO % 2, N_AO)
            split_rows(1, TP)
            split_lo((N_AO + 1) % 2, N_AO + 1)
            dve.wait_ge(S.xt_loaded, 16)
            for m in range(KO):
                dve.wait_ge(S.proj_done, N_AO + m + 1)
                dve.tensor_tensor(seg3(h_t[:, m, :]), G[(N_AO + m) % 2], seg3(h_t[:, m, :]), ALU.add)\
                    .then_inc(S.res_added, 1)
                if m + 2 < KO:
                    split_lo((N_AO + m) % 2, N_AO + m + 2)
            normalise(1)
            split_lo(N_F % 2, N_F, H)
            dve.wait_ge(S.x_lo, 3 * KO)
            dve.wait_ge(S.proj_done, N_F + 1)
            g = G[N_F % 2]
            dve.tensor_scalar(seg3(bsq[0:H, :]), g[0:H], fb_in[0:H, :], None, ALU.add).then_inc(S.f_logit, 1)
            dve.memset(zb[0:H, :], 1.0).then_inc(S.vone_ones, 1)
            dve.memset(vflat[:, :, HD:3 * HD], 1.0).then_inc(S.vone_ones, 1)
            dve.wait_ge(S.f_logit, 1)
            dve.tensor_scalar(kb[0:H, :], bsq[0:H, :], 0.0, None, ALU.min).then_inc(S.f_min, 1)
            dve.wait_ge(S.f_min, 1)
            dve.wait_ge(S.f_ln, 1)
            dve.tensor_tensor(kb[0:H, :], kb[0:H, :], brs[0:H, :], ALU.subtract).then_inc(S.f_log, 1)
            dve.wait_ge(S.f_log, 1)
            dve.wait_ge(S.vone_ones, 2)
            dve.tensor_tensor_scan(vb[0:H, :], zb[0:H, :], kb[0:H, :], 0.0, ALU.mult, ALU.add).then_inc(S.f_cum, 1)
            dve.wait_ge(S.f_cum, 1)
            dve.tensor_scalar(bsq[0:H, :], vb[0:H, :], -1.0 / SCALE, None, ALU.mult).then_inc(S.c_scaled, 1)
            dve.wait_ge(S.c_tr, 1)
            dve.tensor_scalar(ccol[0:META, 0, :], ps[0:META, 6, 0:H], -1.0, None, ALU.mult).then_inc(S.c_col, 1)
            dve.tensor_scalar(ccol[:, 1:, :], ps[:, 6, H:NT * H].rearrange("p (t h) -> p t h", h=H), -1.0, None,
                              ALU.mult).then_inc(S.c_col, 1)
            dve.wait_ge(S.c_hi, 1)
            dve.tensor_tensor(kqr[0:H, 1, :], bsq[0:H, :], f32(kqr[0:H, 0, :]), ALU.subtract).then_inc(S.c_lo, 1)
            dve.wait_ge(S.c_col, 2)
            with dve.Fori(0, KO) as p:
                v = p + 1
                n = 4 * p + N_B
                dve.wait_ge(S.bpair_free, v)
                dve.tensor_copy(cb[0:META, 0, :], ccol[0:META, 0, bass.ds(2 * p, 2)]).then_inc(S.bias_col, 1)
                dve.tensor_copy(cb[:, 1:, :], ccol[:, 1:, bass.ds(2 * p, 2)]).then_inc(S.bias_col, 1)
                for j in range(4):
                    split_lo((N_B + j) % 2, n + j)
                for j, (buf, gain) in enumerate(((kb, C_KN), (qb, C_QN))):
                    dve.wait_ge(S.hn_rstd, 2 * p + j + 1)
                    dve.scalar_tensor_tensor(buf, buf, param(gain), brs, ALU.mult, ALU.mult).then_inc(S.hn_full, 1)
                    dve.wait_ge(S.kq_hi, 2 * p + j + 1)
                    dve.tensor_tensor(kqr[:, 2 * j + 1, :], buf, f32(kqr[:, 2 * j, :]), ALU.subtract)\
                        .then_inc(S.kq_lo, 1)
                dve.wait_ge(S.v_tr, v)
                flat = ps[:, 3:6, :].rearrange("p b c -> p (b c)")
                for e in range(2):
                    c = slice(e * HD, (e + 1) * HD)
                    x0 = e * 3 * HD
                    dve.tensor_copy(vflat[0:META, 0, x0:x0 + HD], flat[0:META, c]).then_inc(S.v_rows, 1)
                    dve.tensor_copy(vflat[:, 1:, x0:x0 + HD],
                                    flat[:, P:NT * P].rearrange("p (t c) -> p t c", c=P)[:, :, c]).then_inc(S.v_rows, 1)
                dve.wait_ge(S.bz_tanh, v)
                dve.scalar_tensor_tensor(zb, bsq, 1.0, zb, ALU.add, ALU.mult).then_inc(S.bz_gate, 1)
                for e in range(2):
                    for t in range(KO):
                        dve.wait_ge(S.smax_done, 16 * p + 8 * e + t + 1)
                        if t == 0 and e:
                            dve.wait_ge(S.m_row_done, 4 * p + 2 * e)
                        dve.tensor_reduce(mcol[:, t:t + 1], ps[:, 0:3, :].rearrange("p b c -> p (b c)")
                                          [:, 512 - META:512 + (t + 1) * P], AX.X, ALU.max).then_inc(S.smax, 1)
                    b = slice(e * HD, (e + 1) * HD)
                    for qb_ in range(2):
                        dve.wait_ge(S.d_recip, 4 * p + 2 * e + qb_ + 1)
                        dve.tensor_tensor(ob[b, qb_ * 512:(qb_ + 1) * 512], ps[b, 6, :], dln[b, :], ALU.mult)\
                            .then_inc(S.o_norm, 1)
                dve.wait_ge(S.o_norm, 4 * p + 4)
                dve.wait_ge(S.bz_gate, v)
                dve.scalar_tensor_tensor(ob, ob, 0.5, zb[:, META:T], ALU.mult, ALU.mult).then_inc(S.o_gated, 1)
            split_lo(N_BO % 2, N_BO)
            split_rows(3, SEQ)
            split_lo((N_BO + 1) % 2, N_BO + 1)
            for m in range(KO):
                dve.wait_ge(S.proj_done, N_BO + m + 1)
                if m >= 2:
                    dve.wait_ge(S.fin_tr, m - 1)
                g = 2 * (m % 2)
                dve.tensor_tensor(fin[m % 2], ps[:, g:g + 2, :].rearrange("p b c -> p (b c)"), h_t[:, m, META:T],
                                  ALU.add).then_inc(S.fin_sum, 1)
                if m + 2 < KO:
                    split_lo((N_BO + m) % 2, N_BO + m + 2)

        @block.tensor
        def _(pe):
            def products(group, slot, width=P, segs=3, seg=SEG):
                for c in range(segs):
                    acc = group[0:width, c, 0:seg]
                    t = slice(c * seg, (c + 1) * seg)
                    for k in range(KO):
                        pe.matmul(acc, wh[:, slot, k, 0:width], xh[:, k, t], start=(k == 0), stop=False)
                        pe.matmul(acc, wl[:, slot, k, 0:width], xh[:, k, t], start=False, stop=False)
                        mm = pe.matmul(acc, wh[:, slot, k, 0:width], xl[:, k, t], start=False, stop=(k == KO - 1))
                return mm

            def over(group, lhs, src):
                for c in range(3):
                    mm = pe.matmul(group[:, c, :], lhs, src[:, c * SEG:(c + 1) * SEG], start=True, stop=True)
                return mm

            def sum_squares(r):
                for k in range(KO):
                    pe.wait_ge(S.h_sq, KO * r + k + 1)
                    for c in range(3):
                        mm = pe.matmul(G[0][:, c, :], all_ones[:, :], sq2[k % 2][:, c * SEG:(c + 1) * SEG],
                                       start=(k == 0), stop=(k == KO - 1))
                    mm.then_inc(S.h_sumsq, 1)

            pe.wait_ge(S.consts_loaded, 80)
            for t in range(NT):
                pe.wait_ge(X_LOADED[t % 2], 16 * (t // 2 + 1))
                if t >= 2:
                    pe.wait_ge(S.x_evac, t - 1)
                n = TILE_TOK[t]
                for k in range(KO):
                    mm = pe.transpose(ps[:, 2 * (t % 2) + k // 4, (k % 4) * P:(k % 4) * P + n],
                                      xrow[t % 2][0:n, k * P:(k + 1) * P], ident[0:n, 0:n])
                mm.then_inc(S.x_tr, 1)
            pe.wait_ge(S.rows_loaded, 16)
            pe.transpose(ps[:, 6, 0:NROWS], prow[0:NROWS, :], ident[0:NROWS, 0:NROWS]).then_inc(S.param_tr, 1)
            pe.wait_ge(S.x_evac, NT)
            pe.wait_ge(S.setup_dve, 6)
            sum_squares(0)
            pe.wait_ge(S.x_lo, KO)
            pe.wait_ge(S.w_lo, 2)
            pe.wait_ge(S.h_rstd, 1)
            products(G[0], 0).then_inc(S.proj_done, 1)
            pe.wait_ge(S.lora_tanh, 1)
            pe.wait_ge(S.setup_pool, 4)
            with pe.Fori(0, KO) as p:
                v = p + 1
                pe.wait_ge(S.pair_free, v)
                pe.wait_ge(S.up_copied, v)
                over(G[0], upf[0:LORA, :], lo[0:LORA, :]).then_inc(S.dec_done, 1)
                over(G[1], upf[LORA:, :], lo[LORA:, :]).then_inc(S.icl_done, 1)
                pe.wait_ge(S.w_lo, 4 * p + 3)
                pe.wait_ge(S.dec_tanh, v)
                products(G[0], (N_A + 0) % 2).then_inc(S.proj_done, 1)
                pe.wait_ge(S.w_lo, 4 * p + 4)
                pe.wait_ge(S.icl_tanh, v)
                products(G[1], (N_A + 1) % 2).then_inc(S.proj_done, 1)
                pe.wait_ge(S.w_lo, 4 * p + 5)
                pe.wait_ge(S.shifted, 4 * p + 2)
                products(G[0], (N_A + 2) % 2).then_inc(S.proj_done, 1)
                pe.wait_ge(S.kk_sq, v)
                pe.wait_ge(S.shifted, 4 * p + 3)
                over(G[1], head_ones[:, :], sq).then_inc(S.kk_sumsq, 1)
                pe.wait_ge(S.w_lo, 4 * p + 6)
                pe.wait_ge(S.shifted, 4 * p + 4)
                products(G[0], (N_A + 3) % 2).then_inc(S.proj_done, 1)
                pe.wait_ge(S.bonus_prod, v)
                pe.wait_ge(S.kk_guard, v)
                over(G[1], head_ones[:, :], mix).then_inc(S.bonus_sum, 1)
                for s, c in ((S.a_tilde, v), (S.r_tilde, v), (S.b_tilde, v), (S.k_tilde, v), (S.bonus, v),
                             (S.shifted, 4 * p + 5)):
                    pe.wait_ge(s, c)

                def chain_pe(u, slot):
                    h, c = slot // 2, 2 * u + slot // 2
                    b = slice(h * CH, (h + 1) * CH)
                    rows_u, t9 = rows_sb[u % 2], 9 * p + u
                    if slot in (0, 2):
                        if c == 0:
                            pe.wait_ge(S.state_zero, v)
                        else:
                            pe.wait_ge(S.s_ready, 36 * p + 2 * c)
                        pe.wait_ge(S.wu_copied, t9 + 1)
                        pe.matmul(ps[b, 7, 0:P], wu[u % 2][:, 0, b], st, start=True, stop=True).then_inc(S.u_done, 1)
                        if h == 0 and u:
                            pe.wait_ge(S.y_copied, t9)
                        pe.matmul(ps[:, 2, b], st, ar[:, 1, u * P + h * CH:u * P + (h + 1) * CH],
                                  start=(h == 0), stop=False, skip_group_check=True)
                        pe.matmul(ps[:, 0, 0:P], rows_u[b, 2, :], rows_u[b, 3, :], start=True, stop=False)
                    elif slot in (1, 3):
                        pe.wait_ge(S.u_ready, 18 * p + c + 1)
                        pe.matmul(ps[:, 0, 0:P], rows_u[b, 1, :], us[b, :], start=False, stop=True)\
                            .then_inc(S.s_done, 1)
                    else:
                        for e in range(2):
                            d = slice(e * HD, (e + 1) * HD)
                            pe.matmul(ps[d, 2, 0:P], us[:, d], amat[u % 2][e][:, P:2 * P], start=False, stop=False,
                                      skip_group_check=True)
                            mm = pe.matmul(ps[d, 2, 0:P], rows_u[:, 3, d], amat[u % 2][e][:, 3 * P:], start=False,
                                           stop=True, skip_group_check=True)
                        mm.then_inc(S.y_done, 1)

                for u in range(NT):
                    t9 = 9 * p + u
                    c = slice(u * P, (u + 1) * P)
                    rows_u = rows_sb[u % 2]
                    if u:
                        pe.wait_ge(S.a_masked, 2 * t9)
                    for i, src in enumerate((ar[:, 0, c], b_t[:, c], k_t[:, c], v_t[:, c])):
                        mm = pe.transpose(ps[:, 4, i * P:(i + 1) * P], src, ident[:, :])
                    mm.then_inc(S.tr_done, 1)
                    for e in range(2):
                        d = slice(e * HD, (e + 1) * HD)
                        if e:
                            pe.wait_ge(S.rows_ready, t9 + 1)
                        pe.matmul(ps[:, 3 + e, 0:2 * P], b_t[d, c], ar[d, :, c], start=True, stop=True)
                        pe.matmul(ps[:, 3 + e, 2 * P:], k_t[d, c], ar[d, :, c], start=True, stop=True)\
                            .then_inc(S.a_done, 1)
                    pe.wait_ge(S.a_masked, 2 * t9 + 2)
                    if u:
                        pe.wait_ge(S.wu_copied, t9)
                    for e in range(2):
                        d = slice(e * HD, (e + 1) * HD)
                        mm = pe.matmul(ps[:, 1, P + e * HD:P + (e + 1) * HD], amat[u % 2][e][:, 2 * P:3 * P],
                                       rows_u[:, 3, d], start=True, stop=True)
                    mm.then_inc(S.q_done, 1)
                    for l in range(6):
                        n6 = 6 * t9 + l
                        if l:
                            pe.wait_ge(S.x_added, n6)
                        for e in range(2):
                            mm = pe.matmul(ps[:, 5, e * P:(e + 1) * P], amat[u % 2][e][:, 0:P],
                                           xs[:, e, 0, :] if l else ident[:, :], start=True, stop=True)
                        mm.then_inc(S.p_done, 1)
                        pe.wait_ge(S.p_masked, n6 + 1)
                        for e in range(2):
                            xt_ = xs[:, e, 1, :] if l else ident[:, :]
                            pe.matmul(ps[:, 6, 2 * e * P:(2 * e + 1) * P], xt_, pm[:, e, :], start=True, stop=True)
                            mm = pe.matmul(ps[:, 6, (2 * e + 1) * P:(2 * e + 2) * P], pm[:, e, :], xt_,
                                           start=True, stop=True)
                        mm.then_inc(S.x_done, 1)
                        if u and l < 5:
                            chain_pe(u - 1, l)
                    pe.wait_ge(S.x_added, 6 * t9 + 6)
                    pe.wait_ge(S.q_copied, t9 + 1)
                    for e in range(2):
                        d = slice(e * HD, (e + 1) * HD)
                        pe.matmul(ps[d, 1, 0:P], rows_u[:, 0, d], xs[:, e, 1, :], start=True, stop=True)
                        mm = pe.matmul(ps[:, 1, 2 * P + e * HD:2 * P + (e + 1) * HD], xs[:, e, 1, :], qs[:, d],
                                       start=True, stop=True)
                    mm.then_inc(S.wu_done, 1)
                for slot in range(5):
                    chain_pe(NT - 1, slot)
                pe.wait_ge(S.y_copied, 9 * p + NT)
                over(G[1], head_ones[:, :], y_t).then_inc(S.gn_mean, 1)
                pe.wait_ge(S.gn_sq, v)
                over(G[0], head_ones[:, :], sq).then_inc(S.gn_var, 1)

            pe.wait_ge(S.x_lo, 2 * KO)
            for m in range(KO):
                n = N_AO + m
                pe.wait_ge(S.w_lo, n + 2)
                if m >= 2:
                    pe.wait_ge(S.res_added, m - 1)
                products(G[n % 2], n % 2).then_inc(S.proj_done, 1)
            pe.wait_ge(S.res_added, KO)
            sum_squares(1)
            pe.wait_ge(S.x_lo, 3 * KO)
            pe.wait_ge(S.w_lo, N_F + 2)
            products(G[N_F % 2], N_F % 2, H).then_inc(S.proj_done, 1)
            pe.wait_ge(S.f_cum, 1)
            for t in range(NT):
                c, n = slice(TILE_AT[t], TILE_AT[t] + TILE_TOK[t]), TILE_TOK[t]
                mm = pe.transpose(ps[0:n, 6, t * H:(t + 1) * H], vb[0:H, c], ident[0:H, 0:H])
            mm.then_inc(S.c_tr, 1)
            with pe.Fori(0, KO) as p:
                v = p + 1
                n = 4 * p + N_B
                pe.wait_ge(S.bpair_free, v)
                pe.wait_ge(S.w_lo, n + 2)
                products(G[0], (N_B + 0) % 2).then_inc(S.proj_done, 1)
                pe.wait_ge(S.w_lo, n + 3)
                products(G[1], (N_B + 1) % 2).then_inc(S.proj_done, 1)
                pe.wait_ge(S.w_lo, n + 4)
                pe.wait_ge(S.b_evac, 4 * p + 1)
                products(G[0], (N_B + 2) % 2).then_inc(S.proj_done, 1)
                pe.wait_ge(S.b_evac, 4 * p + 2)
                pe.wait_ge(S.hn_sq, 2 * p + 1)
                over(G[1], head_ones[:, :], bsq).then_inc(S.hn_sumsq, 1)
                pe.wait_ge(S.w_lo, n + 5)
                pe.wait_ge(S.b_evac, 4 * p + 3)
                products(G[0], (N_B + 3) % 2).then_inc(S.proj_done, 1)
                pe.wait_ge(S.hn_ln, 2 * p + 1)
                pe.wait_ge(S.hn_sq, 2 * p + 2)
                over(G[1], head_ones[:, :], bsq).then_inc(S.hn_sumsq, 1)
                pe.wait_ge(S.hn_ln, 2 * p + 2)
                flat = ps[:, 3:6, :].rearrange("p b c -> p (b c)")
                for t in range(NT):
                    c, nt = slice(TILE_AT[t], TILE_AT[t] + TILE_TOK[t]), TILE_TOK[t]
                    mm = pe.transpose(flat[0:nt, t * P:(t + 1) * P], vb[:, c], ident[:, :])
                mm.then_inc(S.v_tr, 1)
                pe.wait_ge(S.kq_lo, 2 * p + 2)
                pe.wait_ge(S.b_evac, 4 * p + 4)
                pe.wait_ge(S.v_rows, 4 * p + 4)
                for e in range(2):
                    d = slice(e * HD, (e + 1) * HD)
                    keys = ps[:, 0:3, :].rearrange("p b c -> p (b c)")
                    pe.wait_ge(S.c_rows, 32 * p + 16 * (e + 1))
                    for t in range(KO):
                        if t or e:
                            pe.wait_ge(S.smax, 16 * p + 8 * e + t)
                        qs_ = slice(META + t * P, META + (t + 1) * P)
                        parts = [(512 - META, 0, META), (512, META, min(t + 1, 4) * P)]
                        if t >= 4:
                            parts.append((1024, META + 512, (t - 3) * P))
                        for c0, k0, n_ in parts:
                            o = keys[:, c0:c0 + n_]
                            pe.matmul(o, kqr[d, 2, qs_], kqr[d, 0, k0:k0 + n_], start=True, stop=False,
                                      skip_group_check=True)
                            pe.matmul(o, ones_r[0:2, :], crow[0:2, k0:k0 + n_], start=False, stop=True,
                                      skip_group_check=True)
                        mm = pe.matmul(keys[:, 512 + t * P:512 + (t + 1) * P], identb[:, :], causal[:, P:],
                                       start=False, stop=True, skip_group_check=True)
                        mm.then_inc(S.smax_done, 1)
                    for a in range(2):
                        pe.wait_ge(S.smax, 16 * p + 8 * e + 4 * a + 4)
                        if a:
                            pe.wait_ge(S.m_row, 4 * p + 2 * e + 1)
                        for t in range(4):
                            i = 4 * a + t
                            mm = pe.matmul(ps[0:1, 7, t * P:(t + 1) * P], mcol[:, i:i + 1], ident[:, :],
                                           start=True, stop=True)
                        mm.then_inc(S.m_row_done, 1)
                    pe.wait_ge(S.m_row, 4 * p + 2 * e + 2)

                    def scores(w):
                        qb_, kt = UNITS[w]
                        k0 = TILE_AT[kt]
                        q0 = max(qb_ * 512, (kt - 1) * P)
                        n_q = qb_ * 512 + 512 - q0
                        if w >= 3:
                            pe.wait_ge(S.p_exp, 28 * p + 14 * e + w - 2)
                        elif e:
                            pe.wait_ge(S.p_exp, 28 * p + 14)
                        o = ps[:, 3 + w % 3, 0:n_q]
                        ks, qs_ = slice(k0, k0 + P), slice(META + q0, META + q0 + n_q)
                        pe.matmul(o, kqr[d, 0, ks], kqr[d, 2, qs_], start=True, stop=False, skip_group_check=True)
                        pe.matmul(o, kqr[d, 1, ks], kqr[d, 2, qs_], start=False, stop=False, skip_group_check=True)
                        pe.matmul(o, kqr[d, 0, ks], kqr[d, 3, qs_], start=False, stop=False, skip_group_check=True)
                        mm = pe.matmul(o, ones_r[0:1, :], grow[0:1, q0:q0 + n_q], start=False, stop=True,
                                       skip_group_check=True)
                        if kt and (kt - 1) * P >= qb_ * 512:
                            mm = pe.matmul(ps[:, 3 + w % 3, 0:P], identb[:, :], causal[:, 0:P], start=False,
                                           stop=True, skip_group_check=True)
                        mm.then_inc(S.st_done, 1)

                    def weighted(w):
                        qb_, kt = UNITS[w]
                        n_k = TILE_TOK[kt]
                        q0 = max(qb_ * 512, (kt - 1) * P) - qb_ * 512
                        pe.wait_ge(S.p_exp, 28 * p + 14 * e + w + 1)
                        if kt == 0 and (qb_ or e):
                            pe.wait_ge(S.o_norm, 4 * p + 2 * e + qb_)
                        pe.matmul(ps[:, 6, q0:512], vflat[0:n_k, kt, e * P:(e + 1) * P], pt[w % 3][0:n_k, 0:512 - q0],
                                  start=(kt == 0), stop=(kt == 4 * qb_ + 4), skip_group_check=True)\
                            .then_inc(S.pv_done, 1)

                    scores(0)
                    scores(1)
                    for w in range(len(UNITS)):
                        if w + 2 < len(UNITS):
                            scores(w + 2)
                        weighted(w)

            pe.wait_ge(S.bpair_free, KO + 1)
            pe.wait_ge(S.x_lo, 4 * KO)

            def back(m):
                pe.wait_ge(S.fin_sum, m + 1)
                if m >= 2:
                    pe.wait_ge(S.fin_evac, m - 1)
                for t in range(KO):
                    mm = pe.transpose(ps[:, 4 + 2 * (m % 2) + t // 4, (t % 4) * P:(t % 4 + 1) * P],
                                      fin[m % 2][:, t * P:(t + 1) * P], ident[:, :])
                mm.then_inc(S.fin_tr, 1)

            for m in range(KO):
                n = N_BO + m
                pe.wait_ge(S.w_lo, n + 2)
                if m >= 2:
                    pe.wait_ge(S.fin_sum, m - 1)
                products(ps[:, 2 * (m % 2):2 * (m % 2) + 2, :], n % 2, P, 2, 512).then_inc(S.proj_done, 1)
                if m:
                    back(m - 1)
            back(KO - 1)


def kernel(**inputs):
    import concourse.bacc as bacc
    from concourse.bass_utils import run_bass_kernel_spmd

    a = {k: np.asarray(v) for k, v in inputs.items()}
    rows = np.concatenate(
        [a["a_shift_mu"][0][:4 * D].reshape(-1, P)]
        + [a[n][0].reshape(-1, P) for n in ("a_decay_bias", "a_iclr_bias", "a_k_k", "a_k_a", "a_r_k",
                                            "a_gn_w", "a_gn_b")]
        + [a["a_shift_mu"][0][4 * D:].reshape(1, P), a["a_norm"][0].reshape(-1, P),
           a["kv_norm"].reshape(-1, P), a["b_norm"][0].reshape(-1, P),
           np.tile(a["k_norm"], 2)[None], np.tile(a["b_q_norm"][0], 2)[None]], axis=0)
    i = np.arange(P)
    same = i[:, None] // CH == i[None, :] // CH
    masks = np.concatenate([same & (i[:, None] < i[None, :]), same & (i[:, None] <= i[None, :])],
                           axis=1).astype(np.float32)
    lev = []
    for b in (1, 2, 4, 8, 16, 32):
        t, s = i[:, None] // b, i[None, :] // b
        lev.append((t // 2 == s // 2) & (t == s + 1))
    levels = np.concatenate(lev, axis=1).astype(np.float32)
    ident = np.eye(P, dtype=np.float32)
    causal = np.concatenate([np.where(i[:, None] > i[None, :], MASKED, 0.0),
                             np.where(i[:, None] < i[None, :], MASKED, 0.0)], axis=1).astype(np.float32)
    arrays = {
        "x": a["x"][0], "meta": a["meta_tokens"], "rows": rows, "w_in": a["a_w_in"][0],
        "up": np.concatenate([a["a_decay_up"][0], a["a_iclr_up"][0]], axis=0), "w_out": a["a_w_out"][0],
        "kv_w": a["kv_w"], "f_bias": a["kv_f_bias"][:, None], "b_w_in": a["b_w_in"][0],
        "b_w_out": a["b_w_out"][0], "ident_d": ident, "masks_d": masks, "levels_d": levels,
        "causal_d": causal,
    }
    nc = bacc.Bacc("TRN2", target_bir_lowering=False, num_devices=1)
    feeds, aps = {}, {}
    for name, v in arrays.items():
        v = np.ascontiguousarray(v)
        feeds[f"in_{name}"] = v
        aps[name] = nc.dram_tensor(f"in_{name}", v.shape, mybir.dt.from_np(v.dtype), kind="ExternalInput").ap()
    aps["out"] = nc.dram_tensor("out_0", (SEQ, D), F32, kind="ExternalOutput").ap()
    build(nc, **aps)
    r = run_bass_kernel_spmd(nc, [feeds], core_ids=[0])
    return r.results[0]["out_0"].reshape(1, SEQ, D)
```

```python
from contextlib import ExitStack

import numpy as np

import concourse.bass as bass
from concourse import mybir

F32 = mybir.dt.float32
F32R = mybir.dt.float32r
BF16 = mybir.dt.bfloat16
ALU = mybir.AluOpType
ACT = mybir.ActivationFunctionType
AX = mybir.AxisListType

P = 128
D = 1024
SEQ = 1024
META = 16
T = SEQ + META
HD = 64
H = D // HD
KO = D // P
SEG = 348
TP = 3 * SEG
CH = 64
NT = 9
OFF = NT * P - T
TW = OFF + TP
LORA = 64
A_COLS = 4 * D + 2 * LORA
RMS_EPS = 1e-6
GN_EPS = 64e-5
KK_FLOOR = 1e-12
C_DECAY = float(np.exp(-0.5)) / 2
LN_SCALE = 2.0 ** 20
MASKED = -1e30
SCALE = HD ** -0.5

(Q_MUR, Q_MUK, Q_MUV, Q_MUZ, Q_DB, Q_IB, Q_KK, Q_KA, Q_RK, Q_GW, Q_GB,
 Q_NR, Q_NK, Q_NV, Q_NZ, Q_HDB, Q_HIB, Q_NKA) = range(18)
NQ = 18
ROW_LORA, ROW_AN, ROW_KVN, ROW_BN, ROW_KN, ROW_QN, NROWS = 88, 89, 97, 105, 113, 114, 115
C_LORA = NQ * KO
C_AN, C_KVN, C_BN, C_KN, C_QN, C_NLORA = (C_LORA + 1, C_LORA + 9, C_LORA + 17, C_LORA + 25,
                                          C_LORA + 26, C_LORA + 27)
NCOLS = C_LORA + 28

class Signals:

    def __init__(self, sem):
        self.x_loaded0 = sem("x_loaded0")
        self.x_loaded1 = sem("x_loaded1")
        self.rows_loaded = sem("rows_loaded")
        self.w_asked = sem("w_asked")
        self.consts_loaded = sem("consts_loaded")
        self.up_loaded = sem("up_loaded")
        self.w_loaded0 = sem("w_loaded0")
        self.w_loaded1 = sem("w_loaded1")
        self.w_scaled = sem("w_scaled")
        self.w_hi = sem("w_hi")
        self.w_lo = sem("w_lo")
        self.proj_done = sem("proj_done")
        self.param_tr = sem("param_tr")
        self.param_copied = sem("param_copied")
        self.param_derived = sem("param_derived")
        self.pads_zero = sem("pads_zero")
        self.setup_dve = sem("setup_dve")
        self.setup_pool = sem("setup_pool")
        self.x_tr = sem("x_tr")
        self.x_evac = sem("x_evac")
        self.xt_stored = sem("xt_stored")
        self.h_sq = sem("h_sq")
        self.h_sumsq = sem("h_sumsq")
        self.h_ln = sem("h_ln")
        self.h_rstd = sem("h_rstd")
        self.xn_mul = sem("xn_mul")
        self.x_hi = sem("x_hi")
        self.x_lo = sem("x_lo")
        self.mu_done = sem("mu_done")
        self.shifted = sem("shifted")
        self.lora_tanh = sem("lora_tanh")
        self.pair_free = sem("pair_free")
        self.pair_params = sem("pair_params")
        self.up_copied = sem("up_copied")
        self.dec_done = sem("dec_done")
        self.icl_done = sem("icl_done")
        self.dec_tanh = sem("dec_tanh")
        self.icl_tanh = sem("icl_tanh")
        self.logw = sem("logw")
        self.cumlog = sem("cumlog")
        self.iclr = sem("iclr")
        self.cum_before = sem("cum_before")
        self.exp_in = sem("exp_in")
        self.exp_neg = sem("exp_neg")
        self.exp_before = sem("exp_before")
        self.chunk_end = sem("chunk_end")
        self.kk_raw = sem("kk_raw")
        self.kk_sq = sem("kk_sq")
        self.kk_sumsq = sem("kk_sumsq")
        self.kk_guard = sem("kk_guard")
        self.kk_ln = sem("kk_ln")
        self.kk_rn = sem("kk_rn")
        self.kk_norm = sem("kk_norm")
        self.a_tilde = sem("a_tilde")
        self.r_tilde = sem("r_tilde")
        self.k_mix = sem("k_mix")
        self.k_new = sem("k_new")
        self.k_tilde = sem("k_tilde")
        self.kk_a = sem("kk_a")
        self.b_tilde = sem("b_tilde")
        self.bonus_prod = sem("bonus_prod")
        self.bonus_sum = sem("bonus_sum")
        self.bonus = sem("bonus")
        self.z_tanh = sem("z_tanh")
        self.z_gate = sem("z_gate")
        self.state_zero = sem("state_zero")
        self.tr_done = sem("tr_done")
        self.rows_ready = sem("rows_ready")
        self.a_done = sem("a_done")
        self.a_masked = sem("a_masked")
        self.q_done = sem("q_done")
        self.q_copied = sem("q_copied")
        self.p_done = sem("p_done")
        self.p_masked = sem("p_masked")
        self.x_done = sem("x_done")
        self.x_copied = sem("x_copied")
        self.wu_done = sem("wu_done")
        self.wu_copied = sem("wu_copied")
        self.u_done = sem("u_done")
        self.u_ready = sem("u_ready")
        self.s_done = sem("s_done")
        self.s_ready = sem("s_ready")
        self.s_scaled = sem("s_scaled")
        self.y_done = sem("y_done")
        self.y_copied = sem("y_copied")
        self.gn_mean = sem("gn_mean")
        self.gn_centred = sem("gn_centred")
        self.gn_sq = sem("gn_sq")
        self.gn_var = sem("gn_var")
        self.gn_ln = sem("gn_ln")
        self.gn_rstd = sem("gn_rstd")
        self.gn_scaled = sem("gn_scaled")
        self.gn_affine = sem("gn_affine")
        self.gn_bonus = sem("gn_bonus")
        self.out_ready = sem("out_ready")
        self.out_stored = sem("out_stored")
        self.o_loaded0 = sem("o_loaded0")
        self.o_loaded1 = sem("o_loaded1")
        self.xt_loaded = sem("xt_loaded")
        self.res_added = sem("res_added")
        self.f_logit = sem("f_logit")
        self.f_abs = sem("f_abs")
        self.f_exp = sem("f_exp")
        self.f_ln = sem("f_ln")
        self.f_min = sem("f_min")
        self.f_log = sem("f_log")
        self.f_cum = sem("f_cum")
        self.c_scaled = sem("c_scaled")
        self.c_hi = sem("c_hi")
        self.c_lo = sem("c_lo")
        self.c_stored = sem("c_stored")
        self.h_stored = sem("h_stored")
        self.setup_b = sem("setup_b")
        self.setup_bp = sem("setup_bp")
        self.b_done = sem("b_done")
        self.b_evac = sem("b_evac")
        self.hn_sq = sem("hn_sq")
        self.hn_ln = sem("hn_ln")
        self.hn_rstd = sem("hn_rstd")
        self.hn_full = sem("hn_full")
        self.st_hi = sem("st_hi")
        self.stacked = sem("stacked")
        self.c_rows0 = sem("c_rows0")
        self.c_rows1 = sem("c_rows1")
        self.bz_tanh = sem("bz_tanh")
        self.bz_gate = sem("bz_gate")
        self.smax_done = sem("smax_done")
        self.smax = sem("smax")
        self.mcol_ready = sem("mcol_ready")
        self.m_row_done = sem("m_row_done")
        self.m_row = sem("m_row")
        self.st_done = sem("st_done")
        self.p_exp = sem("p_exp")
        self.pv_done = sem("pv_done")
        self.d_ln = sem("d_ln")
        self.d_recip = sem("d_recip")
        self.o_norm = sem("o_norm")
        self.o_gated = sem("o_gated")
        self.ob_stored = sem("ob_stored")
        self.ob_free = sem("ob_free")
        self.h_loaded0 = sem("h_loaded0")
        self.h_loaded1 = sem("h_loaded1")
        self.fin_sum = sem("fin_sum")
        self.fin_tr = sem("fin_tr")
        self.fin_evac = sem("fin_evac")
        self.fin_stored0 = sem("fin_stored0")
        self.fin_stored1 = sem("fin_stored1")


def build(nc, x, meta, rows, w_in, up, w_out, kv_w, f_bias, b_w_in, b_w_out, ident_d, masks_d, levels_d,
          causal_d, out):
    ctx = ExitStack()
    with ctx:
        def sb(name, shape, dt=F32):
            return ctx.enter_context(nc.sbuf_tensor(name, shape, dt))

        S = Signals(lambda name: ctx.enter_context(nc.semaphore(name)))

        X_LOADED, W_LOADED = (S.x_loaded0, S.x_loaded1), (S.w_loaded0, S.w_loaded1)
        O_LOADED, FIN_STORED = (S.o_loaded0, S.o_loaded1), (S.fin_stored0, S.fin_stored1)
        H_LOADED, C_ROWS = (S.h_loaded0, S.h_loaded1), (S.c_rows0, S.c_rows1)

        xt_scr = nc.dram_tensor("xt_scr", (P, KO * TP), F32, kind="Internal").ap()
        oa_scr = nc.dram_tensor("oa_scr", (KO, P, TP), F32, kind="Internal").ap()
        ob_scr = nc.dram_tensor("ob_scr", (KO, P, SEQ), F32, kind="Internal").ap()
        c_scr = nc.dram_tensor("c_scr", (H, 2, TP), F32, kind="Internal").ap()

        ident = sb("ident", [P, P])
        identb = sb("identb", [P, P], BF16)
        head_ones = sb("head_ones", [P, P])
        all_ones = sb("all_ones", [P, P])
        ones_r = sb("ones_r", [P, P], F32R)
        masks = sb("masks", [P, 2 * P])
        levels = sb("levels", [P, 6 * P])
        causal = sb("causal", [P, 2 * P], BF16)
        params = sb("params", [P, NCOLS])
        pp = sb("pp", [P, NQ])
        cst = sb("cst", [P, 4])
        fb_in = sb("fb_in", [P, 1])
        EPS_RMS, EPS_GN, LN_BACK = (cst[:, i:i + 1] for i in range(3))

        xh = sb("xh", [P, KO, TP], F32R)
        xl = sb("xl", [P, KO, TP], F32R)
        wr = sb("wr", [P, 2, KO, P])
        wh = sb("wh", [P, 2, KO, P], F32R)
        wl = sb("wl", [P, 2, KO, P], F32R)
        ARENA = 21800
        with nc.sbuf_tensor("arena", [P, ARENA], F32) as arena:
            pass
        ka = [sb(f"ka{e}", [P, TP], F32R) for e in range(2)]
        qa = [sb(f"qa{e}", [P, TP], F32R) for e in range(2)]
        kb2 = [sb(f"kb2{e}", [P, TP], F32R) for e in range(2)]
        qb2 = [sb(f"qb2{e}", [P, TP], F32R) for e in range(2)]
        qc2 = [sb(f"qc2{e}", [P, TP], F32R) for e in range(2)]
        EXTRA = slice(HD, HD + 3)
        ARENA_B = 13000
        arena_b = sb("arena_b", [P, ARENA_B])
        chl = sb("chl", [P, 2, TP], F32R)
        ps = ctx.enter_context(nc.psum_tensor("ps", [P, 8, 512], F32))

        at = [0]

        def carve(n):
            at[0] += n
            assert at[0] <= ARENA, at[0]
            return arena[:, at[0] - n:at[0]]

        def carve_b(n):
            at[0] += n
            assert at[0] <= ARENA_B, at[0]
            return arena_b[:, at[0] - n:at[0]]

        h_t = carve(KO * TP).rearrange("p (k t) -> p k t", k=KO)
        sq2 = [carve(TP), carve(TP)]
        rstd = carve(TP)
        xrow = [carve(D), carve(D)]
        prow = carve(P)
        causal_f = carve(2 * P)
        at[0] = 0
        reset = carve(TP)
        ar = carve(2 * TW).rearrange("p (a t) -> p a t", a=2)
        b_t, k_t, v_t = carve(TW), carve(TW), carve(TW)
        zz, bon, y_t = (carve(TP) for _ in range(3))
        upall, lo, upf = carve(D), carve(TP), carve(P)
        st, pc = carve(P), carve(2 * NT)
        mut = carve(TP + 1)
        shared = at[0] - TP
        sq, mix = carve(TP), carve(TP)
        lw, cum, aa, kr, kk, rr = (carve(TP) for _ in range(6))
        e_in = y_t
        at[0] = shared
        rows_sb = [carve(4 * P).rearrange("p (a t) -> p a t", a=4) for _ in range(4)]
        amat = [[carve(4 * P) for _ in range(2)] for _ in range(4)]
        xs = [carve(4 * P).rearrange("p (e a t) -> p e a t", e=2, a=2) for _ in range(2)]
        pm = [carve(2 * P).rearrange("p (e t) -> p e t", e=2) for _ in range(2)]
        wu = [carve(2 * P).rearrange("p (a t) -> p a t", a=2) for _ in range(4)]
        qs = [carve(P) for _ in range(2)]
        us, sp = carve(P), carve(P)
        at[0] = KO * TP
        osq = [carve(TP), carve(TP)]
        at[0] = 0
        kb, qb, zb, vb, bsq, brs, zg = (carve_b(TP) for _ in range(7))
        vflat = [carve_b(NT * P).rearrange("p (t x) -> p t x", t=NT) for _ in range(2)]
        pt = [carve_b(512) for _ in range(3)]
        dln = carve_b(512)
        ob = carve_b(SEQ)
        mcol = carve_b(KO)
        mpart = carve_b(3 * KO)
        at[0] = 0
        fin = [carve_b(SEQ), carve_b(SEQ)]
        fo = [carve_b(SEQ).rearrange("p (t c) -> p t c", t=KO) for _ in range(2)]
        obq = [carve_b(SEQ), carve_b(SEQ)]
        hres = [carve_b(SEQ), carve_b(SEQ)]

        G = [ps[:, 0:3, 0:SEG], ps[:, 3:6, 0:SEG]]

        def seg3(a):
            return a.rearrange("p (c t) -> p c t", c=3)

        def param(c, n=1):
            return params[:, c:c + n]

        def q(i):
            return pp[:, i:i + 1]

        def f32(a):
            return a.bitcast(F32)

        TILE_TOK = [META] + [P] * KO
        TILE_AT = [0] + [META + P * i for i in range(KO)]
        N_A = 1
        N_AO = N_A + 4 * KO
        N_F = N_AO + KO
        N_B = N_F + 1
        N_BO = N_B + 4 * KO
        A_ORDER = [Q_MUK, Q_MUV, Q_MUR, Q_MUZ]
        UNITS = [(qb_, kt) for qb_ in range(2) for kt in range(4 * qb_ + 5)]
        NU = len(UNITS)

        def unit(w):
            qb_, kt = UNITS[w]
            q0 = max(qb_ * 512, kt * P - META)
            n_q = qb_ * 512 + 512 - q0
            off = META + q0 - kt * P
            return min(P, T - kt * P), q0, n_q, off, max(0, min(P - off, n_q))

        KSEG = [(t, i, 512 * i, min(512 * i + 512, META + (t + 1) * P)) for t in range(KO)
                for i in range(-(-(META + (t + 1) * P) // 512))]
        NS = len(KSEG)
        L_VROW1, L_K, L_SK, L_Q, L_SQ, L_V, L_VROW0, L_Z = 0, 2, 5, 8, 11, 14, 17, 19
        NCH = 22
        B_G, B_SM, B_ST, B_PV = (0, 1), (2, 3), (4, 5), (6, 7)

        def chunk(p, local):
            return NCH * p + NCH - 2 + local

        def order(e, more):
            at_ = [[] for _ in range(NU)]
            if more and e == 0:
                for i in range(3):
                    at_[i] += [("proj", 0, i)]
                    at_[4 + i] += [("proj", 1, i)]
                at_[3] += [("sumsq", 0, i) for i in range(3)]
                at_[8] += [("sumsq", 1, i) for i in range(3)]
            if more and e == 1:
                for i in range(3):
                    at_[i] += [("proj", 2, i)]
                    at_[5 + i] += [("proj", 3, i)]
                at_[4] += [("vrow", 0, i) for i in range(2)]
            if e == 0:
                at_[0] = [("vrow", 1, 0), ("vrow", 1, 1)] + at_[0]
                at_[10] += [("gate",)]
            if e == 0 or more:
                for i in range(NS):
                    at_[2 + i * 9 // NS] += [("smax", 1 - e, i)]
                at_[12] += [("maxrow", 1 - e)]
            steps = [("scores", e, 0), ("scores", e, 1)]
            if e == 0 or more:
                steps = [("stack", 1 - e)] + steps
            for w in range(NU):
                steps += at_[w] + [("weighted", e, w)]
                if w + 2 < NU:
                    steps += [("scores", e, w + 2)]
            return steps

        def first_round():
            return ([("proj", 0, i) for i in range(3)] + [("sumsq", 0, i) for i in range(3)]
                    + [("proj", 1, i) for i in range(3)] + [("sumsq", 1, i) for i in range(3)]
                    + [("stack", 0)] + [("proj", 2, i) for i in range(3)] + [("vrow", 0, i) for i in range(2)]
                    + [("smax", 0, i) for i in range(5)] + [("proj", 3, i) for i in range(3)]
                    + [("smax", 0, i) for i in range(5, NS)] + [("maxrow", 0)])


        GROUPS = [[0]] + [[u, u + 1] for u in range(1, NT, 2)]
        NG = len(GROUPS)
        LEVELS = [4] + [6] * (NG - 1)
        STEPS = LEVELS[0] + 12 * (NG - 1)
        B_US, B_Y, B_P, B_X, B_M = 0, 1, (2, 3), (4, 5), (6, 7)

        def step(g, l, j):
            return l if g == 0 else LEVELS[0] + 12 * (g - 1) + 2 * l + j

        def ring(g, j):
            return 2 * (g % 2) + j

        def chain_slots(g):
            return [(j, i) for j in range(len(GROUPS[g])) for i in range(5)]

        block = ctx.enter_context(nc.Block())

        @block.sync
        def _(sp_):
            sync = sp_
            for dst, src in ((ident[:, :], ident_d), (masks[:, :], masks_d), (levels[:, :], levels_d),
                             (causal_f, causal_d), (fb_in[0:H, :], f_bias)):
                sync.dma_start(dst, src).then_inc(S.consts_loaded, 16)
            sync.dma_start(prow[0:NROWS, :], rows).then_inc(S.rows_loaded, 16)
            sync.dma_start(xrow[0][0:META, :], meta).then_inc(X_LOADED[0], 16)
            for t in range(1, NT):
                if t >= 2:
                    sync.wait_ge(S.x_tr, t - 1)
                sync.dma_start(xrow[t % 2][:, :], x[(t - 1) * P:t * P, :]).then_inc(X_LOADED[t % 2], 16)

            def load_w(n, src, slot, wait):
                if wait is not None:
                    sync.wait_ge(S.w_lo, wait)
                    if not isinstance(wait, int):
                        sync.sem_inc(S.w_asked, 1)
                sync.dma_start(wr[:, slot, :, 0:src.shape[2]], src).then_inc(W_LOADED[slot], 16)

            wi = w_in.rearrange("(k p) n -> p k n", p=P)
            kvw = kv_w.rearrange("(k p) n -> p k n", p=P)
            bw = b_w_in.rearrange("(k p) n -> p k n", p=P)
            load_w(0, wi[:, :, 4 * D:4 * D + P], 0, None)
            sync.wait_ge(S.xt_stored, 16)
            sync.wait_ge(S.x_lo, KO)
            sync.dma_start(upall, up).then_inc(S.up_loaded, 16)
            with sync.Fori(0, KO) as p:
                cols = [sync.snap(p * P + base) for base in (D, 2 * D, 0, 3 * D)]
                for j, col in enumerate(cols):
                    load_w(None, wi[:, :, bass.ds(col, P)], (N_A + j) % 2, 4 * p + N_A + j)
            wo = w_out.rearrange("(k p) n -> p k n", p=P)
            for m in range(KO):
                if m == 0:
                    sync.wait_ge(S.pair_free, KO + 1)
                    sync.dma_start(h_t.rearrange("p k t -> p (k t)"), xt_scr).then_inc(S.xt_loaded, 16)
                    for k in range(KO):
                        if k >= 2:
                            sync.wait_ge(S.x_lo, KO + k - 1)
                        sync.dma_start(osq[k % 2], oa_scr[k]).then_inc(O_LOADED[k % 2], 16)
                        if k == 0:
                            load_w(N_AO, wo[:, :, 0:P], N_AO % 2, N_AO)
                        if k == 1:
                            load_w(N_AO + 1, wo[:, :, P:2 * P], (N_AO + 1) % 2, N_AO + 1)
                elif m >= 2:
                    load_w(N_AO + m, wo[:, :, m * P:(m + 1) * P], (N_AO + m) % 2, N_AO + m)
            load_w(N_F, kvw[:, :, 2 * D:2 * D + H], N_F % 2, N_F)
            with sync.Fori(0, KO) as p:
                cols = [sync.snap(p * P + base) for base in (0, D)]
                for j, (w, col) in enumerate(((kvw, cols[0]), (bw, cols[0]), (kvw, cols[1]), (bw, cols[1]))):
                    load_w(None, w[:, :, bass.ds(col, P)], (N_B + j) % 2, 4 * p + N_B + j)
            bwo = b_w_out.rearrange("(k p) n -> p k n", p=P)
            for k in range(2):
                load_w(N_BO + k, bwo[:, :, k * P:(k + 1) * P], (N_BO + k) % 2, N_BO + k)
            sync.wait_ge(S.ob_free, KO + 1)
            for k in range(KO):
                if k >= 2:
                    sync.wait_ge(S.x_lo, 3 * KO + k - 1)
                sync.dma_start(obq[k % 2], ob_scr[k]).then_inc(O_LOADED[k % 2], 16)
            out_v = out.rearrange("(t p) c -> p t c", p=P)

            def load_h(m):
                if m >= 2:
                    sync.wait_ge(S.fin_sum, m - 1)
                sync.dma_start(hres[m % 2], xt_scr[:, m * TP + META:m * TP + T]).then_inc(H_LOADED[m % 2], 16)

            load_h(0)
            load_h(1)
            for m in range(KO):
                if m + 2 < KO:
                    n = N_BO + m + 2
                    load_w(n, bwo[:, :, (m + 2) * P:(m + 3) * P], n % 2, n)
                    load_h(m + 2)
                sync.wait_ge(S.fin_evac, m + 1)
                sync.dma_start(out_v[:, :, m * P:(m + 1) * P], fo[m % 2]).then_inc(FIN_STORED[m % 2], 16)
            for i in range(2):
                sync.wait_ge(FIN_STORED[i], 16 * KO // 2)
            sync.wait_ge(S.c_stored, 16)

        @block.gpsimd
        def _(pool):
            pool.memset(f32(ones_r[:, :]), 1.0).then_inc(S.setup_pool, 1)
            pool.memset(head_ones[:, :], 0.0).then_inc(S.setup_pool, 1)
            pool.wait_ge(S.setup_pool, 2)
            for e in range(2):
                b = slice(e * HD, (e + 1) * HD)
                pool.memset(head_ones[b, b], 1.0).then_inc(S.setup_pool, 1)
            pool.wait_ge(S.setup_pool, 4)
            pool.wait_ge(S.x_evac, NT)
            pool.wait_ge(S.pads_zero, 1)
            pool.dma_start(xt_scr, h_t.rearrange("p k t -> p (k t)")).then_inc(S.xt_stored, 16)

            def scale_w(slot, gain, loaded, width=P):
                pool.wait_ge(W_LOADED[slot], loaded)
                pool.tensor_tensor(wr[:, slot, :, 0:width], wr[:, slot, :, 0:width],
                                   param(gain, KO).unsqueeze(2).to_broadcast([P, KO, width]),
                                   ALU.mult).then_inc(S.w_scaled, 1)

            pool.wait_ge(S.param_derived, 4)
            scale_w(0, C_AN, 16)
            pool.wait_ge(S.xt_stored, 16)
            pool.wait_ge(S.x_lo, KO)
            pool.wait_ge(S.shifted, 1)
            pool.sem_inc(S.pair_free, 1)
            with pool.Fori(0, KO) as p:
                v = p + 1
                for j in range(4):
                    scale_w((N_A + j) % 2, C_AN, 32 * p + 16 * ((N_A + j) // 2 + 1))
                pool.wait_ge(S.cumlog, v)
                pool.tensor_tensor(lw, cum, lw, ALU.subtract).then_inc(S.cum_before, 1)
                pool.wait_ge(S.k_mix, v)
                pool.wait_ge(S.shifted, 4 * p + 2)
                pool.wait_ge(S.kk_raw, v)
                pool.tensor_tensor(kr, kr, mix, ALU.mult).then_inc(S.k_new, 1)
                pool.wait_ge(S.exp_neg, v)
                pool.wait_ge(S.k_new, v)
                pool.tensor_tensor(k_t[:, OFF:], kr, cum, ALU.mult).then_inc(S.k_tilde, 1)
                pool.wait_ge(S.kk_norm, v)
                pool.wait_ge(S.kk_sumsq, v)
                pool.tensor_tensor(sq, kk, aa, ALU.mult).then_inc(S.kk_a, 1)
                pool.wait_ge(S.kk_a, v)
                pool.tensor_tensor(b_t[:, OFF:], sq, cum, ALU.mult).then_inc(S.b_tilde, 1)
                pool.wait_ge(S.out_ready, v)
                pool.dma_start(oa_scr[bass.ds(p, 1)].rearrange("a p t -> (a p) t"), y_t).then_inc(S.out_stored, 16)
                pool.wait_ge(S.out_stored, 16 * v)
                pool.sem_inc(S.pair_free, 1)
            scale_w(N_F % 2, C_KVN, 16 * (N_F // 2 + 1), H)
            pool.wait_ge(S.res_added, KO)
            pool.dma_start(xt_scr, h_t.rearrange("p k t -> p (k t)")).then_inc(S.h_stored, 16)
            pool.wait_ge(S.c_lo, 1)
            pool.dma_start(c_scr[:, 0, :], f32(chl[0:H, 0, :])).then_inc(S.c_stored, 16)
            pool.wait_ge(S.c_stored, 16)
            pool.dma_start(c_scr[:, 1, :], f32(chl[0:H, 1, :])).then_inc(S.c_stored, 16)
            pool.wait_ge(S.h_stored, 16)
            pool.wait_ge(S.x_lo, 3 * KO)
            for e in range(2):
                for a in (kb2[e], qb2[e], qc2[e]):
                    pool.memset(f32(a[EXTRA, :]), 1.0).then_inc(S.setup_bp, 1)
            pool.wait_ge(S.setup_bp, 6)
            for e in range(2):
                pool.memset(f32(qc2[e][HD:HD + 1, :]), 0.0).then_inc(S.setup_bp, 1)
            pool.wait_ge(S.setup_bp, 8)
            pool.wait_ge(S.c_stored, 32)
            pool.sem_inc(S.ob_free, 1)

            def scale_b(q_, j):
                scale_w((N_B + j) % 2, (C_KVN, C_BN)[j % 2], 32 * q_ + 16 * ((N_B + j) // 2 + 1))

            def store_ob(p, dst):
                pool.wait_ge(S.o_gated, p + 2)
                pool.dma_start(dst, ob).then_inc(S.ob_stored, 16)
                pool.wait_ge(S.ob_stored, 16 * p + 16)
                pool.sem_inc(S.ob_free, 1)

            for j in range(4):
                scale_b(0, j)
            scale_b(1, 0)
            with pool.Fori(0, KO - 2) as p:
                for j in range(1, 4):
                    scale_b(p + 1, j)
                scale_b(p + 2, 0)
                store_ob(p, ob_scr[bass.ds(p, 1)].rearrange("a p t -> (a p) t"))
            for j in range(1, 4):
                scale_b(KO - 1, j)
            store_ob(KO - 2, ob_scr[KO - 2])
            store_ob(KO - 1, ob_scr[KO - 1])

        @block.scalar
        def _(act):
            def split_hi(slot, loaded, scaled, hi_free, width=P):
                if scaled is None:
                    act.wait_ge(W_LOADED[slot], loaded)
                else:
                    act.wait_ge(S.w_scaled, scaled)
                if hi_free is not None:
                    act.wait_ge(S.proj_done, hi_free)
                act.activation(wh[:, slot, :, 0:width], wr[:, slot, :, 0:width], ACT.Copy).then_inc(S.w_hi, 1)

            def normalise(r):
                for k in range(KO):
                    if k >= 2:
                        act.wait_ge(S.h_sumsq, KO * r + k - 1)
                    if r:
                        act.wait_ge(S.res_added, k + 1)
                    else:
                        act.wait_ge(S.x_evac, NT)
                        act.wait_ge(S.pads_zero, 1)
                    act.activation(sq2[k % 2], h_t[:, k, :], ACT.Square).then_inc(S.h_sq, 1)
                act.wait_ge(S.h_sumsq, KO * (r + 1))
                act.wait_ge(S.setup_dve, 3)
                act.activation(seg3(rstd), G[0], ACT.Ln, scale=1.0 / D, bias=EPS_RMS).then_inc(S.h_ln, 1)
                act.wait_ge(S.h_ln, r + 1)
                act.activation(rstd, rstd, ACT.Exp, scale=-0.5).then_inc(S.h_rstd, 1)
                for k in range(KO):
                    act.wait_ge(S.xn_mul, KO * r + k + 1)
                    act.activation(xh[:, k, :], sq2[k % 2], ACT.Copy).then_inc(S.x_hi, 1)

            def shift_mu(parity, mu, done, free):
                act.wait_ge(S.proj_done, done)
                act.wait_ge(S.shifted, free)
                act.activation(seg3(mut[:, 1:]), G[parity], ACT.Copy, scale=mu).then_inc(S.mu_done, 1)

            normalise(0)
            split_hi(0, None, 1, None)
            act.wait_ge(S.proj_done, 1)
            act.activation(seg3(mut[:, 1:]), G[0], ACT.Copy, scale=param(C_LORA)).then_inc(S.mu_done, 1)
            act.wait_ge(S.shifted, 1)
            act.activation(lo[0:LORA, :], lo[0:LORA, :], ACT.Tanh).then_inc(S.lora_tanh, 1)
            with act.Fori(0, KO) as p:
                v = p + 1
                act.wait_ge(S.pair_free, v)
                act.wait_ge(S.pair_params, v)
                act.wait_ge(S.up_loaded, 16)
                act.activation(upf, upall[:, bass.ds(p * P, P)], ACT.Copy).then_inc(S.up_copied, 1)
                split_hi((N_A + 0) % 2, None, 4 * p + 2, None)
                split_hi((N_A + 1) % 2, None, 4 * p + 3, 4 * p + 1)
                act.wait_ge(S.dec_done, v)
                act.activation(seg3(lw), G[0], ACT.Tanh, scale=0.5, bias=q(Q_HDB)).then_inc(S.dec_tanh, 1)
                act.wait_ge(S.icl_done, v)
                act.activation(seg3(aa), G[1], ACT.Tanh, scale=0.5, bias=q(Q_HIB)).then_inc(S.icl_tanh, 1)
                shift_mu(0, q(Q_MUK), 4 * p + 2, 4 * p + 1)
                split_hi((N_A + 2) % 2, None, 4 * p + 4, 4 * p + 2)
                shift_mu(1, q(Q_MUV), 4 * p + 3, 4 * p + 2)
                split_hi((N_A + 3) % 2, None, 4 * p + 5, 4 * p + 3)
                act.activation(kk, kr, ACT.Copy, scale=q(Q_KK)).then_inc(S.kk_raw, 1)
                act.wait_ge(S.kk_raw, v)
                act.activation(sq, kk, ACT.Square).then_inc(S.kk_sq, 1)
                act.wait_ge(S.iclr, v)
                act.activation(mix, aa, ACT.Identity, scale=q(Q_KA), bias=q(Q_NKA)).then_inc(S.k_mix, 1)
                act.wait_ge(S.cumlog, v)
                act.activation(e_in, cum, ACT.Exp).then_inc(S.exp_in, 1)
                act.wait_ge(S.cum_before, v)
                act.activation(cum, cum, ACT.Exp, scale=-1.0).then_inc(S.exp_neg, 1)
                act.activation(lw, lw, ACT.Exp).then_inc(S.exp_before, 1)
                shift_mu(0, q(Q_MUR), 4 * p + 4, 4 * p + 3)
                shift_mu(0, q(Q_MUZ), 4 * p + 5, 4 * p + 4)
                act.wait_ge(S.kk_guard, v)
                act.activation(bon, bon, ACT.Ln, scale=LN_SCALE)\
                    .then_inc(S.kk_ln, 1)
                act.wait_ge(S.kk_ln, v)
                act.activation(bon, bon, ACT.Exp, scale=-0.5, bias=LN_BACK).then_inc(S.kk_rn, 1)
                act.wait_ge(S.shifted, 4 * p + 5)
                act.wait_ge(S.bonus_sum, v)
                act.activation(mix, zz, ACT.Tanh, scale=0.5).then_inc(S.z_tanh, 1)

                def chain_act(g, j, i):
                    u = GROUPS[g][j]
                    if i in (0, 2):
                        c = 2 * u + i // 2
                        if c == 0:
                            act.wait_ge(S.state_zero, v)
                        else:
                            act.wait_ge(S.s_ready, 36 * p + 2 * c)
                        act.activation(sp, st, ACT.Copy, scale=pc[:, c:c + 1]).then_inc(S.s_scaled, 1)
                    if i == 4:
                        act.wait_ge(S.y_done, 9 * p + u + 1)
                        lo_, n_ = (OFF, META) if u == 0 else (0, P)
                        act.activation(y_t[:, TILE_AT[u]:TILE_AT[u] + n_], ps[:, B_Y, lo_:P], ACT.Copy)\
                            .then_inc(S.y_copied, 1)

                def rows_act(g):
                    for j, u in enumerate(GROUPS[g]):
                        act.wait_ge(S.tr_done, 9 * p + u + 1)
                        if u == 0:
                            act.wait_ge(S.z_gate, v)
                            act.wait_ge(S.b_tilde, v)
                        if g >= 2:
                            act.wait_ge(S.y_done, 9 * p + GROUPS[g - 2][-1] + 1)
                        act.activation(rows_sb[ring(g, j)].rearrange("p a t -> p (a t)"), ps[:, B_M[j], :], ACT.Copy)\
                            .then_inc(S.rows_ready, 1)

                rows_act(0)
                for g, tiles in enumerate(GROUPS):
                    slots = chain_slots(g - 1) if g else []
                    for l in range(LEVELS[g]):
                        if 2 * l < len(slots):
                            chain_act(g - 1, *slots[2 * l])
                        for j, u in enumerate(tiles):
                            act.wait_ge(S.x_done, STEPS * p + step(g, l, j) + 1)
                            bank = ps[:, B_X[j], :].rearrange("p (e a t) -> p e a t", e=2, a=2)
                            if 0 < l < LEVELS[g] - 1:
                                act.activation(xs[j], bank, ACT.Copy).then_inc(S.x_copied, 1)
                            else:
                                act.activation(xs[j][:, :, 1, :], bank[:, :, 1, :], ACT.Copy).then_inc(S.x_copied, 1)
                        if 2 * l + 1 < len(slots):
                            chain_act(g - 1, *slots[2 * l + 1])
                        if l == 0:
                            for j, u in enumerate(tiles):
                                act.wait_ge(S.q_done, 9 * p + u + 1)
                                act.activation(qs[j], ps[:, B_M[j], 0:P], ACT.Copy).then_inc(S.q_copied, 1)
                    if g + 1 < NG:
                        rows_act(g + 1)
                for j, i in chain_slots(NG - 1):
                    chain_act(NG - 1, j, i)
                act.wait_ge(S.gn_centred, v)
                act.activation(sq, y_t, ACT.Square).then_inc(S.gn_sq, 1)
                act.wait_ge(S.gn_var, v)
                act.activation(seg3(sq), G[0], ACT.Ln, scale=1.0 / HD, bias=EPS_GN).then_inc(S.gn_ln, 1)
                act.wait_ge(S.gn_ln, v)
                act.activation(sq, sq, ACT.Exp, scale=-0.5).then_inc(S.gn_rstd, 1)

            def split_rows(r, width):
                for k in range(KO):
                    act.wait_ge(O_LOADED[k % 2], 16 * (KO // 2 * (r // 2) + k // 2 + 1))
                    act.activation(xh[:, k, 0:width], (osq if r == 1 else obq)[k % 2][:, 0:width], ACT.Copy)\
                        .then_inc(S.x_hi, 1)

            for n in (N_AO, N_AO + 1):
                split_hi(n % 2, 16 * (n // 2 + 1), None, n - 1)
                if n == N_AO:
                    split_rows(1, TP)
            for m in range(KO - 2):
                n = N_AO + m + 2
                split_hi(n % 2, 16 * (n // 2 + 1), None, n - 1)
            normalise(1)
            n = N_F
            split_hi(n % 2, None, N_AO + 1, n - 1, H)
            act.wait_ge(S.f_logit, 1)
            act.activation(brs[0:H, :], bsq[0:H, :], ACT.Abs).then_inc(S.f_abs, 1)
            act.wait_ge(S.f_abs, 1)
            act.activation(brs[0:H, :], brs[0:H, :], ACT.Exp, scale=-1.0).then_inc(S.f_exp, 1)
            act.wait_ge(S.f_exp, 1)
            act.activation(brs[0:H, :], brs[0:H, :], ACT.Ln, bias=1.0).then_inc(S.f_ln, 1)
            act.wait_ge(S.c_scaled, 1)
            act.activation(chl[0:H, 0, :], bsq[0:H, :], ACT.Copy).then_inc(S.c_hi, 1)
            act.wait_ge(S.c_lo, 1)
            act.wait_ge(S.setup_bp, 8)
            act.wait_ge(S.c_stored, 32)

            def split_b(p, j):
                act.wait_ge(S.w_scaled, 4 * p + N_AO + 6 + j)
                act.wait_ge(S.b_done, NCH * p + (15, 20, 25, 31)[j])
                act.activation(wh[:, (N_B + j) % 2, :, :], wr[:, (N_B + j) % 2, :, :], ACT.Copy).then_inc(S.w_hi, 1)

            def round_act(p, steps, c_next):
                first = isinstance(p, int) and p < 0
                for st_ in steps:
                    kind = st_[0]
                    if kind == "proj":
                        j, i = st_[1:]
                        n_ = chunk(p, (L_K, L_Q, L_V, L_Z)[j] + i)
                        if i == 0 and j < 3:
                            if first and j == 0:
                                split_hi((N_B + 1) % 2, None, N_AO + 3, N_B)
                            else:
                                split_b(p, j + 1)
                        act.wait_ge(S.b_done, n_ + 1)
                        if i == 0 and not first:
                            if j < 2:
                                act.wait_ge(S.stacked, 10 * p + 10)
                            elif j == 3:
                                act.wait_ge(S.bz_gate, p + 1)
                        act.activation((kb, qb, vb, zb)[j][:, i * SEG:(i + 1) * SEG], ps[:, B_G[(i + (L_K, L_Q, L_V, L_Z)[j]) % 2], 0:SEG],
                                       ACT.Copy).then_inc(S.b_evac, 1)
                        if i == 2 and j < 2:
                            act.wait_ge(S.b_evac, n_ + 1)
                            if j:
                                act.wait_ge(S.b_done, chunk(p, L_SK) + 3)
                            act.activation(bsq, (kb, qb)[j], ACT.Square).then_inc(S.hn_sq, 1)
                    elif kind == "sumsq":
                        j, i = st_[1:]
                        local = (L_SK, L_SQ)[j] + i
                        n_ = chunk(p, local)
                        act.wait_ge(S.b_done, n_ + 1)
                        if i == 0 and not (first and j == 0):
                            act.wait_ge(S.hn_full, 2 * p + 2 + j)
                        act.activation(brs[:, i * SEG:(i + 1) * SEG], ps[:, B_G[local % 2], 0:SEG], ACT.Ln,
                                       scale=1.0 / HD, bias=EPS_RMS).then_inc(S.b_evac, 1)
                        if i == 2:
                            act.wait_ge(S.b_evac, n_ + 1)
                            act.activation(brs, brs, ACT.Exp, scale=-0.5).then_inc(S.hn_rstd, 1)
                    elif kind == "stack":
                        e = st_[1]
                        q_ = p + 1 - e
                        d = slice(e * HD, (e + 1) * HD)
                        act.dma_start(f32(kb2[e][HD + 1:HD + 3, :]), c_next[e]).then_inc(C_ROWS[e], 16)
                        act.wait_ge(S.hn_full, 2 * q_ + 1)
                        act.activation(ka[e][d, :], kb[d, :], ACT.Copy).then_inc(S.st_hi, 1)
                        act.wait_ge(S.hn_full, 2 * q_ + 2)
                        act.activation(qa[e][d, :], qb[d, :], ACT.Copy).then_inc(S.st_hi, 1)
                    elif kind == "vrow":
                        e, i = st_[1:]
                        local = (L_VROW0, L_VROW1)[e] + i
                        act.wait_ge(S.b_done, chunk(p, local) + 1)
                        c = slice(e * HD, (e + 1) * HD)
                        bank = ps[:, B_G[local % 2], :]
                        if i == 0:
                            act.activation(vflat[e][:, 0:7, c], bank[:, 0:7 * HD].rearrange("p (t c) -> p t c", c=HD),
                                           ACT.Copy).then_inc(S.b_evac, 1)
                        else:
                            act.activation(vflat[e][:, 7, c], bank[:, 0:HD], ACT.Copy)
                            act.activation(vflat[e][0:META, 8, c], bank[0:META, HD:2 * HD], ACT.Copy)\
                                .then_inc(S.b_evac, 1)
                    elif kind == "gate":
                        act.wait_ge(S.o_gated, p + 1)
                        act.wait_ge(S.b_evac, chunk(p - 1, L_Z) + 3)
                        act.activation(zg, zb, ACT.Tanh, scale=0.5).then_inc(S.bz_tanh, 1)
                    elif kind == "maxrow":
                        e = st_[1]
                        q_ = p + 1 - e
                        for a in range(2):
                            act.wait_ge(S.m_row_done, 4 * q_ + 2 * e + a + 1)
                            act.activation(qb2[e][HD:HD + 1, META + a * 512:META + (a + 1) * 512], ps[0:1, B_SM[a], :],
                                           ACT.Copy, scale=-1.0).then_inc(S.m_row, 1)
                    elif kind == "scores":
                        e, w = st_[1:]
                        n_k, q0, n_q, _, _ = unit(w)
                        base = 2 * NU * p + NU * e + w
                        act.wait_ge(S.st_done, base + 1)
                        if w >= 3:
                            act.wait_ge(S.pv_done, base - 2)
                        act.activation(pt[w % 3][0:n_k, 0:n_q], ps[0:n_k, B_ST[w % 2], 0:n_q], ACT.Exp,
                                       scale=SCALE).then_inc(S.p_exp, 1)
                    elif kind == "weighted":
                        e, w = st_[1:]
                        qb_, kt = UNITS[w]
                        if kt == 4 * qb_ + 4:
                            b, o = slice(e * HD, (e + 1) * HD), slice((1 - e) * HD, (2 - e) * HD)
                            n_ = 4 * p + 2 * e + qb_
                            act.wait_ge(S.pv_done, 2 * NU * p + NU * e + w + 1)
                            act.wait_ge(S.o_norm, n_ + 2)
                            act.activation(dln[b, :], ps[o, B_PV[qb_], :], ACT.Ln).then_inc(S.d_ln, 1)
                            act.wait_ge(S.d_ln, n_ + 1)
                            act.activation(dln[b, :], dln[b, :], ACT.Exp, scale=-1.0).then_inc(S.d_recip, 1)

            def c_rows_of(head):
                return c_scr[bass.ds(head, 1)].rearrange("a b t -> (a b) t")

            split_hi((N_B + 0) % 2, None, N_AO + 2, N_B - 1)
            round_act(-1, first_round(), [c_scr[0], None])
            with act.Fori(0, KO - 1) as p:
                split_b(p, 0)
                rows_c = [c_rows_of(act.snap(2 * p + 2)), c_rows_of(act.snap(2 * p + 1))]
                round_act(p, order(0, True), rows_c)
                round_act(p, order(1, True), rows_c)
            round_act(KO - 1, order(0, False), [None, c_scr[2 * KO - 1]])
            round_act(KO - 1, order(1, False), None)
            for n in (N_BO, N_BO + 1):
                act.wait_ge(W_LOADED[n % 2], 16 * (n // 2 + 1))
                act.activation(wh[:, n % 2, :, :], wr[:, n % 2, :, :], ACT.Copy).then_inc(S.w_hi, 1)
                if n == N_BO:
                    split_rows(3, SEQ)
            for m in range(KO):
                n = N_BO + m + 2
                if m < KO - 2:
                    split_hi(n % 2, 16 * (n // 2 + 1), None, N_B + m + 1)
                act.wait_ge(S.fin_tr, m + 1)
                if m >= 2:
                    act.wait_ge(FIN_STORED[m % 2], 16 * (m // 2))
                act.activation(fo[m % 2].rearrange("p (b t) c -> p b (t c)", b=2), ps[:, 4 + 2 * (m % 2):6 + 2 * (m % 2), :],
                               ACT.Copy).then_inc(S.fin_evac, 1)

        @block.vector
        def _(dve):
            def split_lo(slot, n, width=P):
                dve.wait_ge(S.w_hi, n + 1)
                dve.tensor_tensor(wl[:, slot, :, 0:width], wr[:, slot, :, 0:width], f32(wh[:, slot, :, 0:width]),
                                  ALU.subtract).then_inc(S.w_lo, 1)

            def normalise(r):
                dve.wait_ge(S.h_rstd, r + 1)

                def lo(k):
                    dve.wait_ge(S.x_hi, 2 * KO * r + k + 1)
                    dve.tensor_tensor(xl[:, k, :], sq2[k % 2], f32(xh[:, k, :]), ALU.subtract).then_inc(S.x_lo, 1)
                for k in range(KO):
                    if k >= 2:
                        lo(k - 2)
                        dve.wait_ge(S.x_lo, 2 * KO * r + k - 1)
                    dve.tensor_tensor(sq2[k % 2], h_t[:, k, :], rstd, ALU.mult).then_inc(S.xn_mul, 1)
                lo(KO - 2)
                lo(KO - 1)

            def shift(dst, parity, keep, count, extra=None):
                dve.wait_ge(S.mu_done, count)
                dve.scalar_tensor_tensor(seg3(dst), G[parity], keep, seg3(mut[:, 0:TP]), ALU.mult, ALU.add)\
                    .then_inc(S.shifted, 1)

            for i, val in enumerate((RMS_EPS, GN_EPS, 0.5 * float(np.log(LN_SCALE)))):
                dve.memset(cst[:, i:i + 1], val).then_inc(S.setup_dve, 1)
            dve.memset(all_ones[:, :], 1.0).then_inc(S.setup_dve, 1)
            dve.wait_ge(S.consts_loaded, 80)
            dve.tensor_copy(causal[:, :], causal_f).then_inc(S.setup_dve, 1)
            dve.tensor_copy(identb[:, :], ident[:, :]).then_inc(S.setup_dve, 1)
            dve.memset(h_t[:, :, T:TP], 0.0).then_inc(S.pads_zero, 1)
            for t in range(NT):
                dve.wait_ge(S.x_tr, t + 1)
                g, n = 2 * (t % 2), TILE_TOK[t]
                dve.tensor_copy(h_t[:, :, TILE_AT[t]:TILE_AT[t] + n],
                                ps[:, g:g + 2, :].rearrange("p b (k t) -> p (b k) t", k=4)[:, :, 0:n])\
                    .then_inc(S.x_evac, 1)
            dve.wait_ge(S.param_tr, 1)
            dve.tensor_copy(params[:, 0:ROW_LORA], ps[:, 6, 0:ROW_LORA]).then_inc(S.param_copied, 1)
            dve.tensor_copy(params[:, C_LORA:C_LORA + NROWS - ROW_LORA], ps[:, 6, ROW_LORA:NROWS])\
                .then_inc(S.param_copied, 1)
            dve.wait_ge(S.param_copied, 2)
            dve.tensor_scalar(param(Q_NR * KO, 4 * KO), param(Q_MUR * KO, 4 * KO), -1.0, 1.0, ALU.mult, ALU.add)\
                .then_inc(S.param_derived, 1)
            dve.tensor_scalar(param(Q_HDB * KO, 2 * KO), param(Q_DB * KO, 2 * KO), 0.5, None, ALU.mult)\
                .then_inc(S.param_derived, 1)
            dve.tensor_scalar(param(Q_NKA * KO, KO), param(Q_KA * KO, KO), -1.0, 1.0, ALU.mult, ALU.add)\
                .then_inc(S.param_derived, 1)
            dve.tensor_scalar(param(C_NLORA), param(C_LORA), -1.0, 1.0, ALU.mult, ALU.add)\
                .then_inc(S.param_derived, 1)
            normalise(0)
            dve.wait_ge(S.xt_stored, 16)
            dve.wait_ge(S.x_lo, KO)
            dve.memset(reset, 1.0).then_inc(S.setup_dve, 1)
            dve.wait_ge(S.setup_dve, 7)
            dve.memset(reset[:, 0:1], 0.0).then_inc(S.setup_dve, 1)
            dve.memset(reset[:, META:TP:CH], 0.0).then_inc(S.setup_dve, 1)
            dve.memset(ar[:, :, 0:OFF], 0.0).then_inc(S.setup_dve, 1)
            for a in (b_t, k_t, v_t):
                dve.memset(a[:, 0:OFF], 0.0).then_inc(S.setup_dve, 1)
            dve.memset(mut[:, 0:1], 0.0).then_inc(S.setup_dve, 1)
            dve.memset(pc[:, 0:1], 1.0).then_inc(S.setup_dve, 1)
            dve.memset(f32(wl[:, 1, 0, 0:1]), 0.0).then_inc(S.w_lo, 1)
            dve.wait_ge(S.setup_dve, 15)
            split_lo(0, 0)
            dve.wait_ge(S.mu_done, 1)
            dve.scalar_tensor_tensor(seg3(lo), G[0], param(C_NLORA), seg3(mut[:, 0:TP]), ALU.mult, ALU.add)\
                .then_inc(S.shifted, 1)
            with dve.Fori(0, KO) as p:
                v = p + 1
                n = 4 * p + N_A
                dve.wait_ge(S.pair_free, v)
                dve.tensor_copy(pp[:, :].unsqueeze(2), param(0, NQ * KO).rearrange("p (q k) -> p q k", k=KO)[:, :, bass.ds(p, 1)])\
                    .then_inc(S.pair_params, 1)
                dve.memset(st, 0.0).then_inc(S.state_zero, 1)
                split_lo((N_A + 0) % 2, n)
                split_lo((N_A + 1) % 2, n + 1)
                dve.wait_ge(S.dec_tanh, v)
                dve.tensor_scalar(lw, lw, -C_DECAY, -C_DECAY, ALU.mult, ALU.add).then_inc(S.logw, 1)
                dve.wait_ge(S.icl_tanh, v)
                dve.tensor_scalar(aa, aa, 0.5, 0.5, ALU.mult, ALU.add).then_inc(S.iclr, 1)
                dve.wait_ge(S.logw, v)
                dve.tensor_tensor_scan(cum, reset, lw, 0.0, ALU.mult, ALU.add).then_inc(S.cumlog, 1)
                dve.wait_ge(S.pair_params, v)
                shift(kr, 0, q(Q_NK), 4 * p + 2)
                split_lo((N_A + 2) % 2, n + 2)
                shift(v_t[:, OFF:], 1, q(Q_NV), 4 * p + 3)
                split_lo((N_A + 3) % 2, n + 3)
                dve.wait_ge(S.exp_in, v)
                dve.tensor_copy(pc[:, 1:2 * NT], e_in[:, META - 1:T:CH]).then_inc(S.chunk_end, 1)
                shift(rr, 0, q(Q_NR), 4 * p + 4)
                dve.wait_ge(S.shifted, 4 * p + 4)
                dve.tensor_tensor(ar[:, 1, OFF:], rr, e_in, ALU.mult).then_inc(S.r_tilde, 1)
                dve.wait_ge(S.kk_sumsq, v)
                dve.tensor_scalar(seg3(bon), G[1], KK_FLOOR ** 2, None, ALU.max).then_inc(S.kk_guard, 1)
                dve.wait_ge(S.k_new, v)
                dve.wait_ge(S.k_mix, v)
                dve.scalar_tensor_tensor(mix, rr, q(Q_RK), kr, ALU.mult, ALU.mult).then_inc(S.bonus_prod, 1)
                shift(zz, 0, q(Q_NZ), 4 * p + 5)
                dve.wait_ge(S.kk_rn, v)
                dve.tensor_tensor(kk, kk, bon, ALU.mult).then_inc(S.kk_norm, 1)
                dve.wait_ge(S.kk_norm, v)
                dve.wait_ge(S.exp_before, v)
                dve.scalar_tensor_tensor(ar[:, 0, OFF:], kk, -1.0, lw, ALU.mult, ALU.mult).then_inc(S.a_tilde, 1)
                dve.wait_ge(S.bonus_sum, v)
                dve.tensor_tensor(seg3(bon), G[1], seg3(v_t[:, OFF:]), ALU.mult).then_inc(S.bonus, 1)
                dve.wait_ge(S.z_tanh, v)
                dve.scalar_tensor_tensor(zz, mix, 1.0, zz, ALU.add, ALU.mult).then_inc(S.z_gate, 1)

                def chain_dve(g, j, i):
                    if i == 4:
                        return
                    u, h = GROUPS[g][j], i // 2
                    c = 2 * u + h
                    b = slice(h * CH, (h + 1) * CH)
                    if i % 2 == 0:
                        dve.wait_ge(S.u_done, 18 * p + c + 1)
                        if h == 0 and u:
                            dve.wait_ge(S.y_done, 9 * p + u)
                        dve.wait_ge(S.wu_copied, 9 * p + u + 1)
                        dve.tensor_tensor(us[b, :], ps[b, B_US, 0:P], wu[ring(g, j)][b, 1, :], ALU.add)\
                            .then_inc(S.u_ready, 1)
                    else:
                        dve.wait_ge(S.s_done, 18 * p + c + 1)
                        dve.wait_ge(S.s_scaled, 18 * p + c + 1)
                        for e in range(2):
                            d = slice(e * HD, (e + 1) * HD)
                            dve.scalar_tensor_tensor(st[d, d], ps[d, B_US, P + e * HD:P + (e + 1) * HD],
                                                     pc[d, c:c + 1], sp[d, d], ALU.mult, ALU.add)\
                                .then_inc(S.s_ready, 1)

                def wu_dve(g):
                    for j, u in enumerate(GROUPS[g]):
                        dve.wait_ge(S.wu_done, 9 * p + u + 1)
                        dve.tensor_copy(wu[ring(g, j)].rearrange("p a t -> p (a t)"), ps[:, B_P[j], 0:2 * P])\
                            .then_inc(S.wu_copied, 1)

                for g, tiles in enumerate(GROUPS):
                    if g >= 2:
                        dve.wait_ge(S.y_done, 9 * p + GROUPS[g - 2][-1] + 1)
                    if g == 0:
                        dve.wait_ge(S.z_gate, v)
                    for j, u in enumerate(tiles):
                        for e in range(2):
                            dve.wait_ge(S.a_done, 18 * p + 2 * u + e + 1)
                            bank = B_M[e] if j else B_X[e]
                            dve.tensor_tensor(amat[ring(g, j)][e].rearrange("p (a t) -> p a t", a=2),
                                              ps[:, bank, :].rearrange("p (a t) -> p a t", a=2),
                                              masks[:, :].unsqueeze(1).to_broadcast([P, 2, 2 * P]), ALU.mult)\
                                .then_inc(S.a_masked, 1)
                    slots = chain_slots(g - 1) if g else []
                    for l in range(LEVELS[g]):
                        for j, u in enumerate(tiles):
                            dve.wait_ge(S.p_done, STEPS * p + step(g, l, j) + 1)
                            dve.tensor_tensor(pm[j] if l else xs[j][:, :, 0, :],
                                              ps[:, B_P[j], 0:2 * P].rearrange("p (e t) -> p e t", e=2),
                                              levels[:, l * P:(l + 1) * P].unsqueeze(1).to_broadcast([P, 2, P]),
                                              ALU.mult).then_inc(S.p_masked, 1)
                        for i in (2 * l, 2 * l + 1):
                            if i < len(slots):
                                chain_dve(g - 1, *slots[i])
                    wu_dve(g)
                for j, i in chain_slots(NG - 1):
                    chain_dve(NG - 1, j, i)
                dve.wait_ge(S.gn_mean, v)
                dve.scalar_tensor_tensor(seg3(y_t), G[1], -1.0 / HD, seg3(y_t), ALU.mult, ALU.add)\
                    .then_inc(S.gn_centred, 1)
                dve.wait_ge(S.gn_rstd, v)
                dve.tensor_tensor(y_t, y_t, sq, ALU.mult).then_inc(S.gn_scaled, 1)
                dve.wait_ge(S.gn_scaled, v)
                dve.tensor_scalar(y_t, y_t, q(Q_GW), q(Q_GB), ALU.mult, ALU.add).then_inc(S.gn_affine, 1)
                dve.wait_ge(S.gn_affine, v)
                dve.tensor_tensor(y_t, y_t, bon, ALU.add).then_inc(S.gn_bonus, 1)
                dve.wait_ge(S.gn_bonus, v)
                dve.scalar_tensor_tensor(y_t, y_t, 0.5, zz, ALU.mult, ALU.mult).then_inc(S.out_ready, 1)

            def split_rows(r, width):
                for k in range(KO):
                    dve.wait_ge(S.x_hi, KO * r + k + 1)
                    dve.tensor_tensor(xl[:, k, 0:width], (osq if r == 1 else obq)[k % 2][:, 0:width], f32(xh[:, k, 0:width]), ALU.subtract)\
                        .then_inc(S.x_lo, 1)

            split_lo(N_AO % 2, N_AO)
            split_rows(1, TP)
            split_lo((N_AO + 1) % 2, N_AO + 1)
            dve.wait_ge(S.xt_loaded, 16)
            for m in range(KO):
                dve.wait_ge(S.proj_done, N_AO + m + 1)
                dve.tensor_tensor(seg3(h_t[:, m, :]), G[(N_AO + m) % 2], seg3(h_t[:, m, :]), ALU.add)\
                    .then_inc(S.res_added, 1)
                if m + 2 < KO:
                    split_lo((N_AO + m) % 2, N_AO + m + 2)
            normalise(1)
            split_lo(N_F % 2, N_F, H)
            dve.wait_ge(S.x_lo, 3 * KO)
            dve.wait_ge(S.proj_done, N_F + 1)
            g = G[N_F % 2]
            dve.tensor_scalar(seg3(bsq[0:H, :]), g[0:H], fb_in[0:H, :], None, ALU.add).then_inc(S.f_logit, 1)
            dve.wait_ge(S.x_lo, 3 * KO)
            dve.memset(zb[0:H, :], 1.0).then_inc(S.setup_b, 1)
            dve.memset(vflat[0][:, :, HD:], 1.0).then_inc(S.setup_b, 1)
            dve.memset(vflat[1][:, :, 0:HD], 1.0).then_inc(S.setup_b, 1)
            dve.memset(mpart, MASKED).then_inc(S.setup_b, 1)
            dve.wait_ge(S.f_logit, 1)
            dve.tensor_scalar(kb[0:H, :], bsq[0:H, :], 0.0, None, ALU.min).then_inc(S.f_min, 1)
            dve.wait_ge(S.f_min, 1)
            dve.wait_ge(S.f_ln, 1)
            dve.tensor_tensor(kb[0:H, :], kb[0:H, :], brs[0:H, :], ALU.subtract).then_inc(S.f_log, 1)
            dve.wait_ge(S.f_log, 1)
            dve.wait_ge(S.setup_b, 4)
            dve.tensor_tensor_scan(vb[0:H, :], zb[0:H, :], kb[0:H, :], 0.0, ALU.mult, ALU.add).then_inc(S.f_cum, 1)
            dve.wait_ge(S.f_cum, 1)
            dve.tensor_scalar(bsq[0:H, :], vb[0:H, :], -1.0 / SCALE, None, ALU.mult).then_inc(S.c_scaled, 1)
            dve.wait_ge(S.c_hi, 1)
            dve.tensor_tensor(chl[0:H, 1, :], bsq[0:H, :], f32(chl[0:H, 0, :]), ALU.subtract).then_inc(S.c_lo, 1)
            dve.wait_ge(S.c_lo, 1)
            dve.wait_ge(S.h_stored, 16)
            dve.wait_ge(S.setup_bp, 8)
            dve.sem_inc(S.o_norm, 2)
            dve.sem_inc(S.o_gated, 1)

            def round_dve(p, steps):
                first = isinstance(p, int) and p < 0
                for st_ in steps:
                    kind = st_[0]
                    if kind == "proj":
                        j, i = st_[1:]
                        if i == 0 and j < 3:
                            split_lo((N_B + j + 1) % 2, 4 * p + 4 + N_B + j + 1)
                    elif kind == "sumsq":
                        j, i = st_[1:]
                        if i == 2:
                            dve.wait_ge(S.hn_rstd, 2 * p + 3 + j)
                            dve.scalar_tensor_tensor((kb, qb)[j], (kb, qb)[j], param((C_KN, C_QN)[j]), brs, ALU.mult,
                                                     ALU.mult).then_inc(S.hn_full, 1)
                    elif kind == "stack":
                        e = st_[1]
                        q_ = p + 1 - e
                        d, o = slice(e * HD, (e + 1) * HD), slice((1 - e) * HD, (2 - e) * HD)
                        dve.wait_ge(S.st_hi, 4 * q_ + 2 * e + 1)
                        dve.tensor_tensor(ka[e][o, :], kb[d, :], f32(ka[e][d, :]), ALU.subtract).then_inc(S.stacked, 1)
                        dve.tensor_copy(kb2[e][0:HD, :], f32(ka[e][d, :])).then_inc(S.stacked, 1)
                        dve.wait_ge(S.st_hi, 4 * q_ + 2 * e + 2)
                        dve.tensor_copy(qc2[e][0:HD, :], f32(qa[e][d, :])).then_inc(S.stacked, 1)
                        dve.tensor_copy(qa[e][o, :], f32(qa[e][d, :])).then_inc(S.stacked, 1)
                        dve.tensor_tensor(qb2[e][0:HD, :], qb[d, :], f32(qa[e][d, :]), ALU.subtract)\
                            .then_inc(S.stacked, 1)
                    elif kind == "gate":
                        dve.wait_ge(S.bz_tanh, p + 1)
                        dve.scalar_tensor_tensor(zg, zg, 1.0, zb, ALU.add, ALU.mult).then_inc(S.bz_gate, 1)
                    elif kind == "smax":
                        e, i = st_[1:]
                        base = NS * (2 * (p + 1 - e) + e)
                        t, part, k0, k1 = KSEG[i]
                        dve.wait_ge(S.smax_done, base + i + 1)
                        dve.tensor_reduce(mpart[:, 3 * t + part:3 * t + part + 1], ps[:, B_SM[i % 2], 0:k1 - k0],
                                          AX.X, ALU.max).then_inc(S.smax, 1)
                        if i == NS - 1:
                            dve.wait_ge(S.smax, base + NS)
                            dve.tensor_reduce(mcol, mpart.rearrange("p (t i) -> p t i", i=3), AX.X, ALU.max)\
                                .then_inc(S.mcol_ready, 1)
                            dve.wait_ge(S.mcol_ready, 2 * (p + 1 - e) + e + 1)
                    elif kind == "weighted":
                        e, w = st_[1:]
                        qb_, kt = UNITS[w]
                        if kt == 4 * qb_ + 4:
                            b = slice(e * HD, (e + 1) * HD)
                            dve.wait_ge(S.d_recip, 4 * p + 2 * e + qb_ + 1)
                            if e == 0 and qb_ == 0:
                                dve.wait_ge(S.ob_free, p + 1)
                            dve.tensor_tensor(ob[b, qb_ * 512:(qb_ + 1) * 512], ps[b, B_PV[qb_], :], dln[b, :], ALU.mult)\
                                .then_inc(S.o_norm, 1)
                            if e and qb_:
                                dve.wait_ge(S.o_norm, 4 * p + 6)
                                dve.wait_ge(S.bz_gate, p + 1)
                                dve.scalar_tensor_tensor(ob, ob, 0.5, zg[:, META:T], ALU.mult, ALU.mult)\
                                    .then_inc(S.o_gated, 1)

            split_lo(N_B % 2, N_B)
            round_dve(-1, first_round())
            with dve.Fori(0, KO - 1) as p:
                split_lo(N_B % 2, 4 * p + 4 + N_B)
                round_dve(p, order(0, True))
                round_dve(p, order(1, True))
            round_dve(KO - 1, order(0, False))
            round_dve(KO - 1, order(1, False))
            split_lo(N_BO % 2, N_BO)
            split_rows(3, SEQ)
            split_lo((N_BO + 1) % 2, N_BO + 1)
            for m in range(KO):
                dve.wait_ge(S.proj_done, N_B + m + 1)
                dve.wait_ge(H_LOADED[m % 2], 16 * (m // 2 + 1))
                if m >= 2:
                    dve.wait_ge(S.fin_tr, m - 1)
                g = 2 * (m % 2)
                dve.tensor_tensor(fin[m % 2], ps[:, g:g + 2, :].rearrange("p b c -> p (b c)"), hres[m % 2],
                                  ALU.add).then_inc(S.fin_sum, 1)
                if m + 2 < KO:
                    split_lo((N_BO + m) % 2, N_BO + m + 2)

        @block.tensor
        def _(pe):
            def products(group, slot, width=P, segs=3, seg=SEG):
                for c in range(segs):
                    acc = group[0:width, c, 0:seg]
                    t = slice(c * seg, (c + 1) * seg)
                    for k in range(KO):
                        pe.matmul(acc, wh[:, slot, k, 0:width], xh[:, k, t], start=(k == 0), stop=False)
                        pe.matmul(acc, wl[:, slot, k, 0:width], xh[:, k, t], start=False, stop=False)
                        mm = pe.matmul(acc, wh[:, slot, k, 0:width], xl[:, k, t], start=False, stop=(k == KO - 1))
                return mm

            def over(group, lhs, src):
                for c in range(3):
                    mm = pe.matmul(group[:, c, :], lhs, src[:, c * SEG:(c + 1) * SEG], start=True, stop=True)
                return mm

            def sum_squares(r):
                for k in range(KO):
                    pe.wait_ge(S.h_sq, KO * r + k + 1)
                    for c in range(3):
                        mm = pe.matmul(G[0][:, c, :], all_ones[:, :], sq2[k % 2][:, c * SEG:(c + 1) * SEG],
                                       start=(k == 0), stop=(k == KO - 1))
                    mm.then_inc(S.h_sumsq, 1)

            pe.wait_ge(S.consts_loaded, 80)
            for t in range(NT):
                pe.wait_ge(X_LOADED[t % 2], 16 * (t // 2 + 1))
                if t >= 2:
                    pe.wait_ge(S.x_evac, t - 1)
                n = TILE_TOK[t]
                for k in range(KO):
                    mm = pe.transpose(ps[:, 2 * (t % 2) + k // 4, (k % 4) * P:(k % 4) * P + n],
                                      xrow[t % 2][0:n, k * P:(k + 1) * P], ident[0:n, 0:n])
                mm.then_inc(S.x_tr, 1)
            pe.wait_ge(S.rows_loaded, 16)
            pe.transpose(ps[:, 6, 0:NROWS], prow[0:NROWS, :], ident[0:NROWS, 0:NROWS]).then_inc(S.param_tr, 1)
            pe.wait_ge(S.x_evac, NT)
            pe.wait_ge(S.setup_dve, 6)
            sum_squares(0)
            pe.wait_ge(S.x_lo, KO)
            pe.wait_ge(S.w_lo, 2)
            pe.wait_ge(S.h_rstd, 1)
            products(G[0], 0).then_inc(S.proj_done, 1)
            pe.wait_ge(S.lora_tanh, 1)
            pe.wait_ge(S.setup_pool, 4)
            with pe.Fori(0, KO) as p:
                v = p + 1
                pe.wait_ge(S.pair_free, v)
                pe.wait_ge(S.up_copied, v)
                over(G[0], upf[0:LORA, :], lo[0:LORA, :]).then_inc(S.dec_done, 1)
                over(G[1], upf[LORA:, :], lo[LORA:, :]).then_inc(S.icl_done, 1)
                pe.wait_ge(S.w_lo, 4 * p + 3)
                pe.wait_ge(S.dec_tanh, v)
                products(G[0], (N_A + 0) % 2).then_inc(S.proj_done, 1)
                pe.wait_ge(S.w_lo, 4 * p + 4)
                pe.wait_ge(S.icl_tanh, v)
                products(G[1], (N_A + 1) % 2).then_inc(S.proj_done, 1)
                pe.wait_ge(S.w_lo, 4 * p + 5)
                pe.wait_ge(S.shifted, 4 * p + 2)
                products(G[0], (N_A + 2) % 2).then_inc(S.proj_done, 1)
                pe.wait_ge(S.kk_sq, v)
                pe.wait_ge(S.shifted, 4 * p + 3)
                over(G[1], head_ones[:, :], sq).then_inc(S.kk_sumsq, 1)
                pe.wait_ge(S.w_lo, 4 * p + 6)
                pe.wait_ge(S.shifted, 4 * p + 4)
                products(G[0], (N_A + 3) % 2).then_inc(S.proj_done, 1)
                pe.wait_ge(S.bonus_prod, v)
                pe.wait_ge(S.kk_guard, v)
                over(G[1], head_ones[:, :], mix).then_inc(S.bonus_sum, 1)
                for s, c in ((S.a_tilde, v), (S.r_tilde, v), (S.b_tilde, v), (S.k_tilde, v), (S.bonus, v),
                             (S.shifted, 4 * p + 5), (S.z_gate, v)):
                    pe.wait_ge(s, c)

                def chain_pe(g, j, i):
                    u, h = GROUPS[g][j], i // 2
                    c, t9 = 2 * u + h, 9 * p + u
                    b = slice(h * CH, (h + 1) * CH)
                    rows_u, am = rows_sb[ring(g, j)], amat[ring(g, j)]
                    if i in (0, 2):
                        if c == 0:
                            pe.wait_ge(S.state_zero, v)
                        else:
                            pe.wait_ge(S.s_ready, 36 * p + 2 * c)
                        pe.wait_ge(S.wu_copied, t9 + 1)
                        pe.matmul(ps[b, B_US, 0:P], wu[ring(g, j)][:, 0, b], st, start=True, stop=True)\
                            .then_inc(S.u_done, 1)
                        if h == 0 and u:
                            pe.wait_ge(S.y_copied, t9)
                        pe.matmul(ps[:, B_Y, b], st, ar[:, 1, u * P + h * CH:u * P + (h + 1) * CH],
                                  start=(h == 0), stop=False, skip_group_check=True)
                    elif i in (1, 3):
                        pe.wait_ge(S.u_ready, 18 * p + c + 1)
                        o = ps[:, B_US, P:2 * P]
                        pe.matmul(o, rows_u[b, 2, :], rows_u[b, 3, :], start=True, stop=False)
                        pe.matmul(o, rows_u[b, 1, :], us[b, :], start=False, stop=True).then_inc(S.s_done, 1)
                    else:
                        for e in range(2):
                            d = slice(e * HD, (e + 1) * HD)
                            pe.matmul(ps[d, B_Y, 0:P], us[:, d], am[e][:, P:2 * P], start=False, stop=False,
                                      skip_group_check=True)
                            mm = pe.matmul(ps[d, B_Y, 0:P], rows_u[:, 3, d], am[e][:, 3 * P:], start=False,
                                           stop=True, skip_group_check=True)
                        mm.then_inc(S.y_done, 1)

                def rows_pe(g):
                    for j, u in enumerate(GROUPS[g]):
                        c = slice(u * P, (u + 1) * P)
                        for i, src in enumerate((ar[:, 0, c], b_t[:, c], k_t[:, c], v_t[:, c])):
                            mm = pe.transpose(ps[:, B_M[j], i * P:(i + 1) * P], src, ident[:, :])
                        mm.then_inc(S.tr_done, 1)

                def wu_pe(g):
                    for j, u in enumerate(GROUPS[g]):
                        pe.wait_ge(S.x_copied, STEPS * p + step(g, LEVELS[g] - 1, j) + 1)
                        for e in range(2):
                            d = slice(e * HD, (e + 1) * HD)
                            pe.matmul(ps[d, B_P[j], 0:P], rows_sb[ring(g, j)][:, 0, d], xs[j][:, e, 1, :],
                                      start=True, stop=True)
                            mm = pe.matmul(ps[:, B_P[j], P + e * HD:P + (e + 1) * HD], xs[j][:, e, 1, :],
                                           qs[j][:, d], start=True, stop=True)
                        mm.then_inc(S.wu_done, 1)

                rows_pe(0)
                for g, tiles in enumerate(GROUPS):
                    for j, u in enumerate(tiles):
                        c = slice(u * P, (u + 1) * P)
                        if j:
                            pe.wait_ge(S.rows_ready, 9 * p + u + 1)
                        for e in range(2):
                            d = slice(e * HD, (e + 1) * HD)
                            bank = B_M[e] if j else B_X[e]
                            pe.matmul(ps[:, bank, 0:2 * P], b_t[d, c], ar[d, :, c], start=True, stop=True)
                            pe.matmul(ps[:, bank, 2 * P:], k_t[d, c], ar[d, :, c], start=True, stop=True)\
                                .then_inc(S.a_done, 1)
                    slots = chain_slots(g - 1) if g else []
                    for l in range(LEVELS[g]):
                        last = l == LEVELS[g] - 1
                        for j, u in enumerate(tiles):
                            if l == 0:
                                pe.wait_ge(S.a_masked, 18 * p + 2 * u + 2)
                                if g:
                                    pe.wait_ge(S.wu_copied, 9 * p + tiles[0])
                            elif l == 1:
                                pe.wait_ge(S.p_masked, STEPS * p + step(g, 0, j) + 1)
                            else:
                                pe.wait_ge(S.x_copied, STEPS * p + step(g, l - 1, j) + 1)
                            pe.matmul(ps[:, B_P[j], 0:2 * P], identb[:, :],
                                      identb[:, :].unsqueeze(1).to_broadcast([P, 2, P]), start=True, stop=False,
                                      skip_group_check=True)
                            for e in range(2):
                                mm = pe.matmul(ps[:, B_P[j], e * P:(e + 1) * P], amat[ring(g, j)][e][:, 0:P],
                                               xs[j][:, e, 0, :] if l else ident[:, :], start=False, stop=True,
                                               skip_group_check=True)
                            mm.then_inc(S.p_done, 1)
                        if 2 * l < len(slots):
                            chain_pe(g - 1, *slots[2 * l])
                        for j, u in enumerate(tiles):
                            pe.wait_ge(S.p_masked, STEPS * p + step(g, l, j) + 1)
                            if l == 0:
                                pe.wait_ge(S.a_masked, 18 * p + 2 * tiles[0] + 2)
                            if l == 1:
                                pe.wait_ge(S.x_copied, STEPS * p + step(g, 0, j) + 1)
                            for e in range(2):
                                xb = ps[:, B_X[j], 2 * e * P:(2 * e + 2) * P].rearrange("p (a t) -> p a t", a=2)
                                if l and not last:
                                    pe.matmul(xb[:, 0, :], xs[j][:, e, 1, :], pm[j][:, e, :], start=True, stop=True)
                                if l:
                                    mm = pe.matmul(xb[:, 1, :], pm[j][:, e, :], xs[j][:, e, 1, :], start=True,
                                                   stop=True)
                                else:
                                    mm = pe.matmul(xb[:, 1, :], xs[j][:, e, 0, :], ident[:, :], start=True,
                                                   stop=True)
                            mm.then_inc(S.x_done, 1)
                        if 2 * l + 1 < len(slots):
                            chain_pe(g - 1, *slots[2 * l + 1])
                        if l == 0:
                            for j, u in enumerate(tiles):
                                pe.wait_ge(S.a_masked, 18 * p + 2 * tiles[-1] + 2)
                                pe.wait_ge(S.rows_ready, 9 * p + tiles[-1] + 1)
                                for e in range(2):
                                    d = slice(e * HD, (e + 1) * HD)
                                    mm = pe.matmul(ps[:, B_M[j], d], amat[ring(g, j)][e][:, 2 * P:3 * P],
                                                   rows_sb[ring(g, j)][:, 3, d], start=True, stop=True)
                                mm.then_inc(S.q_done, 1)
                    pe.wait_ge(S.q_copied, 9 * p + tiles[-1] + 1)
                    if g + 1 < NG:
                        rows_pe(g + 1)
                    wu_pe(g)
                for j, i in chain_slots(NG - 1):
                    chain_pe(NG - 1, j, i)
                pe.wait_ge(S.y_copied, 9 * p + NT)
                over(G[1], head_ones[:, :], y_t).then_inc(S.gn_mean, 1)
                pe.wait_ge(S.gn_sq, v)
                over(G[0], head_ones[:, :], sq).then_inc(S.gn_var, 1)

            pe.wait_ge(S.x_lo, 2 * KO)
            for m in range(KO):
                n = N_AO + m
                pe.wait_ge(S.w_lo, n + 2)
                if m >= 2:
                    pe.wait_ge(S.res_added, m - 1)
                products(G[n % 2], n % 2).then_inc(S.proj_done, 1)
            pe.wait_ge(S.res_added, KO)
            sum_squares(1)
            pe.wait_ge(S.x_lo, 3 * KO)
            pe.wait_ge(S.w_lo, N_F + 2)
            products(G[N_F % 2], N_F % 2, H).then_inc(S.proj_done, 1)

            def round_pe(p, steps):
                first = isinstance(p, int) and p < 0
                for st_ in steps:
                    kind = st_[0]
                    if kind in ("proj", "sumsq", "vrow"):
                        j, i = st_[1:]
                        local = {"proj": (L_K, L_Q, L_V, L_Z), "sumsq": (L_SK, L_SQ), "vrow": (L_VROW0, L_VROW1)}[kind][j] + i
                        bank = ps[:, B_G[local % 2], :]
                        if not (first and local < L_K + 2):
                            pe.wait_ge(S.b_evac, chunk(p, local) - 1)
                    if kind == "proj":
                        slot = (N_B + j) % 2
                        if i == 0:
                            pe.wait_ge(S.w_lo, 4 * p + 4 + N_B + j + 2)
                        t = slice(i * SEG, (i + 1) * SEG)
                        for k in range(KO):
                            pe.matmul(bank[:, 0:SEG], wh[:, slot, k, :], xh[:, k, t], start=(k == 0), stop=False)
                            pe.matmul(bank[:, 0:SEG], wl[:, slot, k, :], xh[:, k, t], start=False, stop=False)
                            mm = pe.matmul(bank[:, 0:SEG], wh[:, slot, k, :], xl[:, k, t], start=False,
                                           stop=(k == KO - 1))
                        mm.then_inc(S.b_done, 1)
                    elif kind == "sumsq":
                        if i == 0:
                            pe.wait_ge(S.hn_sq, 2 * p + 3 + j)
                        pe.matmul(bank[:, 0:SEG], head_ones[:, :], bsq[:, i * SEG:(i + 1) * SEG], start=True, stop=True)\
                            .then_inc(S.b_done, 1)
                    elif kind == "vrow":
                        d = slice(j * HD, (j + 1) * HD)
                        if i == 0:
                            pe.wait_ge(S.b_evac, chunk(p - j, L_V) + 3)
                        for t in range(7) if i == 0 else range(7, NT):
                            n_k, c0 = min(P, T - t * P), (t - 7 * i) * HD
                            mm = pe.matmul(bank[0:n_k, c0:c0 + HD], vb[d, t * P:t * P + n_k], ident[d, d],
                                           start=True, stop=True)
                        mm.then_inc(S.b_done, 1)
                    elif kind == "smax":
                        e, i = st_[1:]
                        q_ = p + 1 - e
                        base = NS * (2 * q_ + e)
                        t, _, k0, k1 = KSEG[i]
                        bank = ps[:, B_SM[i % 2], :]
                        if i == 0:
                            pe.wait_ge(S.stacked, 10 * q_ + 5 * e + 3)
                            pe.wait_ge(C_ROWS[e], 16 * q_ + 16)
                            if not first:
                                pe.wait_ge(S.m_row, 4 * q_ + 2 * e)
                        elif i >= 2:
                            pe.wait_ge(S.smax, base + i - 1)
                        m0 = META + t * P
                        mm = pe.matmul(bank[:, 0:k1 - k0], qc2[e][0:HD + 3, m0:m0 + P], kb2[e][0:HD + 3, k0:k1],
                                       start=True, stop=(k1 <= m0), skip_group_check=True)
                        if k1 > m0:
                            c0 = max(m0, k0)
                            mm = pe.matmul(bank[:, c0 - k0:k1 - k0], identb[:, :], causal[:, P + c0 - m0:P + k1 - m0],
                                           start=False, stop=True, skip_group_check=True)
                        mm.then_inc(S.smax_done, 1)
                    elif kind == "maxrow":
                        e = st_[1]
                        pe.wait_ge(S.mcol_ready, 2 * (p + 1 - e) + e + 1)
                        for a in range(2):
                            for t in range(4):
                                mm = pe.matmul(ps[0:1, B_SM[a], t * P:(t + 1) * P], mcol[:, 4 * a + t:4 * a + t + 1],
                                               ident[:, :], start=True, stop=True)
                            mm.then_inc(S.m_row_done, 1)
                    elif kind == "scores":
                        e, w = st_[1:]
                        n_k, q0, n_q, off, n_diag = unit(w)
                        kt = UNITS[w][1]
                        if w == 0:
                            pe.wait_ge(S.m_row, 4 * p + 2 * e + 2)
                            pe.wait_ge(S.stacked, 10 * p + 5 * e + 5)
                        if w >= 2:
                            pe.wait_ge(S.p_exp, 2 * NU * p + NU * e + w - 1)
                        o = ps[0:n_k, B_ST[w % 2], 0:n_q]
                        ks, qs_ = slice(kt * P, kt * P + n_k), slice(META + q0, META + q0 + n_q)
                        pe.matmul(o, ka[e][:, ks], qa[e][:, qs_], start=True, stop=False, skip_group_check=True)
                        mm = pe.matmul(o, kb2[e][0:HD + 3, ks], qb2[e][0:HD + 3, qs_], start=False,
                                       stop=(n_diag == 0), skip_group_check=True)
                        if n_diag:
                            mm = pe.matmul(ps[0:n_k, B_ST[w % 2], 0:n_diag], identb[:, 0:n_k],
                                           causal[:, off:off + n_diag], start=False, stop=True, skip_group_check=True)
                        mm.then_inc(S.st_done, 1)
                    elif kind == "weighted":
                        e, w = st_[1:]
                        qb_, kt = UNITS[w]
                        n_k, q0, n_q, _, _ = unit(w)
                        pe.wait_ge(S.p_exp, 2 * NU * p + NU * e + w + 1)
                        if w == 0:
                            pe.wait_ge(S.b_evac, chunk(p - 1 + e, (L_VROW0, L_VROW1)[e]) + 2)
                        if kt == 0:
                            pe.wait_ge(S.o_norm, 4 * p + 2 * e + qb_ + 1)
                        pe.matmul(ps[:, B_PV[qb_], q0 - 512 * qb_:512], vflat[e][0:n_k, kt, :], pt[w % 3][0:n_k, 0:n_q],
                                  start=(kt == 0), stop=(kt == 4 * qb_ + 4), skip_group_check=True)\
                            .then_inc(S.pv_done, 1)

            pe.wait_ge(S.f_logit, 1)
            round_pe(-1, first_round())
            with pe.Fori(0, KO - 1) as p:
                round_pe(p, order(0, True))
                round_pe(p, order(1, True))
            round_pe(KO - 1, order(0, False))
            round_pe(KO - 1, order(1, False))
            pe.wait_ge(S.o_norm, 4 * KO + 2)
            pe.wait_ge(S.x_lo, 4 * KO)

            def back(m):
                pe.wait_ge(S.fin_sum, m + 1)
                if m >= 2:
                    pe.wait_ge(S.fin_evac, m - 1)
                for t in range(KO):
                    mm = pe.transpose(ps[:, 4 + 2 * (m % 2) + t // 4, (t % 4) * P:(t % 4 + 1) * P],
                                      fin[m % 2][:, t * P:(t + 1) * P], ident[:, :])
                mm.then_inc(S.fin_tr, 1)

            for m in range(KO):
                n = N_BO + m
                pe.wait_ge(S.w_lo, n + 2)
                if m >= 2:
                    pe.wait_ge(S.fin_sum, m - 1)
                products(ps[:, 2 * (m % 2):2 * (m % 2) + 2, :], n % 2, P, 2, 512).then_inc(S.proj_done, 1)
                if m:
                    back(m - 1)
            back(KO - 1)


def kernel(**inputs):
    import concourse.bacc as bacc
    from concourse.bass_utils import run_bass_kernel_spmd

    a = {k: np.asarray(v) for k, v in inputs.items()}
    rows = np.concatenate(
        [a["a_shift_mu"][0][:4 * D].reshape(-1, P)]
        + [a[n][0].reshape(-1, P) for n in ("a_decay_bias", "a_iclr_bias", "a_k_k", "a_k_a", "a_r_k",
                                            "a_gn_w", "a_gn_b")]
        + [a["a_shift_mu"][0][4 * D:].reshape(1, P), a["a_norm"][0].reshape(-1, P),
           a["kv_norm"].reshape(-1, P), a["b_norm"][0].reshape(-1, P),
           np.tile(a["k_norm"], 2)[None], np.tile(a["b_q_norm"][0], 2)[None]], axis=0)
    i = np.arange(P)
    same = i[:, None] // CH == i[None, :] // CH
    masks = np.concatenate([same & (i[:, None] < i[None, :]), same & (i[:, None] <= i[None, :])],
                           axis=1).astype(np.float32)
    lev = []
    for b in (1, 2, 4, 8, 16, 32):
        t, s = i[:, None] // b, i[None, :] // b
        lev.append(((t // 2 == s // 2) & (t == s + 1)) | (i[:, None] == i[None, :]))
    levels = np.concatenate(lev, axis=1).astype(np.float32)
    ident = np.eye(P, dtype=np.float32)
    causal = np.concatenate([np.where(i[:, None] > i[None, :], MASKED, 0.0),
                             np.where(i[:, None] < i[None, :], MASKED, 0.0)], axis=1).astype(np.float32)
    arrays = {
        "x": a["x"][0], "meta": a["meta_tokens"], "rows": rows, "w_in": a["a_w_in"][0],
        "up": np.concatenate([a["a_decay_up"][0], a["a_iclr_up"][0]], axis=0), "w_out": a["a_w_out"][0],
        "kv_w": a["kv_w"], "f_bias": a["kv_f_bias"][:, None], "b_w_in": a["b_w_in"][0],
        "b_w_out": a["b_w_out"][0], "ident_d": ident, "masks_d": masks, "levels_d": levels,
        "causal_d": causal,
    }
    nc = bacc.Bacc("TRN2", target_bir_lowering=False, num_devices=1)
    feeds, aps = {}, {}
    for name, v in arrays.items():
        v = np.ascontiguousarray(v)
        feeds[f"in_{name}"] = v
        aps[name] = nc.dram_tensor(f"in_{name}", v.shape, mybir.dt.from_np(v.dtype), kind="ExternalInput").ap()
    aps["out"] = nc.dram_tensor("out_0", (SEQ, D), F32, kind="ExternalOutput").ap()
    build(nc, **aps)
    r = run_bass_kernel_spmd(nc, [feeds], core_ids=[0])
    return r.results[0]["out_0"].reshape(1, SEQ, D)
```

```python
from contextlib import ExitStack

import numpy as np

import concourse.bass as bass
from concourse import mybir

F32 = mybir.dt.float32
F32R = mybir.dt.float32r
BF16 = mybir.dt.bfloat16
ALU = mybir.AluOpType
ACT = mybir.ActivationFunctionType
AX = mybir.AxisListType

P = 128
D = 1024
SEQ = 1024
META = 16
T = SEQ + META
HD = 64
H = D // HD
KO = D // P
SEG = 348
TP = 3 * SEG
CH = 64
NT = 9
OFF = NT * P - T
TW = OFF + TP
LORA = 64
A_COLS = 4 * D + 2 * LORA
RMS_EPS = 1e-6
GN_EPS = 64e-5
KK_FLOOR = 1e-12
C_DECAY = float(np.exp(-0.5)) / 2
LN_SCALE = 2.0 ** 20
MASKED = -1e30
SCALE = HD ** -0.5

(Q_MUR, Q_MUK, Q_MUV, Q_MUZ, Q_DB, Q_IB, Q_KK, Q_KA, Q_RK, Q_GW, Q_GB,
 Q_NR, Q_NK, Q_NV, Q_NZ, Q_HDB, Q_HIB, Q_NKA) = range(18)
NQ = 18
ROW_LORA, ROW_AN, ROW_KVN, ROW_BN, ROW_KN, ROW_QN, NROWS = 88, 89, 97, 105, 113, 114, 115
C_LORA = NQ * KO
C_AN, C_KVN, C_BN, C_KN, C_QN, C_NLORA = (C_LORA + 1, C_LORA + 9, C_LORA + 17, C_LORA + 25,
                                          C_LORA + 26, C_LORA + 27)
NCOLS = C_LORA + 28

class Signals:

    def __init__(self, sem):
        self.x_loaded0 = sem("x_loaded0")
        self.x_loaded1 = sem("x_loaded1")
        self.rows_loaded = sem("rows_loaded")
        self.w_asked = sem("w_asked")
        self.consts_loaded = sem("consts_loaded")
        self.up_loaded = sem("up_loaded")
        self.w_loaded0 = sem("w_loaded0")
        self.w_loaded1 = sem("w_loaded1")
        self.w_scaled = sem("w_scaled")
        self.w_hi = sem("w_hi")
        self.w_lo = sem("w_lo")
        self.proj_done = sem("proj_done")
        self.param_tr = sem("param_tr")
        self.param_copied = sem("param_copied")
        self.param_derived = sem("param_derived")
        self.pads_zero = sem("pads_zero")
        self.setup_dve = sem("setup_dve")
        self.setup_pool = sem("setup_pool")
        self.x_tr = sem("x_tr")
        self.x_evac = sem("x_evac")
        self.xt_stored = sem("xt_stored")
        self.h_sq = sem("h_sq")
        self.h_sumsq = sem("h_sumsq")
        self.h_ln = sem("h_ln")
        self.h_rstd = sem("h_rstd")
        self.xn_mul = sem("xn_mul")
        self.x_hi = sem("x_hi")
        self.x_lo = sem("x_lo")
        self.mu_done = sem("mu_done")
        self.carried = sem("carried")
        self.shifted = sem("shifted")
        self.lora_tanh = sem("lora_tanh")
        self.pair_params = sem("pair_params")
        self.gn_params = sem("gn_params")
        self.up_copied = sem("up_copied")
        self.dec_done = sem("dec_done")
        self.icl_done = sem("icl_done")
        self.dec_tanh = sem("dec_tanh")
        self.icl_tanh = sem("icl_tanh")
        self.logw = sem("logw")
        self.cumlog = sem("cumlog")
        self.iclr = sem("iclr")
        self.cum_before = sem("cum_before")
        self.exp_in = sem("exp_in")
        self.exp_neg = sem("exp_neg")
        self.exp_before = sem("exp_before")
        self.chunk_end = sem("chunk_end")
        self.kk_raw = sem("kk_raw")
        self.kk_sq = sem("kk_sq")
        self.kk_sumsq = sem("kk_sumsq")
        self.kk_guard = sem("kk_guard")
        self.kk_ln = sem("kk_ln")
        self.kk_rn = sem("kk_rn")
        self.kk_norm = sem("kk_norm")
        self.a_tilde = sem("a_tilde")
        self.r_tilde = sem("r_tilde")
        self.k_mix = sem("k_mix")
        self.k_new = sem("k_new")
        self.k_tilde = sem("k_tilde")
        self.kk_a = sem("kk_a")
        self.b_tilde = sem("b_tilde")
        self.bonus_prod = sem("bonus_prod")
        self.bonus_sum = sem("bonus_sum")
        self.bonus = sem("bonus")
        self.z_tanh = sem("z_tanh")
        self.z_gate = sem("z_gate")
        self.state_zero = sem("state_zero")
        self.tr_done = sem("tr_done")
        self.rows_ready = sem("rows_ready")
        self.a_done = sem("a_done")
        self.a_masked = sem("a_masked")
        self.q_done = sem("q_done")
        self.q_copied = sem("q_copied")
        self.p_done = sem("p_done")
        self.p_masked = sem("p_masked")
        self.x_done = sem("x_done")
        self.x_copied = sem("x_copied")
        self.wu_done = sem("wu_done")
        self.wu_copied = sem("wu_copied")
        self.u_done = sem("u_done")
        self.u_ready = sem("u_ready")
        self.s_done = sem("s_done")
        self.s_ready = sem("s_ready")
        self.s_scaled = sem("s_scaled")
        self.y_done = sem("y_done")
        self.y_copied = sem("y_copied")
        self.gn_mean = sem("gn_mean")
        self.gn_centred = sem("gn_centred")
        self.gn_sq = sem("gn_sq")
        self.gn_var = sem("gn_var")
        self.gn_ln = sem("gn_ln")
        self.gn_rstd = sem("gn_rstd")
        self.gn_scaled = sem("gn_scaled")
        self.gn_affine = sem("gn_affine")
        self.gn_bonus = sem("gn_bonus")
        self.out_ready = sem("out_ready")
        self.out_stored = sem("out_stored")
        self.out_free = sem("out_free")
        self.o_loaded0 = sem("o_loaded0")
        self.o_loaded1 = sem("o_loaded1")
        self.xt_loaded0 = sem("xt_loaded0")
        self.xt_loaded1 = sem("xt_loaded1")
        self.h_acc = sem("h_acc")
        self.res_added = sem("res_added")
        self.f_logit = sem("f_logit")
        self.f_abs = sem("f_abs")
        self.f_exp = sem("f_exp")
        self.f_ln = sem("f_ln")
        self.f_min = sem("f_min")
        self.f_log = sem("f_log")
        self.f_cum = sem("f_cum")
        self.c_scaled = sem("c_scaled")
        self.c_hi = sem("c_hi")
        self.c_lo = sem("c_lo")
        self.c_stored = sem("c_stored")
        self.h_stored = sem("h_stored")
        self.setup_b = sem("setup_b")
        self.setup_bp = sem("setup_bp")
        self.b_done = sem("b_done")
        self.b_evac = sem("b_evac")
        self.hn_sq = sem("hn_sq")
        self.hn_rstd = sem("hn_rstd")
        self.hn_full = sem("hn_full")
        self.st_hi = sem("st_hi")
        self.stacked = sem("stacked")
        self.c_rows0 = sem("c_rows0")
        self.c_rows1 = sem("c_rows1")
        self.bz_tanh = sem("bz_tanh")
        self.bz_gate = sem("bz_gate")
        self.smax_done = sem("smax_done")
        self.smax = sem("smax")
        self.mcol_ready = sem("mcol_ready")
        self.m_row_done = sem("m_row_done")
        self.m_row = sem("m_row")
        self.st_done = sem("st_done")
        self.p_exp = sem("p_exp")
        self.pv_done = sem("pv_done")
        self.d_ln = sem("d_ln")
        self.d_recip = sem("d_recip")
        self.o_norm = sem("o_norm")
        self.o_gated = sem("o_gated")
        self.ob_stored = sem("ob_stored")
        self.ob_free = sem("ob_free")
        self.h_loaded0 = sem("h_loaded0")
        self.h_loaded1 = sem("h_loaded1")
        self.fin_sum = sem("fin_sum")
        self.fin_tr = sem("fin_tr")
        self.fin_evac = sem("fin_evac")
        self.fin_stored0 = sem("fin_stored0")
        self.fin_stored1 = sem("fin_stored1")


def build(nc, x, meta, rows, w_in, up, w_out, kv_w, f_bias, b_w_in, b_w_out, ident_d, masks_d, levels_d,
          causal_d, out):
    ctx = ExitStack()
    with ctx:
        def sb(name, shape, dt=F32):
            return ctx.enter_context(nc.sbuf_tensor(name, shape, dt))

        S = Signals(lambda name: ctx.enter_context(nc.semaphore(name)))

        X_LOADED, W_LOADED = (S.x_loaded0, S.x_loaded1), (S.w_loaded0, S.w_loaded1)
        O_LOADED, FIN_STORED = (S.o_loaded0, S.o_loaded1), (S.fin_stored0, S.fin_stored1)
        XT_LOADED = (S.xt_loaded0, S.xt_loaded1)
        H_LOADED, C_ROWS = (S.h_loaded0, S.h_loaded1), (S.c_rows0, S.c_rows1)

        xt_scr = nc.dram_tensor("xt_scr", (P, KO * TP), F32, kind="Internal").ap()
        oa_scr = nc.dram_tensor("oa_scr", (KO, P, TP), F32, kind="Internal").ap()
        ob_scr = nc.dram_tensor("ob_scr", (KO, P, SEQ), F32, kind="Internal").ap()
        c_scr = nc.dram_tensor("c_scr", (H, 2, TP), F32, kind="Internal").ap()

        ident = sb("ident", [P, P])
        identb = sb("identb", [P, P], BF16)
        head_ones = sb("head_ones", [P, P])
        all_ones = sb("all_ones", [P, P])
        ones_r = sb("ones_r", [P, P], F32R)
        masks = sb("masks", [P, 2 * P])
        levels = sb("levels", [P, 6 * P])
        causal = sb("causal", [P, 2 * P], BF16)
        params = sb("params", [P, NCOLS])
        pp = sb("pp", [P, NQ])
        cst = sb("cst", [P, 4])
        fb_in = sb("fb_in", [P, 1])
        EPS_RMS, EPS_GN, LN_BACK = (cst[:, i:i + 1] for i in range(3))

        xh = sb("xh", [P, KO, TP], F32R)
        xl = sb("xl", [P, KO, TP], F32R)
        wr = sb("wr", [P, 2, KO, P])
        wh = sb("wh", [P, 4, KO, P], F32R)
        wl = sb("wl", [P, 4, KO, P], F32R)
        gp = sb("gp", [P, 2])
        ARENA = 24288
        with nc.sbuf_tensor("arena", [P, ARENA], F32) as arena:
            pass
        ka = [sb(f"ka{e}", [P, TP], F32R) for e in range(2)]
        qa = [sb(f"qa{e}", [P, TP], F32R) for e in range(2)]
        kb2 = [sb(f"kb2{e}", [P, TP], F32R) for e in range(2)]
        qb2 = [sb(f"qb2{e}", [P, TP], F32R) for e in range(2)]
        qc2 = [sb(f"qc2{e}", [P, TP], F32R) for e in range(2)]
        EXTRA = slice(HD, HD + 3)
        ARENA_B = 12780
        arena_b = sb("arena_b", [P, ARENA_B])
        chi, clo = (a[:, 2:4, :, :].rearrange("p s k c -> p (s k c)")[:, 0:TP] for a in (wh, wl))
        ps = ctx.enter_context(nc.psum_tensor("ps", [P, 8, 512], F32))

        at = [0]

        def carve(n):
            at[0] += n
            assert at[0] <= ARENA, at[0]
            return arena[:, at[0] - n:at[0]]

        def carve_b(n):
            at[0] += n
            assert at[0] <= ARENA_B, at[0]
            return arena_b[:, at[0] - n:at[0]]

        h_t = carve(KO * TP).rearrange("p (k t) -> p k t", k=KO)
        sq2 = [carve(TP), carve(TP)]
        rstd = carve(TP)
        xrow = [carve(D), carve(D)]
        prow = carve(P)
        causal_f = carve(2 * P)
        at[0] = 0
        SEG_T = [(0, META + 2 * P)] + [(META + i * P, META + (i + 2) * P) for i in (2, 4, 6)]
        NSEG, SW = len(SEG_T), META + 2 * P
        reset = [carve(SW), carve(2 * P)]
        ar = carve(2 * NT * P).rearrange("p (a t) -> p a t", a=2)
        b_t, k_t, v_t = carve(3 * P), carve(3 * P), carve(3 * P)
        zz, bon, y_t = (carve(T) for _ in range(3))
        upall, lo, upf = carve(D), carve(TP), carve(P)
        st, pc = carve(P), carve(2 * NT)
        front_at = at[0]
        mut = [carve(SW + 1) for _ in range(4)]
        sq, mix, lw, cum, aa, kr, kk, rr, e_in = (carve(SW) for _ in range(9))
        gsq = carve(SW)
        tiles_at = at[0]
        rows_sb = [carve(4 * P).rearrange("p (a t) -> p a t", a=4) for _ in range(5)]
        amat = [[carve(4 * P) for _ in range(2)] for _ in range(5)]
        xs = [carve(4 * P).rearrange("p (e a t) -> p e a t", e=2, a=2) for _ in range(2)]
        pm = [carve(2 * P).rearrange("p (e t) -> p e t", e=2) for _ in range(2)]
        wu = [carve(2 * P).rearrange("p (a t) -> p a t", a=2) for _ in range(5)]
        qs = [carve(P) for _ in range(2)]
        us, sp = carve(P), carve(P)
        at[0] = tiles_at
        mut_lo = carve(TP + 1)

        at[0] = front_at
        osq = [carve(TP), carve(TP)]
        at[0] = 0
        kb, qb, zb, vb, bsq, brs, zg = (carve_b(TP) for _ in range(7))
        vflat = [carve_b(NT * P).rearrange("p (t x) -> p t x", t=NT) for _ in range(2)]
        pt = [carve_b(512) for _ in range(3)]
        dln = carve_b(512)
        ob = carve_b(SEQ)
        mcol = carve_b(KO)
        mpart = carve_b(3 * KO)
        at[0] = 6 * TP
        f_in = carve_b(TP)
        at[0] += 2 * NT * P
        f_a, f_b = carve_b(TP), carve_b(TP)
        at[0] = 0
        obq = [carve_b(SEQ), carve_b(SEQ)]
        fin = [carve_b(SEQ), carve_b(SEQ)]
        fo = [carve_b(SEQ).rearrange("p (t c) -> p t c", t=KO) for _ in range(2)]
        hres = [carve_b(SEQ), carve_b(SEQ)]

        G = [ps[:, 0:3, 0:SEG], ps[:, 3:6, 0:SEG]]

        def seg3(a):
            return a.rearrange("p (c t) -> p c t", c=3)

        def param(c, n=1):
            return params[:, c:c + n]

        def q(i):
            return pp[:, i:i + 1]

        def f32(a):
            return a.bitcast(F32)

        TILE_TOK = [META] + [P] * KO
        TILE_AT = [0] + [META + P * i for i in range(KO)]
        N_A = 1
        N_AO = N_A + 4 * KO
        N_F = N_AO + KO
        N_B = N_F + 1
        N_BO = N_B + 4 * KO
        A_ORDER = [Q_MUK, Q_MUV, Q_MUR, Q_MUZ]
        UNITS = [(qb_, kt) for qb_ in range(2) for kt in range(4 * qb_ + 5)]
        NU = len(UNITS)

        def unit(w):
            qb_, kt = UNITS[w]
            q0 = max(qb_ * 512, kt * P - META)
            n_q = qb_ * 512 + 512 - q0
            off = META + q0 - kt * P
            return min(P, T - kt * P), q0, n_q, off, max(0, min(P - off, n_q))

        KSEG = [(t, i, 512 * i, min(512 * i + 512, META + (t + 1) * P)) for t in range(KO)
                for i in range(-(-(META + (t + 1) * P) // 512))]
        NS = len(KSEG)
        L_VROW1, L_K, L_SK, L_Q, L_SQ, L_V, L_VROW0, L_Z = 0, 2, 5, 8, 11, 14, 17, 19
        NCH = 22
        B_G, B_SM, B_ST, B_PV = (0, 1), (2, 3), (4, 5), (6, 7)

        def chunk(p, local):
            return NCH * p + NCH - 2 + local

        def order(e, more):
            at_ = [[] for _ in range(NU)]
            if more and e == 0:
                for i in range(3):
                    at_[i] += [("proj", 0, i)]
                    at_[4 + i] += [("proj", 1, i)]
                at_[3] += [("sumsq", 0, i) for i in range(3)]
                at_[5] += [("norm", 0)]
                at_[8] += [("sumsq", 1, i) for i in range(3)]
                at_[10] += [("norm", 1)]
            if more and e == 1:
                for i in range(3):
                    at_[i] += [("proj", 2, i)]
                    at_[5 + i] += [("proj", 3, i)]
                at_[4] += [("vrow", 0, i) for i in range(2)]
                at_[0] += [("stack", 0)]
            if e == 0:
                at_[0] = [("stack", 1)] + at_[0]
                at_[10] += [("gate",)]
            if more and e == 1:
                at_[9] += [("wsplit",)]
            if not more:
                for i in range(4 - e):
                    at_[(6 if e == 0 else 2) + 2 * i] += [("orow", 4 * e + i)]
                if e == 0:
                    at_[3] += [("wsplit",)]
            if e == 0 or more:
                for i in range(NS):
                    at_[2 + e + i * 9 // NS] += [("smax", 1 - e, i)]
                at_[12] += [("maxrow", 1 - e)]
            if e == 0:
                steps = [("vrow", 1, 0), ("scores", e, 0), ("vrow", 1, 1), ("scores", e, 1)]
            else:
                steps = [("scores", e, 0), ("scores", e, 1)]
            for w in range(NU):
                steps += at_[w] + [("weighted", e, w)]
                if w + 2 < NU:
                    steps += [("scores", e, w + 2)]
            return steps

        def first_round():
            return ([("proj", 0, i) for i in range(3)] + [("sumsq", 0, i) for i in range(3)] + [("norm", 0)]
                    + [("proj", 1, i) for i in range(3)] + [("sumsq", 1, i) for i in range(3)] + [("norm", 1)]
                    + [("stack", 0)] + [("proj", 2, i) for i in range(3)] + [("vrow", 0, i) for i in range(2)]
                    + [("smax", 0, i) for i in range(5)] + [("proj", 3, i) for i in range(3)]
                    + [("smax", 0, i) for i in range(5, NS)] + [("maxrow", 0)])


        GROUPS = [[0]] + [[u, u + 1] for u in range(1, NT, 2)]
        NG = len(GROUPS)
        LEVELS = [4] + [6] * (NG - 1)
        STEPS = LEVELS[0] + 12 * (NG - 1)
        B_US, B_Y, B_P, B_X, B_GA = 0, 1, (2, 3), (4, 5), (6, 7)
        ROUNDS = [[0, 1], [2], [3], [4]]
        TILES_IN = [sum((GROUPS[g] for g in r), []) for r in ROUNDS]
        AFTER_A = 3 * 4 * KO

        def step(g, l, j):
            return l if g == 0 else LEVELS[0] + 12 * (g - 1) + 2 * l + j

        def ring(u):
            s_ = 0 if u < 3 else (u - 1) // 2
            return 3 * (s_ % 2) + u - TILES_IN[s_][0]

        def local_cols(u):
            s_ = 0 if u < 3 else (u - 1) // 2
            c0 = (u - TILES_IN[s_][0] + (1 if s_ else 0)) * P
            return slice(c0, c0 + P)

        def tiles_before(p, s_):
            return NT * p + TILES_IN[s_][0]

        AT_LATER = [0, 1, 2, 3, 4, 5, 6, 7, 8, 9, 10, 12, 11, 13, 14, 15]
        AT_FIRST = [-12, -10, -8, -6, -4, -2, 2, 4, 5, 6, 8, 12, 10, 13, 14, 15]
        PARTS = ((0, 3), (3, 6), (6, KO))
        FRONT = ([("low",)] + [("k", i) for i in range(3)] + [("v", i) for i in range(3)] + [("r", 0), ("kks",)]
                 + [("r", 1), ("r", 2), ("bsum",)] + [("z", i) for i in range(3)] + [("zgate",)])

        def round_order(s_, chain, front, weights):
            body, places = [], 0
            for g in ROUNDS[s_]:
                for kind in ([("rows", g), None, ("amat", g), None]
                             + sum(([("p", g, l), None, ("x", g, l), None] for l in range(LEVELS[g])), [])
                             + [("q", g), None, ("w", g), None]):
                    body.append(kind)
                    places += kind is None
            fill = [[] for _ in range(places)]
            start = places - 16
            if chain:
                prev = TILES_IN[s_ - 1]
                slots = [("chain", u, i) for u in prev for i in range(5)]
                for i, c in enumerate(slots):
                    fill[i * (9 if s_ else 12) // len(slots)].append(c)
            if front:
                at_ = AT_LATER
                if s_ == 0:
                    at_ = AT_FIRST
                for a, c in zip(at_, FRONT):
                    fill[start + a].append(c)
                if weights and s_ == 3:
                    fill[0] = [("scale", 2), ("scale", 3)] + fill[0]
                    fill[5] += [("split", 2)]
                    fill[8] += [("split", 3)]
                if weights and s_ == 1:
                    fill[3] += [("scale", 0), ("scale", 1)]
                if weights and s_ == 2:
                    fill[7] += [("split", 0)]
                    fill[10] += [("split", 1)]
            if chain:
                fill[places - 7].append(("gn1",))
                fill[places - 5].append(("gn2",))
                fill[places - 3].append(("gn3",))
            steps, i = [], 0
            for b in body:
                if b is None:
                    steps += fill[i]
                    i += 1
                else:
                    steps.append(b)
            return steps

        def last_round_order():
            steps = []
            for st_ in round_order(NSEG - 1, True, False, False):
                steps.append(st_)
                if st_[0] in ("x", "w"):
                    steps.append(("orow", 6 if st_[0] == "w" else st_[2]))
            return steps

        def tail_order():
            return [("chain", u, i) for u in TILES_IN[3] for i in range(5)] + [("gn1",), ("gn2",), ("gn3",)]

        block = ctx.enter_context(nc.Block())

        @block.sync
        def _(sp_):
            sync = sp_
            for dst, src in ((ident[:, :], ident_d), (masks[:, :], masks_d), (levels[:, :], levels_d),
                             (causal_f, causal_d), (fb_in[0:H, :], f_bias)):
                sync.dma_start(dst, src).then_inc(S.consts_loaded, 16)
            sync.dma_start(prow[0:NROWS, :], rows).then_inc(S.rows_loaded, 16)
            sync.dma_start(xrow[0][0:META, :], meta).then_inc(X_LOADED[0], 16)
            for t in range(1, NT):
                if t >= 2:
                    sync.wait_ge(S.x_tr, t - 1)
                sync.dma_start(xrow[t % 2][:, :], x[(t - 1) * P:t * P, :]).then_inc(X_LOADED[t % 2], 16)

            def load_w(n, src, slot, wait):
                if wait is not None:
                    sync.wait_ge(S.w_lo, wait)
                    if not isinstance(wait, int):
                        sync.sem_inc(S.w_asked, 1)
                sync.dma_start(wr[:, slot, :, 0:src.shape[2]], src).then_inc(W_LOADED[slot], 16)

            wi = w_in.rearrange("(k p) n -> p k n", p=P)
            kvw = kv_w.rearrange("(k p) n -> p k n", p=P)
            bw = b_w_in.rearrange("(k p) n -> p k n", p=P)
            load_w(0, wi[:, :, 4 * D:4 * D + P], 0, None)
            with sync.Fori(0, KO) as p:
                cols = [sync.snap(p * P + base) for base in (D, 2 * D, 0, 3 * D)]
                for j, col in enumerate(cols):
                    load_w(None, wi[:, :, bass.ds(col, P)], (N_A + j) % 2, 4 * p + N_A + j)
            wo = w_out.rearrange("(k p) n -> p k n", p=P)
            for n in (N_AO, N_AO + 1):
                load_w(n, wo[:, :, (n - N_AO) * P:(n - N_AO + 1) * P], n % 2, n)
            sync.wait_ge(S.z_gate, NSEG * KO)
            sync.wait_ge(S.b_tilde, NSEG * KO)
            for k in range(KO):
                sync.wait_ge(S.out_free, NSEG * (k + 2))
                if k >= 2:
                    sync.wait_ge(S.x_lo, KO + k - 1)
                sync.dma_start(osq[k % 2][:, 0:T], oa_scr[k][:, 0:T]).then_inc(O_LOADED[k % 2], 16)
            for m in range(KO):
                if m >= 2:
                    sync.wait_ge(XT_LOADED[m % 2], 16 * (m // 2))
                sync.dma_start(h_t[:, m, :], xt_scr[:, m * TP:(m + 1) * TP]).then_inc(XT_LOADED[m % 2], 16)
            for m in range(2, KO):
                load_w(N_AO + m, wo[:, :, m * P:(m + 1) * P], (N_AO + m) % 2, N_AO + m)
            load_w(N_F, kvw[:, :, 2 * D:2 * D + H], N_F % 2, N_F)
            with sync.Fori(0, KO) as p:
                cols = [sync.snap(p * P + base) for base in (0, D)]
                for j, (w, col) in enumerate(((kvw, cols[0]), (bw, cols[0]), (kvw, cols[1]), (bw, cols[1]))):
                    load_w(None, w[:, :, bass.ds(col, P)], (N_B + j) % 2, 4 * p + N_B + j)
            bwo = b_w_out.rearrange("(k p) n -> p k n", p=P)
            for k in range(2):
                load_w(N_BO + k, bwo[:, :, k * P:(k + 1) * P], (N_BO + k) % 2, N_BO + k)
            sync.wait_ge(S.stacked, 10 * KO)
            for k in range(KO):
                sync.wait_ge(S.ob_free, k + 2)
                if k >= 2:
                    sync.wait_ge(S.x_lo, 3 * KO + k - 1)
                sync.dma_start(obq[k % 2], ob_scr[k]).then_inc(O_LOADED[k % 2], 16)
            out_v = out.rearrange("(t p) c -> p t c", p=P)

            def load_h(m):
                if m >= 2:
                    sync.wait_ge(S.fin_sum, m - 1)
                sync.dma_start(hres[m % 2], xt_scr[:, m * TP + META:m * TP + T]).then_inc(H_LOADED[m % 2], 16)

            load_h(0)
            load_h(1)
            for m in range(KO):
                if m + 2 < KO:
                    n = N_BO + m + 2
                    load_w(n, bwo[:, :, (m + 2) * P:(m + 3) * P], n % 2, n)
                    load_h(m + 2)
                sync.wait_ge(S.fin_evac, m + 1)
                sync.dma_start(out_v[:, :, m * P:(m + 1) * P], fo[m % 2]).then_inc(FIN_STORED[m % 2], 16)
            for i in range(2):
                sync.wait_ge(FIN_STORED[i], 16 * KO // 2)
            sync.wait_ge(S.c_stored, 16)

        @block.gpsimd
        def _(pool):
            pool.memset(f32(ones_r[:, :]), 1.0).then_inc(S.setup_pool, 1)
            pool.memset(head_ones[:, :], 0.0).then_inc(S.setup_pool, 1)
            pool.wait_ge(S.setup_pool, 2)
            for e in range(2):
                b = slice(e * HD, (e + 1) * HD)
                pool.memset(head_ones[b, b], 1.0).then_inc(S.setup_pool, 1)
            pool.wait_ge(S.setup_pool, 4)
            pool.wait_ge(S.x_evac, NT)
            pool.wait_ge(S.pads_zero, 1)
            pool.dma_start(xt_scr, h_t.rearrange("p k t -> p (k t)")).then_inc(S.xt_stored, 16)

            def scale_w(slot, gain, loaded, width=P):
                pool.wait_ge(W_LOADED[slot], loaded)
                pool.tensor_tensor(wr[:, slot, :, 0:width], wr[:, slot, :, 0:width],
                                   param(gain, KO).unsqueeze(2).to_broadcast([P, KO, width]),
                                   ALU.mult).then_inc(S.w_scaled, 1)

            pool.wait_ge(S.param_derived, 4)
            scale_w(0, C_AN, 16)
            def scale_a(q_, j):
                scale_w((N_A + j) % 2, C_AN, 32 * q_ + 16 * ((N_A + j) // 2 + 1))

            def round_pool(p, s_, steps):
                F = NSEG * p + s_ + 1
                s1 = (s_ + 1) % NSEG
                t0, t1 = SEG_T[s1]
                n = t1 - t0
                dst = slice(3 * P - n, 3 * P)
                for st_ in steps:
                    kind = st_[0]
                    if kind in ("k", "v", "r", "z") and st_[1] < 2:
                        continue
                    if kind == "scale":
                        scale_a(p + 1, st_[1])
                    elif kind == "low":
                        pool.wait_ge(S.cumlog, F + 1)
                        pool.tensor_tensor(lw[:, 0:n], cum[:, 0:n], lw[:, 0:n], ALU.subtract).then_inc(S.cum_before, 1)
                    elif kind == "v":
                        pool.wait_ge(S.k_mix, F + 1)
                        pool.wait_ge(S.shifted, 4 * F + 2)
                        pool.wait_ge(S.kk_raw, F + 1)
                        pool.tensor_tensor(kr[:, 0:n], kr[:, 0:n], mix[:, 0:n], ALU.mult).then_inc(S.k_new, 1)
                        pool.wait_ge(S.exp_neg, F + 1)
                        pool.wait_ge(S.k_new, F + 1)
                        if not (isinstance(F, int) and F == 0):
                            pool.wait_ge(S.a_done, 2 * tiles_before(p + (s1 == 0), s1))
                        pool.tensor_tensor(k_t[:, dst], kr[:, 0:n], cum[:, 0:n], ALU.mult).then_inc(S.k_tilde, 1)
                    elif kind == "r":
                        pool.wait_ge(S.kk_norm, F + 1)
                        pool.wait_ge(S.kk_sumsq, F + 1)
                        pool.tensor_tensor(sq[:, 0:n], kk[:, 0:n], aa[:, 0:n], ALU.mult).then_inc(S.kk_a, 1)
                        pool.wait_ge(S.kk_a, F + 1)
                        pool.tensor_tensor(b_t[:, dst], sq[:, 0:n], cum[:, 0:n], ALU.mult).then_inc(S.b_tilde, 1)
                    elif kind == "gn3":
                        i = NSEG * p + s_ - 1
                        sg = (s_ - 1) % NSEG
                        g0, g1 = SEG_T[sg]
                        pool.wait_ge(S.out_ready, i + 1 + NSEG)
                        pair = p - 1 if s_ == 0 or s_ == NSEG else p
                        dst_ = oa_scr[pair] if isinstance(p, int) else \
                            oa_scr[bass.ds(pair, 1)].rearrange("a p t -> (a p) t")
                        pool.dma_start(dst_[:, g0:g1], y_t[:, g0:g1]).then_inc(S.out_stored, 16)
                        pool.wait_ge(S.out_stored, 16 * i + 16)
                        pool.sem_inc(S.out_free, 1)

            for j in range(4):
                scale_a(0, j)
            pool.wait_ge(S.xt_stored, 16)
            pool.wait_ge(S.x_lo, KO)
            pool.wait_ge(S.shifted, 1)
            pool.sem_inc(S.out_free, NSEG)

            round_pool(0, -1, FRONT)
            round_pool(0, 0, round_order(0, False, True, False))
            with pool.Fori(0, KO - 1) as p:
                for s_ in range(1, NSEG):
                    round_pool(p, s_, round_order(s_, True, True, True))
                round_pool(p + 1, 0, round_order(0, True, True, True))
            for s_ in range(1, NSEG - 1):
                round_pool(KO - 1, s_, round_order(s_, True, True, False))
            round_pool(KO - 1, NSEG - 1, last_round_order())
            round_pool(KO, 0, tail_order())
            scale_w(N_F % 2, C_KVN, 16 * (N_F // 2 + 1), H)
            pool.wait_ge(S.res_added, KO)
            pool.dma_start(xt_scr, h_t.rearrange("p k t -> p (k t)")).then_inc(S.h_stored, 16)
            def scale_b(q_, j):
                scale_w((N_B + j) % 2, (C_KVN, C_BN)[j % 2], 32 * q_ + 16 * ((N_B + j) // 2 + 1))

            scale_b(0, 0)
            scale_b(0, 1)
            pool.wait_ge(S.c_lo, 1)
            pool.dma_start(c_scr[:, 0, :], f32(chi[0:H, :])).then_inc(S.c_stored, 16)
            pool.wait_ge(S.c_stored, 16)
            pool.dma_start(c_scr[:, 1, :], f32(clo[0:H, :])).then_inc(S.c_stored, 16)
            pool.wait_ge(S.h_stored, 16)
            pool.wait_ge(S.x_lo, 3 * KO)
            pool.wait_ge(S.w_scaled, N_AO + 3)
            for e in range(2):
                for a in (kb2[e], qb2[e], qc2[e]):
                    pool.memset(f32(a[EXTRA, :]), 1.0).then_inc(S.setup_bp, 1)
            pool.wait_ge(S.setup_bp, 6)
            for e in range(2):
                pool.memset(f32(qc2[e][HD:HD + 1, :]), 0.0).then_inc(S.setup_bp, 1)
            pool.wait_ge(S.setup_bp, 8)
            pool.wait_ge(S.c_stored, 32)
            pool.sem_inc(S.ob_free, 1)

            def store_ob(p, dst):
                pool.wait_ge(S.o_gated, p + 2)
                pool.dma_start(dst, ob).then_inc(S.ob_stored, 16)
                pool.wait_ge(S.ob_stored, 16 * p + 16)
                pool.sem_inc(S.ob_free, 1)

            for j in range(2, 4):
                scale_b(0, j)
            scale_b(1, 0)
            with pool.Fori(0, KO - 2) as p:
                for j in range(1, 4):
                    scale_b(p + 1, j)
                scale_b(p + 2, 0)
                store_ob(p, ob_scr[bass.ds(p, 1)].rearrange("a p t -> (a p) t"))
            for j in range(1, 4):
                scale_b(KO - 1, j)
            pool.wait_ge(W_LOADED[N_BO % 2], 16 * (N_BO // 2 + 1))
            pool.wait_ge(S.w_scaled, N_AO + 1 + 4 * KO)
            pool.sem_inc(S.w_scaled, 1)
            store_ob(KO - 2, ob_scr[KO - 2])
            store_ob(KO - 1, ob_scr[KO - 1])

        @block.scalar
        def _(act):
            def split_hi(slot, loaded, scaled, hi_free, width=P, slot_hi=None):
                if scaled is None:
                    act.wait_ge(W_LOADED[slot], loaded)
                else:
                    act.wait_ge(S.w_scaled, scaled)
                if hi_free is not None:
                    act.wait_ge(S.proj_done, hi_free + AFTER_A)
                act.activation(wh[:, slot if slot_hi is None else slot_hi, :, 0:width], wr[:, slot, :, 0:width], ACT.Copy).then_inc(S.w_hi, 1)

            def normalise(r):
                if r == 0:
                    for k in range(KO):
                        if k >= 2:
                            act.wait_ge(S.h_sumsq, k - 1)
                        act.wait_ge(S.x_evac, NT)
                        act.wait_ge(S.pads_zero, 1)
                        act.activation(sq2[k % 2], h_t[:, k, :], ACT.Square).then_inc(S.h_sq, 1)
                    split_hi(0, None, 1, None, slot_hi=3)
                act.wait_ge(S.h_sumsq, KO + r)
                act.wait_ge(S.setup_dve, 3)
                act.activation(seg3(rstd), G[0], ACT.Ln, scale=1.0 / D, bias=EPS_RMS).then_inc(S.h_ln, 1)
                act.wait_ge(S.h_ln, r + 1)
                act.activation(rstd, rstd, ACT.Exp, scale=-0.5).then_inc(S.h_rstd, 1)
                for k in range(KO):
                    act.wait_ge(S.xn_mul, KO * r + k + 1)
                    act.activation(xh[:, k, :], sq2[k % 2], ACT.Copy).then_inc(S.x_hi, 1)

            def split_a(q_, j, after):
                act.wait_ge(S.w_scaled, 4 * q_ + j + 2)
                if after is not None:
                    act.wait_ge(S.proj_done, after)
                act.activation(wh[:, j, :, :], wr[:, (N_A + j) % 2, :, :], ACT.Copy).then_inc(S.w_hi, 1)

            normalise(0)
            for j in range(2):
                split_a(0, j, None)
            act.wait_ge(S.xt_stored, 16)
            act.wait_ge(S.x_lo, KO)
            act.dma_start(upall, up).then_inc(S.up_loaded, 16)
            act.wait_ge(S.proj_done, 1)
            act.activation(seg3(mut_lo[:, 1:]), G[0], ACT.Copy, scale=param(C_LORA)).then_inc(S.mu_done, 1)
            act.wait_ge(S.shifted, 1)
            act.activation(lo[0:LORA, :], lo[0:LORA, :], ACT.Tanh).then_inc(S.lora_tanh, 1)

            def split_row(r, k):
                act.wait_ge(O_LOADED[k % 2], 16 * (KO // 2 * (r // 2) + k // 2 + 1))
                src = osq[k % 2] if r == 1 else obq[k % 2]
                act.activation(xh[:, k, 0:src.shape[1]], src, ACT.Copy).then_inc(S.x_hi, 1)

            def round_act_a(p, s_, steps):
                F = NSEG * p + s_ + 1
                begin = isinstance(F, int) and F == 0
                s1 = (s_ + 1) % NSEG
                q_ = p + 1 if s_ == NSEG - 1 else p
                t0, t1 = SEG_T[s1]
                n = t1 - t0
                n_prev = (P * 2, SW, P * 2, P * 2)[s1]

                def mu(j, name):
                    act.wait_ge(S.proj_done, 4 * F + j + 2)
                    if not begin:
                        act.wait_ge(S.shifted, 4 * F - 4 + j + 2)
                        act.wait_ge(S.mu_done, 4 * F - 4 + j + 2)
                    act.activation(mut[j][:, 0:1], mut[j][:, n_prev:n_prev + 1] if s1 else cst[:, 3:4], ACT.Copy)\
                        .then_inc(S.carried, 1)
                    act.wait_ge(S.carried, 4 * F + j + 1)
                    act.activation(mut[j][:, 1:n + 1], ps[:, B_GA[(0, 1, 0, 0)[j]], 0:n], ACT.Copy, scale=q(name))\
                        .then_inc(S.mu_done, 1)

                for st_ in steps:
                    kind = st_[0]
                    if kind in ("k", "v", "r", "z") and st_[1] < 2:
                        continue
                    if kind == "orow":
                        split_row(1, st_[1])
                    elif kind == "split":
                        split_a(p + 1, st_[1], 4 * (NSEG * p + 3) + st_[1] + 2)
                    elif kind == "low":
                        act.wait_ge(S.pair_params, q_ + 1)
                        if s1 == 0:
                            act.wait_ge(S.up_loaded, 16)
                            if not begin:
                                act.wait_ge(S.icl_done, F)
                            src = upall[:, q_ * P:(q_ + 1) * P] if isinstance(q_, int) else upall[:, bass.ds(q_ * P, P)]
                            act.activation(upf, src, ACT.Copy).then_inc(S.up_copied, 1)
                        act.wait_ge(S.dec_done, F + 1)
                        if not begin:
                            act.wait_ge(S.a_tilde, F)
                        act.activation(lw[:, 0:n], ps[:, B_GA[0], 0:n], ACT.Tanh, scale=0.5, bias=q(Q_HDB))\
                            .then_inc(S.dec_tanh, 1)
                        act.wait_ge(S.icl_done, F + 1)
                        if not begin:
                            act.wait_ge(S.kk_a, F)
                        act.activation(aa[:, 0:n], ps[:, B_GA[1], 0:n], ACT.Tanh, scale=0.5, bias=q(Q_HIB))\
                            .then_inc(S.icl_tanh, 1)
                    elif kind == "k":
                        mu(0, Q_MUK)
                    elif kind == "v":
                        act.wait_ge(S.shifted, 4 * F + 2)
                        act.activation(kk[:, 0:n], kr[:, 0:n], ACT.Copy, scale=q(Q_KK)).then_inc(S.kk_raw, 1)
                        act.wait_ge(S.iclr, F + 1)
                        if not begin:
                            act.wait_ge(S.z_gate, F)
                        act.activation(mix[:, 0:n], aa[:, 0:n], ACT.Identity, scale=q(Q_KA), bias=q(Q_NKA))\
                            .then_inc(S.k_mix, 1)
                        act.wait_ge(S.kk_raw, F + 1)
                        if not begin:
                            act.wait_ge(S.b_tilde, F)
                        act.activation(sq[:, 0:n], kk[:, 0:n], ACT.Square).then_inc(S.kk_sq, 1)
                        act.wait_ge(S.cumlog, F + 1)
                        if not begin:
                            act.wait_ge(S.r_tilde, F)
                        act.activation(e_in[:, 0:n], cum[:, 0:n], ACT.Exp).then_inc(S.exp_in, 1)
                        act.wait_ge(S.cum_before, F + 1)
                        act.activation(cum[:, 0:n], cum[:, 0:n], ACT.Exp, scale=-1.0).then_inc(S.exp_neg, 1)
                        act.activation(lw[:, 0:n], lw[:, 0:n], ACT.Exp).then_inc(S.exp_before, 1)
                        mu(1, Q_MUV)
                    elif kind == "r":
                        mu(2, Q_MUR)
                    elif kind == "kks":
                        act.wait_ge(S.kk_guard, F + 1)
                        act.activation(bon[:, t0:t1], bon[:, t0:t1], ACT.Ln, scale=LN_SCALE).then_inc(S.kk_ln, 1)
                        act.wait_ge(S.kk_ln, F + 1)
                        act.activation(bon[:, t0:t1], bon[:, t0:t1], ACT.Exp, scale=-0.5, bias=LN_BACK)\
                            .then_inc(S.kk_rn, 1)
                    elif kind == "z":
                        mu(3, Q_MUZ)
                    elif kind == "zgate":
                        act.wait_ge(S.shifted, 4 * F + 5)
                        act.wait_ge(S.bonus_sum, F + 1)
                        act.activation(mix[:, 0:n], zz[:, t0:t1], ACT.Tanh, scale=0.5).then_inc(S.z_tanh, 1)
                    elif kind == "rows":
                        for j, u in enumerate(GROUPS[st_[1]]):
                            act.wait_ge(S.tr_done, 9 * p + u + 1)
                            act.activation(rows_sb[ring(u)].rearrange("p a t -> p (a t)"), ps[:, B_X[j], :], ACT.Copy)\
                                .then_inc(S.rows_ready, 1)
                    elif kind == "x":
                        g, l = st_[1:]
                        for j, u in enumerate(GROUPS[g]):
                            act.wait_ge(S.x_done, STEPS * p + step(g, l, j) + 1)
                            bank = ps[:, B_X[j], :].rearrange("p (e a t) -> p e a t", e=2, a=2)
                            if 0 < l < LEVELS[g] - 1:
                                act.activation(xs[j], bank, ACT.Copy).then_inc(S.x_copied, 1)
                            else:
                                act.activation(xs[j][:, :, 1, :], bank[:, :, 1, :], ACT.Copy).then_inc(S.x_copied, 1)
                    elif kind == "q":
                        for j, u in enumerate(GROUPS[st_[1]]):
                            act.wait_ge(S.q_done, 9 * p + u + 1)
                            act.activation(qs[j], ps[:, B_P[j], 0:P], ACT.Copy).then_inc(S.q_copied, 1)
                    elif kind == "chain":
                        u, i = st_[1:]
                        pp_ = p - 1 if s_ == 0 else p
                        if i in (0, 2):
                            c = 2 * u + i // 2
                            if c == 0:
                                act.wait_ge(S.state_zero, pp_ + 1)
                            else:
                                act.wait_ge(S.s_ready, 36 * pp_ + 2 * c)
                            act.activation(sp, st, ACT.Copy, scale=pc[:, c:c + 1]).then_inc(S.s_scaled, 1)
                        if i == 4:
                            act.wait_ge(S.y_done, 9 * pp_ + u + 1)
                            act.wait_ge(S.out_free, NSEG * pp_ + (s_ - 1) % NSEG + 1)
                            lo_, n_ = (OFF, META) if u == 0 else (0, P)
                            act.activation(y_t[:, TILE_AT[u]:TILE_AT[u] + n_], ps[:, B_Y, lo_:P], ACT.Copy)\
                                .then_inc(S.y_copied, 1)
                    elif kind == "gn1":
                        i = NSEG * p + s_ - 1
                        g0, g1 = SEG_T[(s_ - 1) % NSEG]
                        act.wait_ge(S.gn_centred, i + 2)
                        act.wait_ge(S.gn_scaled, i + 1)
                        act.activation(gsq[:, 0:g1 - g0], y_t[:, g0:g1], ACT.Square).then_inc(S.gn_sq, 1)
                    elif kind == "gn2":
                        i = NSEG * p + s_ - 1
                        g0, g1 = SEG_T[(s_ - 1) % NSEG]
                        act.wait_ge(S.gn_var, i + 1)
                        act.activation(gsq[:, 0:g1 - g0], ps[:, B_GA[1], 0:g1 - g0], ACT.Ln, scale=1.0 / HD, bias=EPS_GN)\
                            .then_inc(S.gn_ln, 1)
                        act.wait_ge(S.gn_ln, i + 2)
                        act.activation(gsq[:, 0:g1 - g0], gsq[:, 0:g1 - g0], ACT.Exp, scale=-0.5).then_inc(S.gn_rstd, 1)

            act.sem_inc(S.gn_ln, 1)
            for j in range(2, 4):
                split_a(0, j, None)
            act.wait_ge(S.setup_dve, 18)
            round_act_a(0, -1, FRONT)
            round_act_a(0, 0, round_order(0, False, True, False))
            with act.Fori(0, KO - 1) as p:
                for s_ in range(1, NSEG):
                    round_act_a(p, s_, round_order(s_, True, True, True))
                round_act_a(p + 1, 0, round_order(0, True, True, True))
            for s_ in range(1, NSEG - 1):
                round_act_a(KO - 1, s_, round_order(s_, True, True, False))
            for n in (N_AO, N_AO + 1):
                split_hi(n % 2, 16 * (n // 2 + 1), None, N_AO)
            act.wait_ge(S.setup_dve, 20)
            round_act_a(KO - 1, NSEG - 1, last_round_order())
            round_act_a(KO, 0, tail_order())

            split_row(1, KO - 1)
            for m in range(KO):
                n = N_AO + m + 2
                if m < KO - 2:
                    split_hi(n % 2, 16 * (n // 2 + 1), None, n - 1)
                act.wait_ge(S.res_added, m + 1)
                if m >= 3:
                    act.wait_ge(S.h_acc, m - 2)
                act.activation(sq2[m % 2] if m else rstd, h_t[:, m, :], ACT.Square).then_inc(S.h_sq, 1)
            n = N_F
            split_hi(n % 2, None, N_AO + 1, n - 1, H)
            normalise(1)
            split_hi((N_B + 0) % 2, None, N_AO + 2, N_B - 2)
            act.wait_ge(S.f_logit, 1)
            act.activation(f_a[0:H, :], f_in[0:H, :], ACT.Abs).then_inc(S.f_abs, 1)
            act.wait_ge(S.f_abs, 1)
            act.activation(f_a[0:H, :], f_a[0:H, :], ACT.Exp, scale=-1.0).then_inc(S.f_exp, 1)
            act.wait_ge(S.f_exp, 1)
            act.activation(f_a[0:H, :], f_a[0:H, :], ACT.Ln, bias=1.0).then_inc(S.f_ln, 1)
            act.wait_ge(S.c_scaled, 1)
            act.activation(chi[0:H, :], f_b[0:H, :], ACT.Copy).then_inc(S.c_hi, 1)

            def split_b(p, j):
                act.wait_ge(S.w_scaled, 4 * p + N_AO + 6 + j)
                act.wait_ge(S.b_done, NCH * p + (15, 20, 25, 31)[j])
                act.activation(wh[:, (N_B + j) % 2, :, :], wr[:, (N_B + j) % 2, :, :], ACT.Copy).then_inc(S.w_hi, 1)

            def round_act(p, steps, c_next):
                first = isinstance(p, int) and p < 0
                for st_ in steps:
                    kind = st_[0]
                    if kind == "wsplit":
                        if isinstance(p, int):
                            act.wait_ge(W_LOADED[(N_BO + 1) % 2], 16 * ((N_BO + 1) // 2 + 1))
                            act.wait_ge(S.b_done, NCH * KO - 2)
                            act.activation(wh[:, (N_BO + 1) % 2, :, :], wr[:, (N_BO + 1) % 2, :, :], ACT.Copy)\
                                .then_inc(S.w_hi, 1)
                        else:
                            split_b(p + 1, 0)
                    elif kind == "orow":
                        if st_[1] == 0:
                            act.wait_ge(S.b_done, NCH * KO - 2)
                        split_row(3, st_[1])
                    elif kind == "proj":
                        j, i = st_[1:]
                        n_ = chunk(p, (L_K, L_Q, L_V, L_Z)[j] + i)
                        if i == 0 and j < 3:
                            if first and j == 0:
                                split_hi((N_B + 1) % 2, None, N_AO + 3, N_B)
                            else:
                                split_b(p, j + 1)
                        act.wait_ge(S.b_done, n_ + 1)
                        if i == 0 and not first:
                            if j < 2:
                                act.wait_ge(S.stacked, 10 * p + 10)
                            elif j == 3:
                                act.wait_ge(S.bz_gate, p + 1)
                        act.activation((kb, qb, vb, zb)[j][:, i * SEG:(i + 1) * SEG], ps[:, B_G[(i + (L_K, L_Q, L_V, L_Z)[j]) % 2], 0:SEG],
                                       ACT.Copy).then_inc(S.b_evac, 1)
                        if i == 2 and j < 2:
                            act.wait_ge(S.b_evac, n_ + 1)
                            if j:
                                act.wait_ge(S.b_done, chunk(p, L_SK) + 3)
                            act.activation(bsq, (kb, qb)[j], ACT.Square).then_inc(S.hn_sq, 1)
                    elif kind == "sumsq":
                        j, i = st_[1:]
                        local = (L_SK, L_SQ)[j] + i
                        n_ = chunk(p, local)
                        act.wait_ge(S.b_done, n_ + 1)
                        if i == 0 and not (first and j == 0):
                            act.wait_ge(S.hn_full, 2 * p + 2 + j)
                        act.activation(brs[:, i * SEG:(i + 1) * SEG], ps[:, B_G[local % 2], 0:SEG], ACT.Ln,
                                       scale=1.0 / HD, bias=EPS_RMS).then_inc(S.b_evac, 1)
                        if i == 2:
                            act.wait_ge(S.b_evac, n_ + 1)
                            act.activation(brs, brs, ACT.Exp, scale=-0.5).then_inc(S.hn_rstd, 1)
                    elif kind == "stack":
                        e = st_[1]
                        q_ = p + 1 - e
                        d = slice(e * HD, (e + 1) * HD)
                        if first:
                            act.wait_ge(S.setup_bp, 8)
                            act.wait_ge(S.c_stored, 32)
                        act.dma_start(f32(kb2[e][HD + 1:HD + 3, :]), c_next[e]).then_inc(C_ROWS[e], 16)
                        act.wait_ge(S.hn_full, 2 * q_ + 1)
                        act.activation(ka[e][d, :], kb[d, :], ACT.Copy).then_inc(S.st_hi, 1)
                        act.wait_ge(S.hn_full, 2 * q_ + 2)
                        act.activation(qa[e][d, :], qb[d, :], ACT.Copy).then_inc(S.st_hi, 1)
                    elif kind == "vrow":
                        e, i = st_[1:]
                        local = (L_VROW0, L_VROW1)[e] + i
                        act.wait_ge(S.b_done, chunk(p, local) + 1)
                        c = slice(e * HD, (e + 1) * HD)
                        bank = ps[:, B_G[local % 2], :]
                        if i == 0:
                            act.activation(vflat[e][:, 0:7, c], bank[:, 0:7 * HD].rearrange("p (t c) -> p t c", c=HD),
                                           ACT.Copy).then_inc(S.b_evac, 1)
                        else:
                            act.activation(vflat[e][:, 7, c], bank[:, 0:HD], ACT.Copy)
                            act.activation(vflat[e][0:META, 8, c], bank[0:META, HD:2 * HD], ACT.Copy)\
                                .then_inc(S.b_evac, 1)
                    elif kind == "gate":
                        act.wait_ge(S.o_gated, p + 1)
                        act.wait_ge(S.b_evac, chunk(p - 1, L_Z) + 3)
                        act.activation(zg, zb, ACT.Tanh, scale=0.5).then_inc(S.bz_tanh, 1)
                    elif kind == "maxrow":
                        e = st_[1]
                        q_ = p + 1 - e
                        for a in range(2):
                            act.wait_ge(S.m_row_done, 4 * q_ + 2 * e + a + 1)
                            act.activation(qb2[e][HD:HD + 1, META + a * 512:META + (a + 1) * 512], ps[0:1, B_SM[a], :],
                                           ACT.Copy, scale=-1.0).then_inc(S.m_row, 1)
                    elif kind == "scores":
                        e, w = st_[1:]
                        n_k, q0, n_q, _, _ = unit(w)
                        base = 2 * NU * p + NU * e + w
                        act.wait_ge(S.st_done, base + 1)
                        if w >= 3:
                            act.wait_ge(S.pv_done, base - 2)
                        act.activation(pt[w % 3][0:n_k, 0:n_q], ps[0:n_k, B_ST[w % 2], 0:n_q], ACT.Exp,
                                       scale=SCALE).then_inc(S.p_exp, 1)
                    elif kind == "weighted":
                        e, w = st_[1:]
                        qb_, kt = UNITS[w]
                        if kt == 4 * qb_ + 4:
                            b, o = slice(e * HD, (e + 1) * HD), slice((1 - e) * HD, (2 - e) * HD)
                            n_ = 4 * p + 2 * e + qb_
                            act.wait_ge(S.pv_done, 2 * NU * p + NU * e + w + 1)
                            act.wait_ge(S.o_norm, n_ + 2)
                            act.activation(dln[b, :], ps[o, B_PV[qb_], :], ACT.Ln).then_inc(S.d_ln, 1)
                            act.wait_ge(S.d_ln, n_ + 1)
                            act.activation(dln[b, :], dln[b, :], ACT.Exp, scale=-1.0).then_inc(S.d_recip, 1)

            def c_rows_of(head):
                return c_scr[bass.ds(head, 1)].rearrange("a b t -> (a b) t")

            round_act(-1, first_round(), [c_scr[0], None])
            split_b(0, 0)
            with act.Fori(0, KO - 1) as p:
                rows_c = [c_rows_of(act.snap(2 * p + 2)), c_rows_of(act.snap(2 * p + 1))]
                round_act(p, order(0, True), rows_c)
                round_act(p, order(1, True), rows_c)
            round_act(KO - 1, order(0, False), [None, c_scr[2 * KO - 1]])
            round_act(KO - 1, order(1, False), None)
            split_row(3, KO - 1)
            for m in range(KO):
                n = N_BO + m + 2
                if m < KO - 2:
                    split_hi(n % 2, 16 * (n // 2 + 1), None, N_B + m + 1)
                act.wait_ge(S.fin_tr, m + 1)
                if m >= 2:
                    act.wait_ge(FIN_STORED[m % 2], 16 * (m // 2))
                act.activation(fo[m % 2].rearrange("p (b t) c -> p b (t c)", b=2), ps[:, 4 + 2 * (m % 2):6 + 2 * (m % 2), :],
                               ACT.Copy).then_inc(S.fin_evac, 1)

        @block.vector
        def _(dve):
            def split_lo(slot, n, width=P, raw=None):
                dve.wait_ge(S.w_hi, n + 1)
                dve.tensor_tensor(wl[:, slot, :, 0:width], wr[:, slot if raw is None else raw, :, 0:width],
                                  f32(wh[:, slot, :, 0:width]), ALU.subtract).then_inc(S.w_lo, 1)

            def normalise(r):
                dve.wait_ge(S.h_rstd, r + 1)

                def lo(k):
                    dve.wait_ge(S.x_hi, 2 * KO * r + k + 1)
                    dve.tensor_tensor(xl[:, k, :], sq2[k % 2], f32(xh[:, k, :]), ALU.subtract).then_inc(S.x_lo, 1)
                for k in range(KO):
                    if k >= 2:
                        lo(k - 2)
                        dve.wait_ge(S.x_lo, 2 * KO * r + k - 1)
                    dve.tensor_tensor(sq2[k % 2], h_t[:, k, :], rstd, ALU.mult).then_inc(S.xn_mul, 1)
                lo(KO - 2)
                lo(KO - 1)

            for i, val in enumerate((RMS_EPS, GN_EPS, 0.5 * float(np.log(LN_SCALE)), 0.0)):
                dve.memset(cst[:, i:i + 1], val).then_inc(S.setup_dve, 1)
            dve.memset(all_ones[:, :], 1.0).then_inc(S.setup_dve, 1)
            dve.wait_ge(S.consts_loaded, 80)
            dve.tensor_copy(causal[:, :], causal_f).then_inc(S.setup_dve, 1)
            dve.tensor_copy(identb[:, :], ident[:, :]).then_inc(S.setup_dve, 1)
            dve.memset(h_t[:, :, T:TP], 0.0).then_inc(S.pads_zero, 1)
            for t in range(NT):
                dve.wait_ge(S.x_tr, t + 1)
                g, n = 2 * (t % 2), TILE_TOK[t]
                dve.tensor_copy(h_t[:, :, TILE_AT[t]:TILE_AT[t] + n],
                                ps[:, g:g + 2, :].rearrange("p b (k t) -> p (b k) t", k=4)[:, :, 0:n])\
                    .then_inc(S.x_evac, 1)
            dve.wait_ge(S.param_tr, 1)
            dve.tensor_copy(params[:, 0:ROW_LORA], ps[:, 6, 0:ROW_LORA]).then_inc(S.param_copied, 1)
            dve.tensor_copy(params[:, C_LORA:C_LORA + NROWS - ROW_LORA], ps[:, 6, ROW_LORA:NROWS])\
                .then_inc(S.param_copied, 1)
            dve.wait_ge(S.param_copied, 2)
            dve.tensor_scalar(param(Q_NR * KO, 4 * KO), param(Q_MUR * KO, 4 * KO), -1.0, 1.0, ALU.mult, ALU.add)\
                .then_inc(S.param_derived, 1)
            dve.tensor_scalar(param(Q_HDB * KO, 2 * KO), param(Q_DB * KO, 2 * KO), 0.5, None, ALU.mult)\
                .then_inc(S.param_derived, 1)
            dve.tensor_scalar(param(Q_NKA * KO, KO), param(Q_KA * KO, KO), -1.0, 1.0, ALU.mult, ALU.add)\
                .then_inc(S.param_derived, 1)
            dve.tensor_scalar(param(C_NLORA), param(C_LORA), -1.0, 1.0, ALU.mult, ALU.add)\
                .then_inc(S.param_derived, 1)
            dve.memset(f32(wl[:, 1, 0, 0:1]), 0.0).then_inc(S.w_lo, 1)
            dve.wait_ge(S.w_lo, 1)
            split_lo(3, 0, raw=0)
            normalise(0)
            dve.wait_ge(S.xt_stored, 16)
            dve.wait_ge(S.x_lo, KO)
            for a in reset:
                dve.memset(a, 1.0).then_inc(S.setup_dve, 1)
            dve.wait_ge(S.setup_dve, 9)
            dve.memset(reset[0][:, 0:1], 0.0).then_inc(S.setup_dve, 1)
            dve.memset(reset[0][:, META::CH], 0.0).then_inc(S.setup_dve, 1)
            dve.memset(reset[1][:, ::CH], 0.0).then_inc(S.setup_dve, 1)
            dve.memset(ar[:, :, 0:OFF], 0.0).then_inc(S.setup_dve, 1)
            for a in (b_t, k_t, v_t):
                dve.memset(a[:, 0:OFF], 0.0).then_inc(S.setup_dve, 1)
            dve.memset(mut_lo[:, 0:1], 0.0).then_inc(S.setup_dve, 1)
            dve.memset(pc[:, 0:1], 1.0).then_inc(S.setup_dve, 1)
            dve.wait_ge(S.setup_dve, 18)
            dve.sem_inc(S.gn_centred, 1)
            dve.sem_inc(S.gn_scaled, 1)
            dve.sem_inc(S.out_ready, NSEG)
            for j in range(2):
                split_lo(j, N_A + j, raw=(N_A + j) % 2)
            dve.wait_ge(S.mu_done, 1)
            dve.scalar_tensor_tensor(seg3(lo), G[0], param(C_NLORA), seg3(mut_lo[:, 0:TP]), ALU.mult, ALU.add)\
                .then_inc(S.shifted, 1)

            def split_row(r, k):
                dve.wait_ge(S.x_hi, KO * r + k + 1)
                src = osq[k % 2] if r == 1 else obq[k % 2]
                dve.tensor_tensor(xl[:, k, 0:src.shape[1]], src, f32(xh[:, k, 0:src.shape[1]]), ALU.subtract)\
                    .then_inc(S.x_lo, 1)

            def split_lo_a(q_, j):
                split_lo(j, 4 * q_ + N_A + j, raw=(N_A + j) % 2)

            def round_dve_a(p, s_, steps):
                F = NSEG * p + s_ + 1
                begin = isinstance(F, int) and F == 0
                s1 = (s_ + 1) % NSEG
                q_ = p + 1 if s_ == NSEG - 1 else p
                t0, t1 = SEG_T[s1]
                n = t1 - t0
                dst = slice(3 * P - n, 3 * P)
                cols = slice(OFF + t0, OFF + t1)

                def shift(out_, j, keep):
                    dve.wait_ge(S.mu_done, 4 * F + j + 2)
                    dve.scalar_tensor_tensor(out_, ps[:, B_GA[(0, 1, 0, 0)[j]], 0:n], q(keep), mut[j][:, 0:n],
                                             ALU.mult, ALU.add).then_inc(S.shifted, 1)

                def start_pair():
                    dve.memset(st, 0.0).then_inc(S.state_zero, 1)
                    dve.tensor_copy(gp[:, :], pp[:, Q_GW:Q_GW + 2]).then_inc(S.gn_params, 1)

                if s_ == 0 and isinstance(p, int) and p == 0:
                    start_pair()
                for st_ in steps:
                    kind = st_[0]
                    if kind in ("k", "v", "r", "z") and st_[1] < 2:
                        continue
                    if kind == "orow":
                        split_row(1, st_[1])
                    elif kind == "split":
                        split_lo_a(p + 1, st_[1])
                    elif kind == "low":
                        if s1 == 0:
                            src = param(0, NQ * KO).rearrange("p (q k) -> p q k", k=KO)
                            src = src[:, :, q_:q_ + 1] if isinstance(q_, int) else src[:, :, bass.ds(q_, 1)]
                            dve.tensor_copy(pp[:, :].unsqueeze(2), src).then_inc(S.pair_params, 1)
                        dve.wait_ge(S.dec_tanh, F + 1)
                        dve.tensor_scalar(lw[:, 0:n], lw[:, 0:n], -C_DECAY, -C_DECAY, ALU.mult, ALU.add)\
                            .then_inc(S.logw, 1)
                        dve.wait_ge(S.icl_tanh, F + 1)
                        dve.tensor_scalar(aa[:, 0:n], aa[:, 0:n], 0.5, 0.5, ALU.mult, ALU.add).then_inc(S.iclr, 1)
                        dve.wait_ge(S.logw, F + 1)
                        if not begin:
                            dve.wait_ge(S.b_tilde, F)
                        dve.tensor_tensor_scan(cum[:, 0:n], reset[1 if s1 else 0], lw[:, 0:n], 0.0, ALU.mult, ALU.add)\
                            .then_inc(S.cumlog, 1)
                    elif kind == "k":
                        dve.wait_ge(S.pair_params, q_ + 1)
                        shift(kr[:, 0:n], 0, Q_NK)
                    elif kind == "v":
                        if not begin:
                            dve.wait_ge(S.a_done, 2 * tiles_before(p + (s1 == 0), s1))
                        shift(v_t[:, dst], 1, Q_NV)
                    elif kind == "r":
                        dve.wait_ge(S.exp_in, F + 1)
                        if s1 == 0:
                            dve.tensor_copy(pc[:, 1:6], e_in[:, META - 1:n:CH]).then_inc(S.chunk_end, 1)
                        else:
                            dve.tensor_copy(pc[:, 4 * s1 + 2:4 * s1 + 6], e_in[:, CH - 1:n:CH]).then_inc(S.chunk_end, 1)
                        shift(rr[:, 0:n], 2, Q_NR)
                        dve.wait_ge(S.shifted, 4 * F + 4)
                        dve.tensor_tensor(ar[:, 1, cols], rr[:, 0:n], e_in[:, 0:n], ALU.mult).then_inc(S.r_tilde, 1)
                        dve.wait_ge(S.k_new, F + 1)
                        dve.scalar_tensor_tensor(mix[:, 0:n], rr[:, 0:n], q(Q_RK), kr[:, 0:n], ALU.mult, ALU.mult)\
                            .then_inc(S.bonus_prod, 1)
                        dve.wait_ge(S.kk_rn, F + 1)
                        dve.tensor_tensor(kk[:, 0:n], kk[:, 0:n], bon[:, t0:t1], ALU.mult).then_inc(S.kk_norm, 1)
                        dve.wait_ge(S.kk_norm, F + 1)
                        dve.wait_ge(S.exp_before, F + 1)
                        dve.scalar_tensor_tensor(ar[:, 0, cols], kk[:, 0:n], -1.0, lw[:, 0:n], ALU.mult, ALU.mult)\
                            .then_inc(S.a_tilde, 1)
                    elif kind == "kks":
                        dve.wait_ge(S.kk_sumsq, F + 1)
                        dve.wait_ge(S.out_ready, F + 1)
                        dve.tensor_scalar(bon[:, t0:t1], ps[:, B_GA[1], 0:n], KK_FLOOR ** 2, None, ALU.max)\
                            .then_inc(S.kk_guard, 1)
                    elif kind == "z":
                        shift(zz[:, t0:t1], 3, Q_NZ)
                    elif kind == "zgate":
                        dve.wait_ge(S.z_tanh, F + 1)
                        dve.scalar_tensor_tensor(zz[:, t0:t1], mix[:, 0:n], 1.0, zz[:, t0:t1], ALU.add, ALU.mult)\
                            .then_inc(S.z_gate, 1)
                    elif kind == "bsum":
                        dve.wait_ge(S.bonus_sum, F + 1)
                        dve.tensor_tensor(bon[:, t0:t1], ps[:, B_GA[1], 0:n], v_t[:, dst], ALU.mult).then_inc(S.bonus, 1)
                    elif kind == "amat":
                        for j, u in enumerate(GROUPS[st_[1]]):
                            for e in range(2):
                                dve.wait_ge(S.a_done, 18 * p + 2 * u + e + 1)
                                bank = (B_P[j], B_X[j])[e]
                                dve.tensor_tensor(amat[ring(u)][e].rearrange("p (a t) -> p a t", a=2),
                                                  ps[:, bank, :].rearrange("p (a t) -> p a t", a=2),
                                                  masks[:, :].unsqueeze(1).to_broadcast([P, 2, 2 * P]), ALU.mult)\
                                    .then_inc(S.a_masked, 1)
                    elif kind == "p":
                        g, l = st_[1:]
                        for j, u in enumerate(GROUPS[g]):
                            dve.wait_ge(S.p_done, STEPS * p + step(g, l, j) + 1)
                            dve.tensor_tensor(pm[j] if l else xs[j][:, :, 0, :],
                                              ps[:, B_P[j], 0:2 * P].rearrange("p (e t) -> p e t", e=2),
                                              levels[:, l * P:(l + 1) * P].unsqueeze(1).to_broadcast([P, 2, P]),
                                              ALU.mult).then_inc(S.p_masked, 1)
                    elif kind == "w":
                        for j, u in enumerate(GROUPS[st_[1]]):
                            dve.wait_ge(S.wu_done, 9 * p + u + 1)
                            dve.tensor_copy(wu[ring(u)].rearrange("p a t -> p (a t)"), ps[:, B_X[j], 0:2 * P])\
                                .then_inc(S.wu_copied, 1)
                    elif kind == "chain" and st_[2] < 4:
                        u, i = st_[1:]
                        pp_ = p - 1 if s_ == 0 else p
                        h = i // 2
                        c = 2 * u + h
                        b = slice(h * CH, (h + 1) * CH)
                        if i % 2 == 0:
                            dve.wait_ge(S.u_done, 18 * pp_ + c + 1)
                            if h == 0 and u:
                                dve.wait_ge(S.y_done, 9 * pp_ + u)
                            dve.wait_ge(S.wu_copied, 9 * pp_ + u + 1)
                            dve.tensor_tensor(us[b, :], ps[b, B_US, 0:P], wu[ring(u)][b, 1, :], ALU.add)\
                                .then_inc(S.u_ready, 1)
                        else:
                            dve.wait_ge(S.s_done, 18 * pp_ + c + 1)
                            dve.wait_ge(S.s_scaled, 18 * pp_ + c + 1)
                            for e in range(2):
                                d = slice(e * HD, (e + 1) * HD)
                                dve.scalar_tensor_tensor(st[d, d], ps[d, B_US, P + e * HD:P + (e + 1) * HD],
                                                         pc[d, c:c + 1], sp[d, d], ALU.mult, ALU.add)\
                                    .then_inc(S.s_ready, 1)
                    elif kind in ("gn1", "gn3"):
                        i = NSEG * p + s_ - 1
                        g0, g1 = SEG_T[(s_ - 1) % NSEG]
                        y_s = y_t[:, g0:g1]
                        if kind == "gn1":
                            dve.wait_ge(S.gn_mean, i + 1)
                            dve.scalar_tensor_tensor(y_s, ps[:, B_GA[1], 0:g1 - g0], -1.0 / HD, y_s, ALU.mult, ALU.add)\
                                .then_inc(S.gn_centred, 1)
                        else:
                            dve.wait_ge(S.gn_rstd, i + 1)
                            dve.tensor_tensor(y_s, y_s, gsq[:, 0:g1 - g0], ALU.mult).then_inc(S.gn_scaled, 1)
                            dve.wait_ge(S.gn_scaled, i + 2)
                            dve.tensor_scalar(y_s, y_s, gp[:, 0:1], gp[:, 1:2], ALU.mult, ALU.add)\
                                .then_inc(S.gn_affine, 1)
                            dve.wait_ge(S.gn_affine, i + 1)
                            dve.tensor_tensor(y_s, y_s, bon[:, g0:g1], ALU.add).then_inc(S.gn_bonus, 1)
                            dve.wait_ge(S.gn_bonus, i + 1)
                            dve.scalar_tensor_tensor(y_s, y_s, 0.5, zz[:, g0:g1], ALU.mult, ALU.mult)\
                                .then_inc(S.out_ready, 1)
                            if s_ == 0 and not (isinstance(p, int) and p == KO):
                                start_pair()

            for j in range(2, 4):
                split_lo_a(0, j)
            round_dve_a(0, -1, FRONT)
            round_dve_a(0, 0, round_order(0, False, True, False))
            with dve.Fori(0, KO - 1) as p:
                for s_ in range(1, NSEG):
                    round_dve_a(p, s_, round_order(s_, True, True, True))
                round_dve_a(p + 1, 0, round_order(0, True, True, True))
            for s_ in range(1, NSEG - 1):
                round_dve_a(KO - 1, s_, round_order(s_, True, True, False))
            for n in (N_AO, N_AO + 1):
                split_lo(n % 2, n)
            dve.wait_ge(S.b_tilde, NSEG * KO)
            dve.wait_ge(S.z_gate, NSEG * KO)
            for a in osq:
                dve.memset(a[:, T:TP], 0.0).then_inc(S.setup_dve, 1)
            dve.wait_ge(S.setup_dve, 20)
            round_dve_a(KO - 1, NSEG - 1, last_round_order())
            round_dve_a(KO, 0, tail_order())
            split_row(1, KO - 1)
            for m in range(KO):
                dve.wait_ge(S.proj_done, AFTER_A + N_AO + m + 1)
                dve.wait_ge(XT_LOADED[m % 2], 16 * (m // 2 + 1))
                dve.tensor_tensor(seg3(h_t[:, m, :]), G[(N_AO + m) % 2], seg3(h_t[:, m, :]), ALU.add)\
                    .then_inc(S.res_added, 1)
                if m + 2 < KO:
                    split_lo((N_AO + m) % 2, N_AO + m + 2)
                if m:
                    dve.wait_ge(S.h_sq, KO + m + 1)
                    if m > 1:
                        dve.wait_ge(S.h_acc, m - 1)
                    dve.tensor_tensor(rstd, rstd, sq2[m % 2], ALU.add).then_inc(S.h_acc, 1)
            split_lo(N_F % 2, N_F, H)
            normalise(1)
            split_lo(N_B % 2, N_B)
            dve.wait_ge(S.x_lo, 3 * KO)
            dve.wait_ge(S.proj_done, AFTER_A + N_F + 1)
            g = G[N_F % 2]
            dve.tensor_scalar(seg3(f_in[0:H, :]), g[0:H], fb_in[0:H, :], None, ALU.add).then_inc(S.f_logit, 1)
            dve.memset(vflat[0][:, :, HD:], 1.0).then_inc(S.setup_b, 1)
            dve.memset(vflat[1][:, :, 0:HD], 1.0).then_inc(S.setup_b, 1)
            dve.memset(f_b[0:H, :], 1.0).then_inc(S.setup_b, 1)
            dve.wait_ge(S.f_logit, 1)
            dve.wait_ge(S.f_abs, 1)
            dve.tensor_scalar(f_in[0:H, :], f_in[0:H, :], 0.0, None, ALU.min).then_inc(S.f_min, 1)
            dve.wait_ge(S.f_min, 1)
            dve.wait_ge(S.f_ln, 1)
            dve.tensor_tensor(f_in[0:H, :], f_in[0:H, :], f_a[0:H, :], ALU.subtract).then_inc(S.f_log, 1)
            dve.wait_ge(S.f_log, 1)
            dve.wait_ge(S.setup_b, 3)
            dve.tensor_tensor_scan(f_a[0:H, :], f_b[0:H, :], f_in[0:H, :], 0.0, ALU.mult, ALU.add).then_inc(S.f_cum, 1)
            dve.wait_ge(S.f_cum, 1)
            dve.tensor_scalar(f_b[0:H, :], f_a[0:H, :], -1.0 / SCALE, None, ALU.mult).then_inc(S.c_scaled, 1)
            dve.wait_ge(S.c_hi, 1)
            dve.tensor_tensor(clo[0:H, :], f_b[0:H, :], f32(chi[0:H, :]), ALU.subtract).then_inc(S.c_lo, 1)
            dve.wait_ge(S.c_lo, 1)
            dve.memset(mpart, MASKED).then_inc(S.setup_b, 1)
            dve.wait_ge(S.setup_b, 4)
            dve.sem_inc(S.o_norm, 2)
            dve.sem_inc(S.o_gated, 1)

            def round_dve(p, steps):
                first = isinstance(p, int) and p < 0
                for st_ in steps:
                    kind = st_[0]
                    if kind == "wsplit":
                        if isinstance(p, int):
                            split_lo((N_BO + 1) % 2, N_BO + 1)
                        else:
                            split_lo(N_B % 2, 4 * p + 8 + N_B)
                    elif kind == "orow":
                        split_row(3, st_[1])
                    elif kind == "proj":
                        j, i = st_[1:]
                        if i == 0 and j < 3:
                            split_lo((N_B + j + 1) % 2, 4 * p + 4 + N_B + j + 1)
                    elif kind == "norm":
                        j = st_[1]
                        dve.wait_ge(S.hn_rstd, 2 * p + 3 + j)
                        dve.scalar_tensor_tensor((kb, qb)[j], (kb, qb)[j], param((C_KN, C_QN)[j]), brs, ALU.mult,
                                                 ALU.mult).then_inc(S.hn_full, 1)
                    elif kind == "stack":
                        e = st_[1]
                        q_ = p + 1 - e
                        d, o = slice(e * HD, (e + 1) * HD), slice((1 - e) * HD, (2 - e) * HD)
                        dve.wait_ge(S.st_hi, 4 * q_ + 2 * e + 1)
                        dve.tensor_tensor(ka[e][o, :], kb[d, :], f32(ka[e][d, :]), ALU.subtract).then_inc(S.stacked, 1)
                        dve.tensor_copy(kb2[e][0:HD, :], f32(ka[e][d, :])).then_inc(S.stacked, 1)
                        dve.wait_ge(S.st_hi, 4 * q_ + 2 * e + 2)
                        dve.tensor_copy(qc2[e][0:HD, :], f32(qa[e][d, :])).then_inc(S.stacked, 1)
                        dve.tensor_copy(qa[e][o, :], f32(qa[e][d, :])).then_inc(S.stacked, 1)
                        dve.tensor_tensor(qb2[e][0:HD, :], qb[d, :], f32(qa[e][d, :]), ALU.subtract)\
                            .then_inc(S.stacked, 1)
                    elif kind == "gate":
                        dve.wait_ge(S.bz_tanh, p + 1)
                        dve.scalar_tensor_tensor(zg, zg, 1.0, zb, ALU.add, ALU.mult).then_inc(S.bz_gate, 1)
                    elif kind == "smax":
                        e, i = st_[1:]
                        base = NS * (2 * (p + 1 - e) + e)
                        t, part, k0, k1 = KSEG[i]
                        dve.wait_ge(S.smax_done, base + i + 1)
                        dve.tensor_reduce(mpart[:, 3 * t + part:3 * t + part + 1], ps[:, B_SM[i % 2], 0:k1 - k0],
                                          AX.X, ALU.max).then_inc(S.smax, 1)
                        if i == NS - 1:
                            dve.wait_ge(S.smax, base + NS)
                            dve.tensor_reduce(mcol, mpart.rearrange("p (t i) -> p t i", i=3), AX.X, ALU.max)\
                                .then_inc(S.mcol_ready, 1)
                            dve.wait_ge(S.mcol_ready, 2 * (p + 1 - e) + e + 1)
                    elif kind == "weighted":
                        e, w = st_[1:]
                        qb_, kt = UNITS[w]
                        if kt == 4 * qb_ + 4:
                            b = slice(e * HD, (e + 1) * HD)
                            dve.wait_ge(S.d_recip, 4 * p + 2 * e + qb_ + 1)
                            if e == 0 and qb_ == 0:
                                dve.wait_ge(S.ob_free, p + 1)
                            dve.tensor_tensor(ob[b, qb_ * 512:(qb_ + 1) * 512], ps[b, B_PV[qb_], :], dln[b, :], ALU.mult)\
                                .then_inc(S.o_norm, 1)
                            if e and qb_:
                                dve.wait_ge(S.o_norm, 4 * p + 6)
                                dve.wait_ge(S.bz_gate, p + 1)
                                dve.scalar_tensor_tensor(ob, ob, 0.5, zg[:, META:T], ALU.mult, ALU.mult)\
                                    .then_inc(S.o_gated, 1)

            round_dve(-1, first_round())
            split_lo(N_B % 2, N_B + 4)
            with dve.Fori(0, KO - 1) as p:
                round_dve(p, order(0, True))
                round_dve(p, order(1, True))
            round_dve(KO - 1, order(0, False))
            round_dve(KO - 1, order(1, False))
            split_row(3, KO - 1)
            for m in range(KO):
                dve.wait_ge(S.proj_done, AFTER_A + N_B + m + 1)
                dve.wait_ge(H_LOADED[m % 2], 16 * (m // 2 + 1))
                if m >= 2:
                    dve.wait_ge(S.fin_tr, m - 1)
                g = 2 * (m % 2)
                dve.tensor_tensor(fin[m % 2], ps[:, g:g + 2, :].rearrange("p b c -> p (b c)"), hres[m % 2],
                                  ALU.add).then_inc(S.fin_sum, 1)
                if m + 2 < KO:
                    split_lo((N_BO + m) % 2, N_BO + m + 2)

        @block.tensor
        def _(pe):
            def products(group, slot, width=P, segs=3, seg=SEG, channels=range(KO)):
                for c in range(segs):
                    acc = group[0:width, c, 0:seg]
                    t = slice(c * seg, (c + 1) * seg)
                    for k in channels:
                        pe.matmul(acc, wh[:, slot, k, 0:width], xh[:, k, t], start=(k == 0), stop=False)
                        pe.matmul(acc, wl[:, slot, k, 0:width], xh[:, k, t], start=False, stop=False)
                        mm = pe.matmul(acc, wh[:, slot, k, 0:width], xl[:, k, t], start=False, stop=(k == KO - 1))
                return mm

            def over(group, lhs, src):
                for c in range(3):
                    mm = pe.matmul(group[:, c, :], lhs, src[:, c * SEG:(c + 1) * SEG], start=True, stop=True)
                return mm

            def sum_squares(r):
                for k in range(KO):
                    pe.wait_ge(S.h_sq, KO * r + k + 1)
                    for c in range(3):
                        mm = pe.matmul(G[0][:, c, :], all_ones[:, :], sq2[k % 2][:, c * SEG:(c + 1) * SEG],
                                       start=(k == 0), stop=(k == KO - 1))
                    mm.then_inc(S.h_sumsq, 1)

            pe.wait_ge(S.consts_loaded, 80)
            for t in range(NT):
                pe.wait_ge(X_LOADED[t % 2], 16 * (t // 2 + 1))
                if t >= 2:
                    pe.wait_ge(S.x_evac, t - 1)
                n = TILE_TOK[t]
                for k in range(KO):
                    mm = pe.transpose(ps[:, 2 * (t % 2) + k // 4, (k % 4) * P:(k % 4) * P + n],
                                      xrow[t % 2][0:n, k * P:(k + 1) * P], ident[0:n, 0:n])
                mm.then_inc(S.x_tr, 1)
            pe.wait_ge(S.rows_loaded, 16)
            pe.transpose(ps[:, 6, 0:NROWS], prow[0:NROWS, :], ident[0:NROWS, 0:NROWS]).then_inc(S.param_tr, 1)
            pe.wait_ge(S.x_evac, NT)
            pe.wait_ge(S.setup_dve, 7)
            sum_squares(0)
            pe.wait_ge(S.w_lo, 2)
            pe.wait_ge(S.h_rstd, 1)
            for k in range(KO):
                pe.wait_ge(S.x_lo, k + 1)
                mm = products(G[0], 3, channels=[k])
            mm.then_inc(S.proj_done, 1)
            pe.wait_ge(S.lora_tanh, 1)
            pe.wait_ge(S.setup_pool, 4)

            def round_pe_a(p, s_, steps):
                F = NSEG * p + s_ + 1
                begin = isinstance(F, int) and F == 0
                s1 = (s_ + 1) % NSEG
                q_ = p + 1 if s_ == NSEG - 1 else p
                t0, t1 = SEG_T[s1]
                n = t1 - t0
                g_even, g_odd = ps[:, B_GA[0], 0:n], ps[:, B_GA[1], 0:n]

                def product(j, bank, part):
                    if part == 0:
                        pe.wait_ge(S.w_lo, 4 * q_ + N_A + j + 2)
                    for k in range(*PARTS[part]):
                        pe.matmul(bank, wh[:, j, k, :], xh[:, k, t0:t1], start=(k == 0), stop=False)
                        pe.matmul(bank, wl[:, j, k, :], xh[:, k, t0:t1], start=False, stop=False)
                        mm = pe.matmul(bank, wh[:, j, k, :], xl[:, k, t0:t1], start=False, stop=(k == KO - 1))
                    if part == 2:
                        mm.then_inc(S.proj_done, 1)

                for st_ in steps:
                    kind = st_[0]
                    if kind == "low":
                        pe.wait_ge(S.up_copied, q_ + 1)
                        pe.wait_ge(S.shifted, 4 * F + 1)
                        pe.matmul(g_even, upf[0:LORA, :], lo[0:LORA, t0:t1], start=True, stop=True)\
                            .then_inc(S.dec_done, 1)
                        if not begin:
                            pe.wait_ge(S.bonus, F)
                        pe.matmul(g_odd, upf[LORA:, :], lo[LORA:, t0:t1], start=True, stop=True)\
                            .then_inc(S.icl_done, 1)
                    elif kind == "k":
                        if st_[1] == 0:
                            pe.wait_ge(S.dec_tanh, F + 1)
                        product(0, g_even, st_[1])
                    elif kind == "v":
                        if st_[1] == 0:
                            pe.wait_ge(S.icl_tanh, F + 1)
                        product(1, g_odd, st_[1])
                    elif kind == "r":
                        if st_[1] == 0:
                            pe.wait_ge(S.shifted, 4 * F + 2)
                        product(2, g_even, st_[1])
                    elif kind == "kks":
                        pe.wait_ge(S.kk_sq, F + 1)
                        pe.wait_ge(S.shifted, 4 * F + 3)
                        pe.matmul(g_odd, head_ones[:, :], sq[:, 0:n], start=True, stop=True).then_inc(S.kk_sumsq, 1)
                    elif kind == "z":
                        if st_[1] == 0:
                            pe.wait_ge(S.shifted, 4 * F + 4)
                        product(3, g_even, st_[1])
                    elif kind == "bsum":
                        pe.wait_ge(S.bonus_prod, F + 1)
                        pe.wait_ge(S.kk_guard, F + 1)
                        if not begin:
                            pe.wait_ge(S.gn_ln, F)
                        pe.matmul(g_odd, head_ones[:, :], mix[:, 0:n], start=True, stop=True).then_inc(S.bonus_sum, 1)
                    elif kind == "rows":
                        g = st_[1]
                        if g < 2:
                            n_op = NSEG * p + 1
                        else:
                            n_op = NSEG * p + g
                        for j, u in enumerate(GROUPS[g]):
                            c, lc = slice(u * P, (u + 1) * P), local_cols(u)
                            if j == 0:
                                for sem in (S.a_tilde, S.r_tilde, S.b_tilde, S.k_tilde):
                                    pe.wait_ge(sem, n_op)
                                pe.wait_ge(S.shifted, 4 * n_op - 1)
                                if not (isinstance(p, int) and p == 0 and u == 0):
                                    pe.wait_ge(S.wu_copied, 9 * p + u)
                            for i, src in enumerate((ar[:, 0, c], b_t[:, lc], k_t[:, lc], v_t[:, lc])):
                                mm = pe.transpose(ps[:, B_X[j], i * P:(i + 1) * P], src, ident[:, :])
                            mm.then_inc(S.tr_done, 1)
                    elif kind == "amat":
                        for j, u in enumerate(GROUPS[st_[1]]):
                            c, lc = slice(u * P, (u + 1) * P), local_cols(u)
                            for e in range(2):
                                d = slice(e * HD, (e + 1) * HD)
                                bank = (B_P[j], B_X[j])[e]
                                if e:
                                    pe.wait_ge(S.rows_ready, 9 * p + u + 1)
                                pe.matmul(ps[:, bank, 0:2 * P], b_t[d, lc], ar[d, :, c], start=True, stop=True)
                                pe.matmul(ps[:, bank, 2 * P:], k_t[d, lc], ar[d, :, c], start=True, stop=True)\
                                    .then_inc(S.a_done, 1)
                    elif kind == "p":
                        g, l = st_[1:]
                        for j, u in enumerate(GROUPS[g]):
                            if l == 0:
                                pe.wait_ge(S.a_masked, 18 * p + 2 * u + 2)
                            elif l == 1:
                                pe.wait_ge(S.p_masked, STEPS * p + step(g, 0, j) + 1)
                            else:
                                pe.wait_ge(S.x_copied, STEPS * p + step(g, l - 1, j) + 1)
                            pe.matmul(ps[:, B_P[j], 0:2 * P], identb[:, :],
                                      identb[:, :].unsqueeze(1).to_broadcast([P, 2, P]), start=True, stop=False,
                                      skip_group_check=True)
                            for e in range(2):
                                mm = pe.matmul(ps[:, B_P[j], e * P:(e + 1) * P], amat[ring(u)][e][:, 0:P],
                                               xs[j][:, e, 0, :] if l else ident[:, :], start=False, stop=True,
                                               skip_group_check=True)
                            mm.then_inc(S.p_done, 1)
                    elif kind == "x":
                        g, l = st_[1:]
                        last = l == LEVELS[g] - 1
                        for j, u in enumerate(GROUPS[g]):
                            pe.wait_ge(S.p_masked, STEPS * p + step(g, l, j) + 1)
                            if l == 1:
                                pe.wait_ge(S.x_copied, STEPS * p + step(g, 0, j) + 1)
                            for e in range(2):
                                xb = ps[:, B_X[j], 2 * e * P:(2 * e + 2) * P].rearrange("p (a t) -> p a t", a=2)
                                if l and not last:
                                    pe.matmul(xb[:, 0, :], xs[j][:, e, 1, :], pm[j][:, e, :], start=True, stop=True)
                                if l:
                                    mm = pe.matmul(xb[:, 1, :], pm[j][:, e, :], xs[j][:, e, 1, :], start=True,
                                                   stop=True)
                                else:
                                    mm = pe.matmul(xb[:, 1, :], xs[j][:, e, 0, :], ident[:, :], start=True,
                                                   stop=True)
                            mm.then_inc(S.x_done, 1)
                    elif kind == "q":
                        for j, u in enumerate(GROUPS[st_[1]]):
                            for e in range(2):
                                d = slice(e * HD, (e + 1) * HD)
                                mm = pe.matmul(ps[:, B_P[j], d], amat[ring(u)][e][:, 2 * P:3 * P],
                                               rows_sb[ring(u)][:, 3, d], start=True, stop=True)
                            mm.then_inc(S.q_done, 1)
                    elif kind == "w":
                        g = st_[1]
                        for j, u in enumerate(GROUPS[g]):
                            pe.wait_ge(S.x_copied, STEPS * p + step(g, LEVELS[g] - 1, j) + 1)
                            pe.wait_ge(S.q_copied, 9 * p + u + 1)
                            for e in range(2):
                                d = slice(e * HD, (e + 1) * HD)
                                pe.matmul(ps[d, B_X[j], 0:P], rows_sb[ring(u)][:, 0, d], xs[j][:, e, 1, :],
                                          start=True, stop=True)
                                mm = pe.matmul(ps[:, B_X[j], P + e * HD:P + (e + 1) * HD], xs[j][:, e, 1, :],
                                               qs[j][:, d], start=True, stop=True)
                            mm.then_inc(S.wu_done, 1)
                    elif kind == "chain":
                        u, i = st_[1:]
                        pp_ = p - 1 if s_ == 0 else p
                        h = i // 2
                        c, t9 = 2 * u + h, 9 * pp_ + u
                        b = slice(h * CH, (h + 1) * CH)
                        rows_u, am = rows_sb[ring(u)], amat[ring(u)]
                        if i in (0, 2):
                            if c == 0:
                                pe.wait_ge(S.state_zero, pp_ + 1)
                            else:
                                pe.wait_ge(S.s_ready, 36 * pp_ + 2 * c)
                            pe.wait_ge(S.wu_copied, t9 + 1)
                            pe.matmul(ps[b, B_US, 0:P], wu[ring(u)][:, 0, b], st, start=True, stop=True)\
                                .then_inc(S.u_done, 1)
                            if h == 0 and u:
                                pe.wait_ge(S.y_copied, t9)
                            pe.matmul(ps[:, B_Y, b], st, ar[:, 1, u * P + h * CH:u * P + (h + 1) * CH],
                                      start=(h == 0), stop=False, skip_group_check=True)
                        elif i in (1, 3):
                            pe.wait_ge(S.u_ready, 18 * pp_ + c + 1)
                            o = ps[:, B_US, P:2 * P]
                            pe.matmul(o, rows_u[b, 2, :], rows_u[b, 3, :], start=True, stop=False)
                            pe.matmul(o, rows_u[b, 1, :], us[b, :], start=False, stop=True).then_inc(S.s_done, 1)
                        else:
                            for e in range(2):
                                d = slice(e * HD, (e + 1) * HD)
                                pe.matmul(ps[d, B_Y, 0:P], us[:, d], am[e][:, P:2 * P], start=False, stop=False,
                                          skip_group_check=True)
                                mm = pe.matmul(ps[d, B_Y, 0:P], rows_u[:, 3, d], am[e][:, 3 * P:], start=False,
                                               stop=True, skip_group_check=True)
                            mm.then_inc(S.y_done, 1)
                    elif kind in ("gn1", "gn2"):
                        i = NSEG * p + s_ - 1
                        g0, g1 = SEG_T[(s_ - 1) % NSEG]
                        if kind == "gn1":
                            n_t = 9 * p + (TILES_IN[s_ - 1][-1] + 1 if s_ else 0)
                            pe.wait_ge(S.y_copied, n_t)
                            last_f = 4 * KO if isinstance(F, int) and F >= 4 * KO else F + 1
                            pe.wait_ge(S.kk_guard, last_f)
                            pe.wait_ge(S.gn_ln, i + 1)
                            pe.matmul(ps[:, B_GA[1], 0:g1 - g0], head_ones[:, :], y_t[:, g0:g1], start=True, stop=True)\
                                .then_inc(S.gn_mean, 1)
                        else:
                            pe.wait_ge(S.gn_centred, i + 2)
                            pe.wait_ge(S.gn_sq, i + 1)
                            pe.matmul(ps[:, B_GA[1], 0:g1 - g0], head_ones[:, :], gsq[:, 0:g1 - g0], start=True,
                                      stop=True).then_inc(S.gn_var, 1)

            round_pe_a(0, -1, FRONT)
            round_pe_a(0, 0, round_order(0, False, True, False))
            with pe.Fori(0, KO - 1) as p:
                for s_ in range(1, NSEG):
                    round_pe_a(p, s_, round_order(s_, True, True, True))
                round_pe_a(p + 1, 0, round_order(0, True, True, True))
            for s_ in range(1, NSEG - 1):
                round_pe_a(KO - 1, s_, round_order(s_, True, True, False))
            round_pe_a(KO - 1, NSEG - 1, last_round_order())
            round_pe_a(KO, 0, tail_order())

            pe.wait_ge(S.w_lo, N_AO + 3)
            pe.wait_ge(S.gn_rstd, NSEG * KO)
            pe.wait_ge(S.gn_centred, NSEG * KO + 1)
            for k in range(KO):
                pe.wait_ge(S.x_lo, KO + k + 1)
                for n in (N_AO, N_AO + 1):
                    mm = products(G[n % 2], n % 2, channels=[k])
                    if k == KO - 1:
                        mm.then_inc(S.proj_done, 1)
            for m in range(2, KO):
                n = N_AO + m
                pe.wait_ge(S.w_lo, n + 2)
                if m >= 2:
                    pe.wait_ge(S.res_added, m - 1)
                products(G[n % 2], n % 2).then_inc(S.proj_done, 1)
            pe.wait_ge(S.res_added, KO)
            pe.wait_ge(S.h_acc, KO - 1)
            over(G[0], all_ones[:, :], rstd).then_inc(S.h_sumsq, 1)
            pe.wait_ge(S.w_lo, N_F + 2)
            for k in range(KO):
                pe.wait_ge(S.x_lo, 2 * KO + k + 1)
                mm = products(G[N_F % 2], N_F % 2, H, channels=[k])
            mm.then_inc(S.proj_done, 1)

            def round_pe(p, steps):
                first = isinstance(p, int) and p < 0
                for st_ in steps:
                    kind = st_[0]
                    if kind in ("proj", "sumsq", "vrow"):
                        j, i = st_[1:]
                        local = {"proj": (L_K, L_Q, L_V, L_Z), "sumsq": (L_SK, L_SQ), "vrow": (L_VROW0, L_VROW1)}[kind][j] + i
                        bank = ps[:, B_G[local % 2], :]
                        if not (first and local < L_K + 2):
                            pe.wait_ge(S.b_evac, chunk(p, local) - 1)
                    if kind == "proj":
                        slot = (N_B + j) % 2
                        if i == 0:
                            pe.wait_ge(S.w_lo, 4 * p + 4 + N_B + j + 2)
                        t = slice(i * SEG, (i + 1) * SEG)
                        for k in range(KO):
                            pe.matmul(bank[:, 0:SEG], wh[:, slot, k, :], xh[:, k, t], start=(k == 0), stop=False)
                            pe.matmul(bank[:, 0:SEG], wl[:, slot, k, :], xh[:, k, t], start=False, stop=False)
                            mm = pe.matmul(bank[:, 0:SEG], wh[:, slot, k, :], xl[:, k, t], start=False,
                                           stop=(k == KO - 1))
                        mm.then_inc(S.b_done, 1)
                    elif kind == "sumsq":
                        if i == 0:
                            pe.wait_ge(S.hn_sq, 2 * p + 3 + j)
                        pe.matmul(bank[:, 0:SEG], head_ones[:, :], bsq[:, i * SEG:(i + 1) * SEG], start=True, stop=True)\
                            .then_inc(S.b_done, 1)
                    elif kind == "vrow":
                        d = slice(j * HD, (j + 1) * HD)
                        if i == 0:
                            pe.wait_ge(S.b_evac, chunk(p - j, L_V) + 3)
                        for t in range(7) if i == 0 else range(7, NT):
                            n_k, c0 = min(P, T - t * P), (t - 7 * i) * HD
                            mm = pe.matmul(bank[0:n_k, c0:c0 + HD], vb[d, t * P:t * P + n_k], ident[d, d],
                                           start=True, stop=True)
                        mm.then_inc(S.b_done, 1)
                    elif kind == "smax":
                        e, i = st_[1:]
                        q_ = p + 1 - e
                        base = NS * (2 * q_ + e)
                        t, _, k0, k1 = KSEG[i]
                        bank = ps[:, B_SM[i % 2], :]
                        if i == 0:
                            pe.wait_ge(S.stacked, 10 * q_ + 5 * e + 3)
                            pe.wait_ge(C_ROWS[e], 16 * q_ + 16)
                            if not first:
                                pe.wait_ge(S.m_row, 4 * q_ + 2 * e)
                        elif i >= 2:
                            pe.wait_ge(S.smax, base + i - 1)
                        m0 = META + t * P
                        mm = pe.matmul(bank[:, 0:k1 - k0], qc2[e][0:HD + 3, m0:m0 + P], kb2[e][0:HD + 3, k0:k1],
                                       start=True, stop=(k1 <= m0), skip_group_check=True)
                        if k1 > m0:
                            c0 = max(m0, k0)
                            mm = pe.matmul(bank[:, c0 - k0:k1 - k0], identb[:, :], causal[:, P + c0 - m0:P + k1 - m0],
                                           start=False, stop=True, skip_group_check=True)
                        mm.then_inc(S.smax_done, 1)
                    elif kind == "maxrow":
                        e = st_[1]
                        pe.wait_ge(S.mcol_ready, 2 * (p + 1 - e) + e + 1)
                        for a in range(2):
                            for t in range(4):
                                mm = pe.matmul(ps[0:1, B_SM[a], t * P:(t + 1) * P], mcol[:, 4 * a + t:4 * a + t + 1],
                                               ident[:, :], start=True, stop=True)
                            mm.then_inc(S.m_row_done, 1)
                    elif kind == "scores":
                        e, w = st_[1:]
                        n_k, q0, n_q, off, n_diag = unit(w)
                        kt = UNITS[w][1]
                        if w == 0:
                            pe.wait_ge(S.m_row, 4 * p + 2 * e + 2)
                            pe.wait_ge(S.stacked, 10 * p + 5 * e + 5)
                        if w >= 2:
                            pe.wait_ge(S.p_exp, 2 * NU * p + NU * e + w - 1)
                        o = ps[0:n_k, B_ST[w % 2], 0:n_q]
                        ks, qs_ = slice(kt * P, kt * P + n_k), slice(META + q0, META + q0 + n_q)
                        pe.matmul(o, ka[e][:, ks], qa[e][:, qs_], start=True, stop=False, skip_group_check=True)
                        mm = pe.matmul(o, kb2[e][0:HD + 3, ks], qb2[e][0:HD + 3, qs_], start=False,
                                       stop=(n_diag == 0), skip_group_check=True)
                        if n_diag:
                            mm = pe.matmul(ps[0:n_k, B_ST[w % 2], 0:n_diag], identb[:, 0:n_k],
                                           causal[:, off:off + n_diag], start=False, stop=True, skip_group_check=True)
                        mm.then_inc(S.st_done, 1)
                    elif kind == "weighted":
                        e, w = st_[1:]
                        qb_, kt = UNITS[w]
                        n_k, q0, n_q, _, _ = unit(w)
                        pe.wait_ge(S.p_exp, 2 * NU * p + NU * e + w + 1)
                        if w == 0:
                            pe.wait_ge(S.b_evac, chunk(p - 1 + e, (L_VROW0, L_VROW1)[e]) + 2)
                        if kt == 0:
                            pe.wait_ge(S.o_norm, 4 * p + 2 * e + qb_ + 1)
                        pe.matmul(ps[:, B_PV[qb_], q0 - 512 * qb_:512], vflat[e][0:n_k, kt, :], pt[w % 3][0:n_k, 0:n_q],
                                  start=(kt == 0), stop=(kt == 4 * qb_ + 4), skip_group_check=True)\
                            .then_inc(S.pv_done, 1)

            round_pe(-1, first_round())
            with pe.Fori(0, KO - 1) as p:
                round_pe(p, order(0, True))
                round_pe(p, order(1, True))
            round_pe(KO - 1, order(0, False))
            round_pe(KO - 1, order(1, False))
            pe.wait_ge(S.o_norm, 4 * KO + 2)

            def back(m):
                pe.wait_ge(S.fin_sum, m + 1)
                if m >= 2:
                    pe.wait_ge(S.fin_evac, m - 1)
                for t in range(KO):
                    mm = pe.transpose(ps[:, 4 + 2 * (m % 2) + t // 4, (t % 4) * P:(t % 4 + 1) * P],
                                      fin[m % 2][:, t * P:(t + 1) * P], ident[:, :])
                mm.then_inc(S.fin_tr, 1)

            def bank_pair(m):
                return ps[:, 2 * (m % 2):2 * (m % 2) + 2, :]

            pe.wait_ge(S.w_lo, N_BO + 3)
            for k in range(KO):
                pe.wait_ge(S.x_lo, 3 * KO + k + 1)
                for m in range(2):
                    mm = products(bank_pair(m), (N_BO + m) % 2, P, 2, 512, channels=[k])
                    if k == KO - 1:
                        mm.then_inc(S.proj_done, 1)
            back(0)
            for m in range(2, KO):
                pe.wait_ge(S.w_lo, N_BO + m + 2)
                pe.wait_ge(S.fin_sum, m - 1)
                products(bank_pair(m), (N_BO + m) % 2, P, 2, 512).then_inc(S.proj_done, 1)
                back(m - 1)
            back(KO - 1)


def kernel(**inputs):
    import concourse.bacc as bacc
    from concourse.bass_utils import run_bass_kernel_spmd

    a = {k: np.asarray(v) for k, v in inputs.items()}
    rows = np.concatenate(
        [a["a_shift_mu"][0][:4 * D].reshape(-1, P)]
        + [a[n][0].reshape(-1, P) for n in ("a_decay_bias", "a_iclr_bias", "a_k_k", "a_k_a", "a_r_k",
                                            "a_gn_w", "a_gn_b")]
        + [a["a_shift_mu"][0][4 * D:].reshape(1, P), a["a_norm"][0].reshape(-1, P),
           a["kv_norm"].reshape(-1, P), a["b_norm"][0].reshape(-1, P),
           np.tile(a["k_norm"], 2)[None], np.tile(a["b_q_norm"][0], 2)[None]], axis=0)
    i = np.arange(P)
    same = i[:, None] // CH == i[None, :] // CH
    masks = np.concatenate([same & (i[:, None] < i[None, :]), same & (i[:, None] <= i[None, :])],
                           axis=1).astype(np.float32)
    lev = []
    for b in (1, 2, 4, 8, 16, 32):
        t, s = i[:, None] // b, i[None, :] // b
        lev.append(((t // 2 == s // 2) & (t == s + 1)) | (i[:, None] == i[None, :]))
    levels = np.concatenate(lev, axis=1).astype(np.float32)
    ident = np.eye(P, dtype=np.float32)
    causal = np.concatenate([np.where(i[:, None] > i[None, :], MASKED, 0.0),
                             np.where(i[:, None] < i[None, :], MASKED, 0.0)], axis=1).astype(np.float32)
    arrays = {
        "x": a["x"][0], "meta": a["meta_tokens"], "rows": rows, "w_in": a["a_w_in"][0],
        "up": np.concatenate([a["a_decay_up"][0], a["a_iclr_up"][0]], axis=0), "w_out": a["a_w_out"][0],
        "kv_w": a["kv_w"], "f_bias": a["kv_f_bias"][:, None], "b_w_in": a["b_w_in"][0],
        "b_w_out": a["b_w_out"][0], "ident_d": ident, "masks_d": masks, "levels_d": levels,
        "causal_d": causal,
    }
    nc = bacc.Bacc("TRN2", target_bir_lowering=False, num_devices=1)
    feeds, aps = {}, {}
    for name, v in arrays.items():
        v = np.ascontiguousarray(v)
        feeds[f"in_{name}"] = v
        aps[name] = nc.dram_tensor(f"in_{name}", v.shape, mybir.dt.from_np(v.dtype), kind="ExternalInput").ap()
    aps["out"] = nc.dram_tensor("out_0", (SEQ, D), F32, kind="ExternalOutput").ap()
    build(nc, **aps)
    r = run_bass_kernel_spmd(nc, [feeds], core_ids=[0])
    return r.results[0]["out_0"].reshape(1, SEQ, D)
```
